# Optimizing a Trainium2 kernel written in Bass

```python
import jax, jax.numpy as jnp
from jax import lax
import numpy as np
import math, functools

D_MODEL = 1024
BATCH = 1
SEQ = 256
DEPTH = 2

HEAD_DIM = 64
A_HEADS = 8
B_HEADS = 4
C_HEADS = 4
A_WIDTH = A_HEADS * HEAD_DIM
B_WIDTH = B_HEADS * HEAD_DIM
C_WIDTH = C_HEADS * HEAD_DIM
MIX_WIDTH = A_WIDTH + B_WIDTH + C_WIDTH
MOBA_BLOCK = 256
MOBA_TOPK = 3
MOBA_QCHUNK = 128
RET_CHUNK = 256
MLSTM_CHUNK = 128
PAD_MULT = 256
CONV_K = 4
RMS_EPS = 1e-6
HEAD_NORM_EPS = 1e-5
ROPE_BASE = 10000.0
SPLIT_SIZES = [A_WIDTH] * 4 + [B_WIDTH] * 4 + [C_WIDTH] * 5 + [C_HEADS, C_HEADS]
N_IN = sum(SPLIT_SIZES)


def rmsnorm(x, w):
    x32 = x.astype(jnp.float32)
    y = x32 * lax.rsqrt(jnp.mean(x32 * x32, axis=-1, keepdims=True) + RMS_EPS)
    return (y * w.astype(jnp.float32)).astype(x.dtype)

def split_heads(t, n_heads):
    b, s, _ = t.shape
    return t.reshape(b, s, n_heads, HEAD_DIM).transpose(0, 2, 1, 3)

def merge_heads(t):
    b, h, s, d = t.shape
    return t.transpose(0, 2, 1, 3).reshape(b, s, h * d)

def head_norm(y, w):
    mu = jnp.mean(y, axis=-1, keepdims=True)
    var = jnp.mean(jnp.square(y - mu), axis=-1, keepdims=True)
    y = (y - mu) * lax.rsqrt(var + HEAD_NORM_EPS)
    return merge_heads(y) * w.astype(jnp.float32)

def alibi_slopes(n_heads):
    return jnp.exp2(-8.0 * jnp.arange(1, n_heads + 1, dtype=jnp.float32) / n_heads)

def rotate(t, pos):
    half = t.shape[-1] // 2
    theta = 1.0 / (ROPE_BASE ** jnp.linspace(0.0, 1.0, half, dtype=jnp.float32))
    ang = pos[:, None] * theta[None, :]
    cos, sin = jnp.cos(ang), jnp.sin(ang)
    t1, t2 = t[..., :half], t[..., half:]
    return jnp.concatenate([t1 * cos - t2 * sin, t1 * sin + t2 * cos], axis=-1)

def moba_attention(q, k, v):
    b, h, s, dh = q.shape
    nb = s // MOBA_BLOCK
    n_sel = min(MOBA_TOPK, nb - 1)
    scale = dh ** -0.5
    slopes = alibi_slopes(h)[None, :, None, None]
    kb = k.reshape(b, h, nb, MOBA_BLOCK, dh)
    vb = v.reshape(b, h, nb, MOBA_BLOCK, dh)
    kmean = jnp.mean(kb, axis=3)
    bi = jnp.arange(b)[:, None, None, None]
    hi = jnp.arange(h)[None, :, None, None]
    offs = jnp.arange(MOBA_BLOCK)
    qloc = jnp.arange(MOBA_QCHUNK)

    def one_chunk(c):
        t0 = c * MOBA_QCHUNK
        qc = lax.dynamic_slice_in_dim(q, t0, MOBA_QCHUNK, axis=2)
        tpos = t0 + qloc
        j = t0 // MOBA_BLOCK
        k_own = lax.dynamic_slice_in_dim(k, j * MOBA_BLOCK, MOBA_BLOCK, axis=2)
        v_own = lax.dynamic_slice_in_dim(v, j * MOBA_BLOCK, MOBA_BLOCK, axis=2)
        dist_own = tpos[:, None] - (j * MOBA_BLOCK + offs)[None, :]
        s_own = jnp.einsum('bhqd,bhkd->bhqk', qc, k_own) * scale - slopes * dist_own
        s_own = jnp.where(dist_own >= 0, s_own, -jnp.inf)
        if n_sel == 0:
            p = jax.nn.softmax(s_own, axis=-1)
            return jnp.einsum('bhqk,bhkd->bhqd', p, v_own)
        gate = jnp.einsum('bhqd,bhnd->bhqn', qc, kmean)
        gate = jnp.where(jnp.arange(nb) < j, gate, -jnp.inf)
        _, idx = lax.top_k(gate, n_sel)
        valid = jnp.arange(n_sel) < j
        k_sel = kb[bi, hi, idx]
        v_sel = vb[bi, hi, idx]
        dist = tpos[:, None, None] - (idx[..., None] * MOBA_BLOCK + offs)
        s_sel = jnp.einsum('bhqd,bhqnkd->bhqnk', qc, k_sel) * scale - slopes[..., None] * dist
        s_sel = jnp.where(valid[:, None], s_sel, -jnp.inf)
        n_k = n_sel * MOBA_BLOCK
        s_all = jnp.concatenate([s_sel.reshape(b, h, MOBA_QCHUNK, n_k), s_own], axis=-1)
        p = jax.nn.softmax(s_all, axis=-1)
        p_sel = p[..., :n_k].reshape(b, h, MOBA_QCHUNK, n_sel, MOBA_BLOCK)
        p_own = p[..., n_k:]
        return (jnp.einsum('bhqnk,bhqnkd->bhqd', p_sel, v_sel)
                + jnp.einsum('bhqk,bhkd->bhqd', p_own, v_own))

    outs = lax.map(one_chunk, jnp.arange(s // MOBA_QCHUNK))
    return outs.transpose(1, 2, 0, 3, 4).reshape(b, h, s, dh)

def retention(q, k, v):
    b, h, s, dh = q.shape
    L = RET_CHUNK
    nc = s // L
    log_gamma = jnp.log(1.0 - jnp.exp2(-5.0 - jnp.arange(h, dtype=jnp.float32)))
    k = k * (dh ** -0.5)
    qc = q.reshape(b, h, nc, L, dh)
    kc = k.reshape(b, h, nc, L, dh)
    vc = v.reshape(b, h, nc, L, dh)
    pos = jnp.arange(L, dtype=jnp.float32)
    diff = pos[:, None] - pos[None, :]
    decay = jnp.where(diff >= 0, jnp.exp(log_gamma[:, None, None] * jnp.maximum(diff, 0.0)), 0.0)
    scores = jnp.einsum('bhcnd,bhcmd->bhcnm', qc, kc) * decay[None, :, None]
    o_intra = jnp.einsum('bhcnm,bhcme->bhcne', scores, vc)
    zeta = jnp.exp(log_gamma[:, None] * (L - 1.0 - pos))
    kv = jnp.einsum('bhcmd,bhcme->bhcde', kc * zeta[None, :, None, :, None], vc)
    chunk_decay = jnp.exp(log_gamma * L)[None, :, None, None]

    def step(state, kv_c):
        return chunk_decay * state + kv_c, state

    r0 = jnp.zeros((b, h, dh, dh), jnp.float32)
    _, r_prev = lax.scan(step, r0, kv.transpose(2, 0, 1, 3, 4))
    r_prev = r_prev.transpose(1, 2, 0, 3, 4)
    xi = jnp.exp(log_gamma[:, None] * (pos + 1.0))
    o_cross = jnp.einsum('bhcnd,bhcde->bhcne', qc, r_prev) * xi[None, :, None, :, None]
    return (o_intra + o_cross).reshape(b, h, s, dh)

def mlstm(q, k, v, i_pre, f_pre):
    b, h, s, dh = q.shape
    L = MLSTM_CHUNK
    nc = s // L
    k = k * (dh ** -0.5)
    to_chunks = lambda t: t.reshape(b, h, nc, L, dh).transpose(2, 0, 1, 3, 4)
    qc, kc, vc = to_chunks(q), to_chunks(k), to_chunks(v)
    ic = i_pre.reshape(b, h, nc, L).transpose(2, 0, 1, 3)
    bc = jnp.cumsum(jax.nn.log_sigmoid(f_pre).reshape(b, h, nc, L), axis=-1).transpose(2, 0, 1, 3)
    pos = jnp.arange(L)
    causal = pos[:, None] >= pos[None, :]

    def step(carry, inp):
        c_st, n_st, m_st = carry
        qt, kt, vt, it, bt = inp
        d_log = jnp.where(causal, bt[..., :, None] - bt[..., None, :] + it[..., None, :], -jnp.inf)
        inter_log = bt + m_st[..., None]
        m_t = jnp.maximum(inter_log, jnp.max(d_log, axis=-1))
        w_intra = jnp.exp(d_log - m_t[..., None])
        w_inter = jnp.exp(inter_log - m_t)
        sc = jnp.einsum('bhtd,bhsd->bhts', qt, kt) * w_intra
        num = (jnp.einsum('bhts,bhse->bhte', sc, vt)
               + w_inter[..., None] * jnp.einsum('bhtd,bhde->bhte', qt, c_st))
        den = jnp.sum(sc, axis=-1) + w_inter * jnp.einsum('bhtd,bhd->bht', qt, n_st)
        h_t = num / jnp.maximum(jnp.abs(den), jnp.exp(-m_t))[..., None]
        b_last = bt[..., -1]
        g = b_last[..., None] - bt + it
        m_new = jnp.maximum(b_last + m_st, jnp.max(g, axis=-1))
        a = jnp.exp(b_last + m_st - m_new)
        w = jnp.exp(g - m_new[..., None])
        c_new = a[..., None, None] * c_st + jnp.einsum('bhs,bhsd,bhse->bhde', w, kt, vt)
        n_new = a[..., None] * n_st + jnp.einsum('bhs,bhsd->bhd', w, kt)
        return (c_new, n_new, m_new), h_t

    init = (jnp.zeros((b, h, dh, dh), jnp.float32), jnp.zeros((b, h, dh), jnp.float32),
            jnp.zeros((b, h), jnp.float32))
    _, hs = lax.scan(step, init, (qc, kc, vc, ic, bc))
    return hs.transpose(1, 2, 0, 3, 4).reshape(b, h, s, dh)

def causal_dwconv(x, w, bias):
    c = x.shape[-1]
    y = lax.conv_general_dilated(x, w.astype(x.dtype)[:, None, :], window_strides=(1,),
                                 padding=[(CONV_K - 1, 0)], dimension_numbers=('NWC', 'WIO', 'NWC'),
                                 feature_group_count=c)
    return y + bias.astype(x.dtype)

def hybrid_layer(x, norm_w, w_in, conv_w, conv_b, gate_bias, ret_norm_w, mlstm_norm_w, w_out):
    b, s, _ = x.shape
    s_pad = -(-s // PAD_MULT) * PAD_MULT
    h = rmsnorm(x, norm_w)
    proj = jnp.matmul(h, w_in).astype(jnp.float32)
    proj = jnp.pad(proj, ((0, 0), (0, s_pad - s), (0, 0)))
    cuts = np.cumsum(SPLIT_SIZES)[:-1].tolist()
    (aq, ak, av, ag, bq, bk, bv, bg, cq, ck, cv, co, cg, ci, cf) = jnp.split(proj, cuts, axis=-1)

    ya = moba_attention(split_heads(aq, A_HEADS), split_heads(ak, A_HEADS), split_heads(av, A_HEADS))
    ya = merge_heads(ya) * jax.nn.silu(ag)

    pos = jnp.arange(s_pad, dtype=jnp.float32)
    yb = retention(rotate(split_heads(bq, B_HEADS), pos), rotate(split_heads(bk, B_HEADS), pos),
                   split_heads(bv, B_HEADS))
    yb = head_norm(yb, ret_norm_w) * jax.nn.silu(bg)

    qk = jax.nn.silu(causal_dwconv(jnp.concatenate([cq, ck], axis=-1), conv_w, conv_b))
    cq_c, ck_c = qk[..., :C_WIDTH], qk[..., C_WIDTH:]
    gb = gate_bias.astype(jnp.float32)
    i_pre = ci.transpose(0, 2, 1) + gb[:C_HEADS][None, :, None]
    f_pre = cf.transpose(0, 2, 1) + gb[C_HEADS:][None, :, None]
    yc = mlstm(split_heads(cq_c, C_HEADS), split_heads(ck_c, C_HEADS), split_heads(cv, C_HEADS),
               i_pre, f_pre)
    yc = yc * split_heads(jax.nn.sigmoid(co), C_HEADS)
    yc = head_norm(yc, mlstm_norm_w) * jax.nn.silu(cg)

    y = jnp.concatenate([ya, yb, yc], axis=-1)[:, :s].astype(x.dtype)
    return x + jnp.matmul(y, w_out)

def first_inputs(seed: int = 0) -> dict:
    key = jax.random.key(seed)
    ks = jax.random.split(key, 12)
    f32 = jnp.float32
    x = jax.random.normal(ks[0], (BATCH, SEQ, D_MODEL), f32)
    norm_w = 1.0 + 0.02 * jax.random.normal(ks[1], (DEPTH, D_MODEL), f32)
    w_in = jax.random.normal(ks[2], (DEPTH, D_MODEL, N_IN), f32) * D_MODEL ** -0.5
    conv_w = jax.random.normal(ks[3], (DEPTH, CONV_K, 2 * C_WIDTH), f32) * CONV_K ** -0.5
    conv_b = 0.02 * jax.random.normal(ks[4], (DEPTH, 2 * C_WIDTH), f32)
    i_bias = 0.1 * jax.random.normal(ks[5], (DEPTH, C_HEADS), f32)
    f_bias = jnp.linspace(3.0, 6.0, C_HEADS, dtype=f32)[None, :] + 0.1 * jax.random.normal(ks[6], (DEPTH, C_HEADS), f32)
    gate_bias = jnp.concatenate([i_bias, f_bias], axis=-1)
    ret_norm_w = 1.0 + 0.02 * jax.random.normal(ks[7], (DEPTH, B_WIDTH), f32)
    mlstm_norm_w = 1.0 + 0.02 * jax.random.normal(ks[8], (DEPTH, C_WIDTH), f32)
    w_out = jax.random.normal(ks[9], (DEPTH, MIX_WIDTH, D_MODEL), f32) * MIX_WIDTH ** -0.5
    final_norm_w = 1.0 + 0.02 * jax.random.normal(ks[10], (D_MODEL,), f32)
    return {"x": x, "norm_w": norm_w, "w_in": w_in, "conv_w": conv_w, "conv_b": conv_b,
            "gate_bias": gate_bias, "ret_norm_w": ret_norm_w, "mlstm_norm_w": mlstm_norm_w,
            "w_out": w_out, "final_norm_w": final_norm_w}

def first_block(x, norm_w, w_in, conv_w, conv_b, gate_bias, ret_norm_w, mlstm_norm_w, w_out, final_norm_w):
    for layer in range(DEPTH):
        x = hybrid_layer(x, norm_w[layer], w_in[layer], conv_w[layer], conv_b[layer], gate_bias[layer],
                         ret_norm_w[layer], mlstm_norm_w[layer], w_out[layer])
    return rmsnorm(x, final_norm_w)


DEPTH_2 = 1

GRID_W = 64
D_MIX = D_MODEL
N_Q_HEADS = 8
N_KV_HEADS = 2
GQA_GROUP = N_Q_HEADS // N_KV_HEADS
ATTN_W = N_Q_HEADS * HEAD_DIM
KV_W = N_KV_HEADS * HEAD_DIM
LRU_W = D_MIX - ATTN_W
LRU_BLOCKS = 8
LRU_BW = LRU_W // LRU_BLOCKS
LRU_C = 8.0
CONV_W = 4
CONV_PAD_L = 2
ROPE_THETA = 10000.0
ROPE_HALF = HEAD_DIM // 2
Q_BLOCK = 128
N_EXPERTS = 32
TOP_K = 4
D_FF = D_MODEL
SWIGLU_ALPHA = 1.702
SWIGLU_LIMIT = 7.0
MOE_BLOCK = 256
NORM_EPS = 1e-5
IN_W = ATTN_W + 2 * KV_W + 2 * LRU_W


def rms_norm(x, g, eps=NORM_EPS):
    xf = x.astype(jnp.float32)
    y = xf * lax.rsqrt(jnp.mean(xf * xf, axis=-1, keepdims=True) + eps)
    return (y * g.astype(jnp.float32)).astype(x.dtype)

def rope_1d(x, pos):
    m = x.shape[-1] // 2
    inv_freq = ROPE_THETA ** (-jnp.arange(m, dtype=jnp.float32) / m)
    ang = pos.astype(jnp.float32)[:, None] * inv_freq[None, :]
    cos = jnp.cos(ang)[None, :, None, :]
    sin = jnp.sin(ang)[None, :, None, :]
    xf = x.astype(jnp.float32)
    x1, x2 = xf[..., :m], xf[..., m:]
    out = jnp.concatenate([x1 * cos - x2 * sin, x2 * cos + x1 * sin], axis=-1)
    return out.astype(x.dtype)

def rope_axial_2d(x, rows, cols):
    return jnp.concatenate([rope_1d(x[..., :ROPE_HALF], rows),
                            rope_1d(x[..., ROPE_HALF:], cols)], axis=-1)

def block_attention(q, k, v):
    B, S = q.shape[0], q.shape[1]
    nblk = S // Q_BLOCK
    qb = q.reshape(B, nblk, Q_BLOCK, N_KV_HEADS, GQA_GROUP, HEAD_DIM)
    qb = jnp.moveaxis(qb, 1, 0)
    scale = HEAD_DIM ** -0.5

    def one_block(qi):
        s = jnp.einsum('bqkgd,bskd->bkgqs', qi, k).astype(jnp.float32) * scale
        p = jax.nn.softmax(s, axis=-1).astype(v.dtype)
        return jnp.einsum('bkgqs,bskd->bqkgd', p, v)

    o = lax.map(one_block, qb)
    return jnp.moveaxis(o, 0, 1).reshape(B, S, ATTN_W)

def centred_depthwise_conv(u, w, b):
    S = u.shape[1]
    up = jnp.pad(u, ((0, 0), (CONV_PAD_L, CONV_W - 1 - CONV_PAD_L), (0, 0)))
    acc = b
    for j in range(CONV_W):
        acc = acc + up[:, j:j + S, :] * w[j]
    return acc

def _lin_combine(c1, c2):
    a1, b1 = c1
    a2, b2 = c2
    return a1 * a2, a2 * b1 + b2

def rglru_direction(xc, wa, ba, wi, bi, lam, reverse):
    B, S, _ = xc.shape
    xb = xc.reshape(B, S, LRU_BLOCKS, LRU_BW)
    r = jax.nn.sigmoid((jnp.einsum('bsni,nij->bsnj', xb, wa).reshape(B, S, LRU_W) + ba).astype(jnp.float32))
    i = jax.nn.sigmoid((jnp.einsum('bsni,nij->bsnj', xb, wi).reshape(B, S, LRU_W) + bi).astype(jnp.float32))
    log_a = -LRU_C * r * jax.nn.softplus(-lam.astype(jnp.float32))
    a = jnp.exp(log_a)
    mult = jnp.sqrt(-jnp.expm1(2.0 * log_a))
    bterm = mult * i * xc.astype(jnp.float32)
    _, h = lax.associative_scan(_lin_combine, (a, bterm), reverse=reverse, axis=1)
    return h

def moe_ffn(xn, w_router, b_router, w_gate, b_gate, w_up, b_up, w_down, b_down):
    B, S, D = xn.shape
    T = B * S
    xf = xn.reshape(T, D)
    logits = (xf @ w_router + b_router).astype(jnp.float32)
    top_v, top_i = lax.top_k(logits, TOP_K)
    gates = jax.nn.softmax(top_v, axis=-1).astype(xn.dtype)

    TK = T * TOP_K
    flat_e = top_i.reshape(TK).astype(jnp.int32)
    flat_tok = jnp.arange(TK, dtype=jnp.int32) // TOP_K
    flat_g = gates.reshape(TK)
    order = jnp.argsort(flat_e, stable=True)
    sorted_e = flat_e[order]
    counts = jnp.bincount(flat_e, length=N_EXPERTS)
    padded = ((counts + MOE_BLOCK - 1) // MOE_BLOCK) * MOE_BLOCK
    start = jnp.cumsum(counts) - counts
    pend = jnp.cumsum(padded)
    pstart = pend - padded
    dest = pstart[sorted_e] + (jnp.arange(TK, dtype=jnp.int32) - start[sorted_e])

    n_rows = TK + N_EXPERTS * MOE_BLOCK
    n_blocks = n_rows // MOE_BLOCK
    row_tok = jnp.full((n_rows,), T, dtype=jnp.int32).at[dest].set(flat_tok[order])
    row_gate = jnp.zeros((n_rows,), dtype=xn.dtype).at[dest].set(flat_g[order])
    block_e = jnp.searchsorted(pend, jnp.arange(n_blocks) * MOE_BLOCK, side='right')
    block_e = jnp.minimum(block_e, N_EXPERTS - 1).astype(jnp.int32)

    xpad = jnp.concatenate([xf, jnp.zeros((1, D), xf.dtype)], axis=0)
    x_rows = xpad[row_tok].reshape(n_blocks, MOE_BLOCK, D)

    def expert_block(args):
        xb, e = args
        g = xb @ w_gate[e] + b_gate[e]
        u = xb @ w_up[e] + b_up[e]
        g = jnp.minimum(g, SWIGLU_LIMIT)
        u = jnp.clip(u, -SWIGLU_LIMIT, SWIGLU_LIMIT)
        glu = g * jax.nn.sigmoid(SWIGLU_ALPHA * g)
        return ((u + 1.0) * glu) @ w_down[e] + b_down[e]

    y_rows = lax.map(expert_block, (x_rows, block_e)).reshape(n_rows, D)
    y_rows = y_rows * row_gate[:, None]
    out = jax.ops.segment_sum(y_rows, row_tok, num_segments=T + 1)[:T]
    return out.reshape(B, S, D)

def second_inputs(seed: int = 0) -> dict:
    key = jax.random.key(seed)
    ks = jax.random.split(key, 32)
    f32 = jnp.float32
    L = DEPTH_2

    def nrm(k, shape, fan_in):
        return jax.random.normal(k, shape, f32) * (fan_in ** -0.5)

    def gain(k, shape):
        return 1.0 + 0.05 * jax.random.normal(k, shape, f32)

    def bias(k, shape, s=0.01):
        return s * jax.random.normal(k, shape, f32)

    u = jax.random.uniform(ks[10], (L, 2, LRU_W), f32, minval=0.9, maxval=0.999)
    sgm = u ** (1.0 / LRU_C)
    lru_lam = jnp.log(sgm) - jnp.log1p(-sgm)

    return {
        'x': jax.random.normal(ks[0], (BATCH, SEQ, D_MODEL), f32),
        'norm1_g': gain(ks[1], (L, D_MODEL)),
        'w_in': nrm(ks[2], (L, D_MODEL, IN_W), D_MODEL),
        'q_norm_g': gain(ks[3], (L, HEAD_DIM)),
        'k_norm_g': gain(ks[4], (L, HEAD_DIM)),
        'conv_w': nrm(ks[5], (L, CONV_W, LRU_W), CONV_W),
        'conv_b': bias(ks[6], (L, LRU_W)),
        'lru_wa': nrm(ks[7], (L, 2, LRU_BLOCKS, LRU_BW, LRU_BW), LRU_BW),
        'lru_ba': bias(ks[8], (L, 2, LRU_W), 0.1),
        'lru_wi': nrm(ks[9], (L, 2, LRU_BLOCKS, LRU_BW, LRU_BW), LRU_BW),
        'lru_bi': bias(ks[11], (L, 2, LRU_W), 0.1),
        'lru_lam': lru_lam,
        'attn_out_g': gain(ks[12], (L, ATTN_W)),
        'lru_out_g': gain(ks[13], (L, LRU_W)),
        'w_out': nrm(ks[14], (L, D_MIX, D_MODEL), D_MIX),
        'norm2_g': gain(ks[15], (L, D_MODEL)),
        'w_router': nrm(ks[16], (L, D_MODEL, N_EXPERTS), D_MODEL),
        'b_router': bias(ks[17], (L, N_EXPERTS)),
        'w_gate': nrm(ks[18], (L, N_EXPERTS, D_MODEL, D_FF), D_MODEL),
        'b_gate': bias(ks[19], (L, N_EXPERTS, D_FF)),
        'w_up': nrm(ks[20], (L, N_EXPERTS, D_MODEL, D_FF), D_MODEL),
        'b_up': bias(ks[21], (L, N_EXPERTS, D_FF)),
        'w_down': nrm(ks[22], (L, N_EXPERTS, D_FF, D_MODEL), D_FF),
        'b_down': bias(ks[23], (L, N_EXPERTS, D_MODEL)),
        'final_g': gain(ks[24], (D_MODEL,)),
    }

def second_block(x, norm1_g, w_in, q_norm_g, k_norm_g, conv_w, conv_b, lru_wa, lru_ba,
              lru_wi, lru_bi, lru_lam, attn_out_g, lru_out_g, w_out, norm2_g,
              w_router, b_router, w_gate, b_gate, w_up, b_up, w_down, b_down, final_g):
    B, S, _ = x.shape
    n_rows_grid = S // GRID_W
    rows = jnp.broadcast_to(jnp.arange(n_rows_grid)[:, None], (n_rows_grid, GRID_W)).reshape(S)
    cols = jnp.broadcast_to(jnp.arange(GRID_W)[None, :], (n_rows_grid, GRID_W)).reshape(S)

    for l in range(DEPTH_2):
        xn = rms_norm(x, norm1_g[l])
        h_in = xn @ w_in[l]
        o0, o1, o2, o3 = ATTN_W, ATTN_W + KV_W, ATTN_W + 2 * KV_W, ATTN_W + 2 * KV_W + LRU_W
        q = h_in[..., :o0].reshape(B, S, N_Q_HEADS, HEAD_DIM)
        k = h_in[..., o0:o1].reshape(B, S, N_KV_HEADS, HEAD_DIM)
        v = h_in[..., o1:o2].reshape(B, S, N_KV_HEADS, HEAD_DIM)
        lru_x = h_in[..., o2:o3]
        lru_gate = h_in[..., o3:]

        q = rope_axial_2d(rms_norm(q, q_norm_g[l], 1e-6), rows, cols)
        k = rope_axial_2d(rms_norm(k, k_norm_g[l], 1e-6), rows, cols)
        attn = block_attention(q, k, v)

        xc = centred_depthwise_conv(lru_x, conv_w[l], conv_b[l])
        h_f = rglru_direction(xc, lru_wa[l, 0], lru_ba[l, 0], lru_wi[l, 0], lru_bi[l, 0],
                              lru_lam[l, 0], False)
        h_b = rglru_direction(xc, lru_wa[l, 1], lru_ba[l, 1], lru_wi[l, 1], lru_bi[l, 1],
                              lru_lam[l, 1], True)
        lru = ((h_f + h_b).astype(x.dtype)) * jax.nn.gelu(lru_gate)

        mixed = jnp.concatenate([rms_norm(attn, attn_out_g[l]),
                                 rms_norm(lru, lru_out_g[l])], axis=-1)
        x = x + mixed @ w_out[l]

        x = x + moe_ffn(rms_norm(x, norm2_g[l]), w_router[l], b_router[l], w_gate[l],
                        b_gate[l], w_up[l], b_up[l], w_down[l], b_down[l])

    return rms_norm(x, final_g)


def setup_inputs(seed=0):
    out = dict(first_inputs(seed))
    for name, value in second_inputs(seed + 1).items():
        if name != "x":
            out[name + "_2"] = value
    return out


def reference(
    x, norm_w, w_in, conv_w, conv_b, gate_bias, ret_norm_w, mlstm_norm_w, w_out, final_norm_w,
    norm1_g_2, w_in_2, q_norm_g_2, k_norm_g_2, conv_w_2, conv_b_2, lru_wa_2, lru_ba_2, lru_wi_2,
    lru_bi_2, lru_lam_2, attn_out_g_2, lru_out_g_2, w_out_2, norm2_g_2, w_router_2, b_router_2,
    w_gate_2, b_gate_2, w_up_2, b_up_2, w_down_2, b_down_2, final_g_2,
):
    x = first_block(
        x, norm_w, w_in, conv_w, conv_b, gate_bias, ret_norm_w, mlstm_norm_w, w_out,
        final_norm_w,
    )
    return second_block(
        x, norm1_g_2, w_in_2, q_norm_g_2, k_norm_g_2, conv_w_2, conv_b_2, lru_wa_2, lru_ba_2,
        lru_wi_2, lru_bi_2, lru_lam_2, attn_out_g_2, lru_out_g_2, w_out_2, norm2_g_2,
        w_router_2, b_router_2, w_gate_2, b_gate_2, w_up_2, b_up_2, w_down_2, b_down_2,
        final_g_2,
    )


_drawn_inputs = setup_inputs


def setup_inputs(seed=0):
    import zlib

    import numpy as np

    out = dict(_drawn_inputs(seed))
    spreads = {}
    factors = {'b_gate_2': 8.0, 'b_up_2': 24.172, 'b_down_2': 8.0}
    for name, (base, spread) in spreads.items():
        noise = np.random.default_rng([zlib.crc32(name.encode()), seed]).standard_normal(out[name].shape)
        drawn = base * np.exp(spread * noise) if base else spread * noise
        out[name] = __import__('jax').numpy.asarray(drawn.astype(out[name].dtype))
    for name, factor in factors.items():
        out[name] = (out[name] * factor).astype(out[name].dtype)
    return out
```

```python
from contextlib import ExitStack

import numpy as np

import concourse.bass as bass
from concourse import mybir

F32 = mybir.dt.float32
BF16 = mybir.dt.bfloat16
I32 = mybir.dt.int32
U32 = mybir.dt.uint32
ALU = mybir.AluOpType
ACT = mybir.ActivationFunctionType
AX = mybir.AxisListType.X

P = 128
D = 1024
S = 256
TC = S // P
KC = D // P
HD = 64
DEPTH = 2
A_HEADS, B_HEADS, C_HEADS = 8, 4, 4
N_IN = 4360
IN2 = 1792
LRU = 512
LC = LRU // P
Q_HEADS, KV_HEADS = 8, 2
E = 32
TOPK = 4
T = 64
SLOTS = 6
SLOT = 4096
CAUSAL = 3 * P
LRU_C, SWIGLU_ALPHA, SWIGLU_LIMIT = 8.0, 1.702, 7.0
RMS_EPS, HEAD_EPS, NORM_EPS = 1e-6, 1e-5, 1e-5
SCALE = HD ** -0.5

IN_GROUPS = [(4096, 264), (3072, 512), (0, 512), (512, 512), (3584, 512),
             (1024, 512), (1536, 512), (2048, 512), (2560, 512)]
LAYER_TURNS = 12
IN2_GROUPS = [(768, 512), (512, 256), (0, 512), (1280, 512)]
BLOCK2_TURNS = 6
EXPERT_LOADS = [("w_gate_2", 0), ("w_up_2", 0), ("w_gate_2", 1), ("w_up_2", 1), ("w_down_2", 0), ("w_down_2", 1)]
EXPERT_TURNS = len(EXPERT_LOADS)

TR_L, PJ_L, SC_L = 16, 18, 27
ARG_L, RES_L, POW_L = 8, 11, 3
PJ_0, OUT_0 = 5, 1
STEPS_L = 106
MAIN_STEPS, PRE_STEPS, EX_STEPS = 6, 1, 8

N_ROWS1 = 28
COL1 = {"norm": 0, "conv_w": 8, "conv_b": 24}
COL2 = {k: DEPTH * N_ROWS1 + v for k, v in
        {"norm1": 0, "conv_w": 8, "conv_b": 24, "ba": 28, "bi": 36, "lam": 44, "attn_g": 52, "lru_g": 56, "norm2": 60}.items()}
N_ROWS = DEPTH * N_ROWS1 + 68
N_PARAM_LOADS = 3 * DEPTH + 9 + 6


def shape_constants():
    f = np.float32
    p = np.arange(P)
    t = {}
    t["ident"] = np.eye(P, dtype=f)
    t["ones"] = np.ones((P, P), f)
    swap = (p // HD) * HD + (p % HD + HD // 2) % HD
    t["swap"] = np.eye(P, dtype=f)[:, swap]
    half = HD // 2
    theta = (1.0 / (f(10000.0) ** np.linspace(0.0, 1.0, half, dtype=f))).astype(f)
    ang = (np.arange(S, dtype=f)[None, :] * theta[p % half][:, None]).astype(f)
    sign = np.where(p % HD < half, -1.0, 1.0).astype(f)
    t["ret_cos"] = np.cos(ang).astype(f)
    t["ret_sin"] = (np.sin(ang) * sign[:, None]).astype(f)
    lg = np.log(1.0 - 2.0 ** (-5.0 - np.arange(B_HEADS, dtype=f))).astype(f)
    dec = []
    for h in range(B_HEADS):
        for m0, n0, n1 in ((0, 0, 256), (128, 128, 256)):
            diff = (np.arange(n0, n1)[None, :] - (m0 + p)[:, None]).astype(f)
            dec.append(np.where(diff >= 0, np.exp(lg[h] * np.maximum(diff, 0)), 0.0) * SCALE)
    t["decay"] = np.concatenate(dec, 1).astype(f)
    dist = [(q0 + p)[:, None] - np.arange(n)[None, :] for q0, n in ((0, 128), (128, 256))]
    dist = np.concatenate(dist, 1).astype(f)
    t["dist"] = np.where(dist >= 0, dist, 1e30).astype(f)
    t["tri"] = (p[:, None] <= p[None, :]).astype(f)
    t["before"] = (p[:, None] < p[None, :]).astype(f)
    inv = (f(10000.0) ** (-np.arange(16, dtype=f) / 16)).astype(f)
    for name, fn in (("rope_cos", np.cos), ("rope_sin", np.sin)):
        cols = []
        for c in range(TC):
            tok = 128 * c + p
            for pos in (tok // 64, tok % 64):
                a = (pos.astype(f)[:, None] * inv[None, :]).astype(f)
                v = fn(a).astype(f)
                cols += [-v, v] if name == "rope_sin" else [v, v]
        t[name] = np.concatenate(cols, 1)
    t["iota64"] = np.tile(np.arange(T, dtype=f), (P, 2))
    t["iota32"] = np.tile(np.arange(E, dtype=f), (P, 1))
    t["row_head"] = np.concatenate([np.repeat((p == h).astype(f)[:, None], P, 1) for h in range(C_HEADS)], 1)
    at, pos = {}, 0
    for k, v in t.items():
        at[k] = (pos, v.shape[1])
        pos += v.shape[1]
    return np.concatenate([v.astype(f) for v in t.values()], 1), at


def build(nc, ins, out):
    consts_at = ins["consts_at"]
    ctx = ExitStack()
    with ctx:
        def sb(name, shape, dt=F32):
            return ctx.enter_context(nc.sbuf_tensor(name, shape, dt))

        def sem(name):
            return ctx.enter_context(nc.semaphore(name))

        ring = sb("ring", [P, SLOTS, SLOT])
        const = sb("const", [P, ins["consts"].shape[1]])

        def K(name):
            a, n = consts_at[name]
            return const[:, a:a + n]

        ident, ones = K("ident"), K("ones")
        x = sb("x", [P, TC, D])
        xn = sb("xn", [P, TC, D])
        hT = sb("hT", [P, KC, S])
        yT = hT
        rows = sb("rows", [P, P])
        cols_all = sb("cols_all", [P, P])
        cols = sb("cols", [P, 32])
        gb_all = sb("gb_all", [C_HEADS, DEPTH, 2])
        gb = sb("gb", [C_HEADS, 2])
        hw_all = sb("hw_all", [P, DEPTH, 2, 256])
        hw = sb("hw", [P, 2, 256])
        roww = sb("roww", [P, D])
        qkw = sb("qkw", [P, 2, HD])
        brout = sb("brout", [P, E])
        small = sb("small", [P, 256])
        wr = sb("wr", [P, KC, E])

        mem1 = sb("mem1", [P, 8 * S])
        mem2 = sb("mem2", [P, 4 * 260])
        mem3 = sb("mem3", [P, 8 * S])
        mem4 = sb("mem4", [P, C_HEADS * CAUSAL])
        mem5 = sb("mem5", [P, 6 * CAUSAL])
        vA = sb("vA", [P, TC, 512])
        vC = sb("vC", [P, TC, C_HEADS, HD + 1])
        cg = sb("cg", [P, TC, 264])
        vgB = sb("vgB", [P, TC, 512])
        agT = sb("agT", [P, 4, S])
        eg = sb("eg", [P, 4, S])
        eB = sb("eB", [P, TC, 256])
        qkA = mem1[:, :].rearrange("p (c s) -> p c s", c=8)
        rawC = mem2[:, :].rearrange("p (c s) -> p c s", c=4)
        rawB = mem2[:, 0:4 * S].rearrange("p (c s) -> p c s", c=4)
        rotB = mem3[:, 0:4 * S].rearrange("p (c s) -> p c s", c=4)
        qkC = mem3[:, 4 * S:].rearrange("p (c s) -> p c s", c=4)
        wC = mem4[:, :].rearrange("p (h n) -> p h n", h=C_HEADS)
        sB = wC
        prob = mem5[:, 0:4 * CAUSAL].rearrange("p (h n) -> p h n", h=4)
        probT = mem5[:, 4 * CAUSAL:].rearrange("p (h n) -> p h n", h=2)
        rw = mem5[0:C_HEADS, :].rearrange("p (r n) -> p r n", r=9)
        xn_flat = xn[:, :, :].rearrange("p c d -> p (c d)")
        yBC = xn_flat[:, 0:512].rearrange("p (g d) -> p g d", d=HD)
        tmp = xn_flat[:, 512:1024].rearrange("p (g d) -> p g d", d=HD)
        eC = xn_flat[:, 1024:2048].rearrange("p (c n) -> p c n", c=TC)


        def four(a):
            return a.rearrange("p (c s) -> p c s", c=4)

        free_at = consts_at["swap"][0]
        lraw = mem2[:, :].rearrange("p (c s) -> p c s", c=4)
        xc, sq2 = four(mem3[:, 0:4 * S]), four(mem3[:, 4 * S:8 * S])
        flat2 = lambda a: a[:, :, :].rearrange("p c n -> p (c n)")
        gate = [[four(mem1[:, 0:4 * S]), four(mem1[:, 4 * S:8 * S])], [four(flat2(vA)), four(flat2(vgB))]]
        decay2 = [agT, eg]
        gel = four(xn_flat[:, 0:4 * S])
        lru_w = mem5[:, 0:2048].rearrange("p (u n) -> p u n", u=16)
        p2 = mem5[:, 0:2048].rearrange("p (h n) -> p h n", h=4)
        qk = mem4[:, 0:1280].rearrange("p (c h d) -> p c h d", c=TC, h=Q_HEADS + KV_HEADS)
        v2 = vC[:, :, :, :].rearrange("p c h d -> p (c h d)")[:, 0:2 * P].rearrange("p (c n) -> p c n", c=TC)
        rot1 = xn_flat[:, 1024:1664].rearrange("p (h d) -> p h d", d=HD)
        rot2 = mem2[:, 0:640].rearrange("p (h d) -> p h d", d=HD)
        qkT = const[:, free_at:free_at + 5 * S].rearrange("p (c s) -> p c s", c=5)
        pT2 = const[:, free_at + 5 * S:free_at + 9 * S].rearrange("p (j n) -> p j n", j=2)
        ao = agT
        sqL, sqA = gate[1][1], sq2
        neg2, sum2, half_b = small[:, 80:88], small[:, 88:96], small[:, 192:208]

        def lam(i):
            return small[:, 136 + 8 * i:144 + 8 * i]

        top_at = sb("top_at", [P, TC, 8], U32)
        n_more, n_before = sb("n_more", [P, E], I32), sb("n_before", [P, E], I32)
        at = [0]

        def piece(*shape):
            n = int(np.prod(shape))
            a = mem2[:, at[0]:at[0] + n]
            at[0] += n
            return a if len(shape) == 1 else a.rearrange("p (c n) -> p c n", c=shape[0])

        logits, mask, expL, gates, half_gates = (piece(TC, E) for _ in range(5))
        top, top_atf, place = piece(TC, 8), piece(TC, 8), piece(TC, E + 1)
        negL, rsum, rest = piece(TC), piece(TC), piece(TC)
        nblk, ncum = piece(E), piece(E)
        gatesT = mem4[0:E, 0:S]
        bdown = flat2(vA)[0:E, :]
        bias = const[:, free_at:free_at + 2 * D].rearrange("p (m n) -> p m n", m=2)
        xs_sb, xT, g_sb, tanh_g = (mem1[:, 512 * i:512 * (i + 1)] for i in range(4))
        u_sb, h_sb, hT_sb, y_sb = (mem3[:, 512 * i:512 * (i + 1)] for i in range(4))
        xTx, yx_sb = mem5[:, 0:512], mem5[:, 512:1024]
        gT, gTx = mem5[:, 1024:1280], mem5[:, 1280:1536]
        sel = mem5[:, 1536:1664].rearrange("p (c n) -> p c n", c=TC)
        selg = mem5[:, 1664:1920].rearrange("p (c n) -> p c n", c=TC)
        bsel = mem5[:, 1920:1984]

        bank = [ctx.enter_context(nc.psum_tensor(f"bank{i}", [P, 512], F32)) for i in range(8)]
        PJ, TR, SC = bank[0:4], bank[4:6], bank[6:8]
        LB = [bank[6], bank[7], bank[4], bank[5]]
        GB, UB, YB, XS, XTB, HTB, OB = bank[0], bank[1], bank[2], bank[3], bank[4], bank[5], bank[6:8]

        x_in, consts_in = sem("x_in"), sem("consts_in")
        ident_in = sem("ident_in")
        params_in, roww_in = sem("params_in"), sem("roww_in")
        w_in_slot = [sem(f"w_in_slot{i}") for i in range(SLOTS)]
        w_used = sem("w_used")
        load_begun = sem("load_begun")
        x_ready = sem("x_ready")
        xn_ready = sem("xn_ready")
        xw_ready = sem("xw_ready")
        tr_ready, tr_used = sem("tr_ready"), sem("tr_used")
        pj_ready, pj_used = sem("pj_ready"), sem("pj_used")
        sc_ready, sc_used = sem("sc_ready"), sem("sc_used")
        out_ready = sem("out_ready")
        act_arg, act_res = sem("act_arg"), sem("act_res")
        pow_arg, pow_res = sem("pow_arg"), sem("pow_res")
        probs_ready = sem("probs_ready")
        rows_ready = sem("rows_ready")
        qkC_ready, rotB_ready = sem("qkC_ready"), sem("rotB_ready")
        yC_ready, yB_ready, agT_done = sem("yC_ready"), sem("yB_ready"), sem("agT_done")
        fills = sem("fills")
        dve_step = sem("dve_step")
        ex_step = sem("ex_step")
        xc_ready, lru_w_in, lru_w_zero = sem("xc_ready"), sem("lru_w_in"), sem("lru_w_zero")
        qk_ready, lru_ready, y2_ready = sem("qk_ready"), sem("lru_ready"), sem("y2_ready")
        bias_zero, bias_in, bdown_in, wr_in = sem("bias_zero"), sem("bias_in"), sem("bdown_in"), sem("wr_in")
        mask_ready, gates_ready, count_ready = sem("mask_ready"), sem("gates_ready"), sem("count_ready")
        out_done = sem("out_done")
        ex = {n: sem("ex_" + n) for n in
              ("sel", "xs", "xs_out", "xt", "xt_out", "gu", "gc", "eg", "h", "ht", "ht_out", "y", "y_out",
               "selg", "gt", "gt_out", "o", "acc", "pe", "dve", "act", "bsel")}

        class Steps:

            def __init__(self, eng, s, base=0):
                self.eng, self.s, self.base, self.n = eng, s, base, 0

            def go(self, i):
                i.then_inc(self.s, 1)
                self.n += 1

            def wait(self):
                self.eng.wait_ge(self.s, self.base + self.n)

            def do(self, i):
                self.go(i)
                self.wait()

        block = ctx.enter_context(nc.Block())
        in_loads = [len([t for t in range(LAYER_TURNS - 1) if t % SLOTS == s]) for s in range(SLOTS)]

        @block.sync
        def _(sp):
            sp.dma_start(const[:, 0:2 * P], ins["consts"][:, 0:2 * P]).then_inc(ident_in, 16)
            sp.dma_start(x[:, :, :], ins["x"][0].rearrange("(c p) d -> p c d", p=P)).then_inc(x_in, 16)

            sp.wait_ge(params_in, 16 * N_PARAM_LOADS)

            def load(slot, dst, src):
                sp.dma_start(dst, src).then_inc(w_in_slot[slot], 16)

            def load_cols(slot, w, c0, n):
                load(slot, ring[:, slot, 0:KC * n].rearrange("p (k n) -> p k n", n=n),
                     w[:, c0:c0 + n].rearrange("(k p) n -> p k n", p=P))

            def slot_free(turn, l):
                if turn >= SLOTS:
                    sp.wait_ge(pj_ready, l * PJ_L + (PJ_0 + 2 * (turn - SLOTS + 1)))
                elif turn in (3, 4):
                    sp.wait_ge(out_ready, l + OUT_0)
                else:
                    sp.wait_ge(pj_ready, l * PJ_L + [1, 3, 5, 0, 0, 1][turn])
                sp.sem_inc(load_begun, 1)

            with sp.Fori(0, DEPTH) as l:
                w_in = ins["w_in"][bass.ds(l, 1)].rearrange("a k n -> (a k) n")
                w_out = ins["w_out"][bass.ds(l, 1)].rearrange("a k n -> (a k) n")
                for turn in range(LAYER_TURNS - 1):
                    slot_free(turn, l)
                    if turn < len(IN_GROUPS):
                        load_cols(turn % SLOTS, w_in, *IN_GROUPS[turn])
                    else:
                        load_cols(turn % SLOTS, w_out, 512 * (turn - len(IN_GROUPS)), 512)

            for turn in range(BLOCK2_TURNS):
                slot_free(turn, DEPTH)
                if turn < len(IN2_GROUPS):
                    load_cols(turn, ins["w_in_2"][0], *IN2_GROUPS[turn])
                else:
                    load_cols(turn, ins["w_out_2"][0], 512 * (turn - len(IN2_GROUPS)), 512)

            def load_expert(e, free):
                for turn, (name, h) in enumerate(EXPERT_LOADS):
                    free(turn)
                    src = ins[name][0, e, 512 * h:512 * h + 512, :]
                    load(turn, ring[:, turn, :], src.rearrange("a (p c) n -> p (a c n)", p=P))

            def free_of_block2(turn):
                if turn < 4:
                    sp.wait_ge(pj_ready, PJ_0 + DEPTH * PJ_L + [2, 4, 14, 16][turn])
                else:
                    sp.wait_ge(out_ready, OUT_0 + DEPTH + turn)

            load_expert(slice(0, 1), free_of_block2)
            with sp.Fori(0, E - 1) as e:
                def free_of_expert(turn):
                    sp.wait_ge(w_used, e * EXPERT_TURNS + (turn + 1))
                    sp.sem_inc(load_begun, 1)

                load_expert(bass.ds(e + 1, 1), free_of_expert)

            sp.wait_ge(x_ready, DEPTH + 5)
            sp.dma_start(out[0].rearrange("(c p) d -> p c d", p=P), xn[:, :, :]).then_inc(out_done, 16)
            sp.wait_ge(out_done, 16)

        @block.gpsimd
        def _(pool):
            def load(dst, src, s):
                pool.dma_start(dst, src).then_inc(s, 16)

            load(wr[:, :, :], ins["w_router_2"][0].rearrange("(k p) n -> p k n", p=P), wr_in)
            load(roww[:, :], ins["final_norm_w"].partition_broadcast(P), roww_in)
            pool.memset(vC[:, :, :, HD:HD + 1], 1.0).then_inc(fills, 1)
            minus_half = small[:, 224:256]
            pool.memset(minus_half, -0.5).then_inc(fills, 1)

            def power(n, count):
                pool.wait_ge(pow_arg, count)
                pool.tensor_tensor(small[:, 32:32 + n], small[:, 0:n], minus_half[:, 0:n], ALU.pow).then_inc(pow_res, 1)

            pool.wait_ge(w_in_slot[1], 16)
            rest = const[:, 2 * P:]
            load(rest, ins["consts"][:, 2 * P:], consts_in)
            pool.wait_ge(fills, 2)
            with pool.Fori(0, DEPTH) as l:
                for i, n in enumerate((2, 8, 8)):
                    power(n, l * POW_L + (i + 1))
            base_pow = DEPTH * POW_L
            pow_count = [base_pow]

            def power2(n):
                pow_count[0] += 1
                power(n, pow_count[0])

            pool.wait_ge(sc_ready, DEPTH * SC_L)
            pool.memset(lru_w[:, :, :], 0.0).then_inc(lru_w_zero, 1)
            power2(4)
            pool.wait_ge(x_ready, DEPTH + 2)
            load(roww[:, :], ins["norm2_g_2"][0].partition_broadcast(P), roww_in)
            power2(20)
            power2(4)
            pool.wait_ge(x_ready, DEPTH + 3)
            pool.memset(bias[:, :, :], 0.0).then_inc(bias_zero, 1)
            pool.wait_ge(bias_zero, 1)
            load(bias[0:E, 0, :], ins["b_gate_2"][0], bias_in)
            load(bias[0:E, 1, :], ins["b_up_2"][0], bias_in)
            load(bdown[:, :], ins["b_down_2"][0], bdown_in)
            power2(2)
            pool.wait_ge(xn_ready, DEPTH + 2)
            load(roww[:, :], ins["final_g_2"].partition_broadcast(P), roww_in)
            power2(2)

        @block.scalar
        def _(act):
            A = nc.scalar.activation
            def load(dst, src, s, **kw):
                act.dma_start(dst, src, **kw).then_inc(s, 16)

            for l in range(DEPTH):
                r = N_ROWS1 * l
                load(rows[r:r + 8, :], ins["norm_w"][l].rearrange("(c p) -> c p", p=P), params_in)
                load(rows[r + 8:r + 24, :], ins["conv_w"][l].rearrange("t (c p) -> (t c) p", p=P), params_in)
                load(rows[r + 24:r + 28, :], ins["conv_b"][l].rearrange("(c p) -> c p", p=P), params_in)
            for name, key, pat in (("norm1_g_2", "norm1", "(c p) -> c p"), ("conv_w_2", "conv_w", "t (c p) -> (t c) p"),
                                   ("conv_b_2", "conv_b", "(c p) -> c p"), ("lru_ba_2", "ba", "d (c p) -> (d c) p"),
                                   ("lru_bi_2", "bi", "d (c p) -> (d c) p"), ("lru_lam_2", "lam", "d (c p) -> (d c) p"),
                                   ("attn_out_g_2", "attn_g", "(c p) -> c p"), ("lru_out_g_2", "lru_g", "(c p) -> c p"),
                                   ("norm2_g_2", "norm2", "(c p) -> c p")):
                src = ins[name][0].rearrange(pat, p=P)
                load(rows[COL2[key]:COL2[key] + src.shape[0], :], src, params_in)
            load(gb_all[:, :, :], ins["gate_bias"].rearrange("l (g h) -> h l g", g=2), params_in,
                 allow_slow_non_contiguous=True)
            load(hw_all[:, :, 0, :], ins["ret_norm_w"].partition_broadcast(P), params_in)
            load(hw_all[:, :, 1, :], ins["mlstm_norm_w"].partition_broadcast(P), params_in)
            load(qkw[:, 0, :], ins["q_norm_g_2"][0].partition_broadcast(P), params_in)
            load(qkw[:, 1, :], ins["k_norm_g_2"][0].partition_broadcast(P), params_in)
            load(brout[:, :], ins["b_router_2"][0].partition_broadcast(P), params_in)
            act.wait_ge(x_in, 16)
            act.wait_ge(fills, 2)

            hT_rows = hT[:, :, :].rearrange("p (c k) s -> p c (k s)", c=TC)

            def squares(s, ready, src, unread, at=64):
                act.wait_ge(s, ready)
                for c in range(TC):
                    i = A(unread[:, c, :], src[:, c, :], ACT.Square, accum_out=small[:, at + c:at + 1 + c])
                i.then_inc(act_res, 1)

            with act.Fori(0, DEPTH) as l:
                def unit(u):
                    act.wait_ge(pj_ready, l * PJ_L + (PJ_0 + u + 1))
                    return PJ[u % 4]

                def used(i):
                    i.then_inc(pj_used, 1)

                def arg(n):
                    act.wait_ge(act_arg, l * ARG_L + n)

                def result(i):
                    i.then_inc(act_res, 1)

                def softmax_exp(pair):
                    arg(5 + pair)
                    for h in (2 * pair, 2 * pair + 1):
                        for j, (a, b) in enumerate(((0, P), (P, CAUSAL))):
                            n = 2 * (h % 4) + j
                            i = A(prob[:, h % 4, a:b], prob[:, h % 4, a:b], ACT.Exp, bias=small[:, 96 + n:97 + n],
                                  accum_out=small[:, 104 + n:105 + n])
                    result(i)

                squares(x_ready, l + 1, x, xn)
                for c in range(TC):
                    b = unit(c)
                    A(cg[:, c, :], b[:, 0:264], ACT.Copy)
                    used(A(eC[:, c, 256:512], b[:, 0:256], ACT.Tanh, scale=0.5))
                for c in range(2):
                    b = unit(2 + c)
                    used(A(rawC[:, 2 * c:2 * c + 2, 3:3 + S], b[:, :].rearrange("p (c s) -> p c s", c=2), ACT.Copy))
                arg(1)
                result(A(rw[:, 3, :], rw[:, 2, :], ACT.Exp))
                for c in range(2):
                    b = unit(4 + c)
                    used(A(qkA[:, 2 * c:2 * c + 2, :], b[:, :].rearrange("p (c s) -> p c s", c=2), ACT.Copy, scale=SCALE))
                arg(2)
                result(A(rw[:, 5, :], rw[:, 4, :], ACT.Ln))
                for c in range(2):
                    b = unit(6 + c)
                    used(A(qkA[:, 4 + 2 * c:6 + 2 * c, :], b[:, :].rearrange("p (c s) -> p c s", c=2), ACT.Copy))
                arg(3)
                result(A(eg[:, :, :], qkC[:, :, :], ACT.Tanh, scale=0.5))
                arg(4)
                result(A(rw[:, 1, :], rw[:, 2, :], ACT.Exp, scale=-1.0))
                for c in range(TC):
                    b = unit(8 + c)
                    A(vC[:, c, :, 0:HD], b[:, 0:256].rearrange("p (h d) -> p h d", d=HD), ACT.Copy)
                    used(A(eC[:, c, 0:256], b[:, 256:512], ACT.Tanh, scale=0.5))
                for pair in range(2):
                    act.wait_ge(sc_used, l * SC_L + (pair + 1))
                    w = wC[:, 2 * pair:2 * pair + 2, :]
                    result(A(w, w, ACT.Exp, scale=-1.0))
                for c in range(TC):
                    b = unit(10 + c)
                    used(A(vA[:, c, :], b[:, :], ACT.Copy))
                softmax_exp(0)
                act.wait_ge(qkC_ready, l + 1)
                for c in range(2):
                    b = unit(12 + c)[:, :].rearrange("p (c s) -> p c s", c=2)
                    A(agT[:, 2 * c:2 * c + 2, :], b, ACT.Copy)
                    used(A(eg[:, 2 * c:2 * c + 2, :], b, ACT.Tanh, scale=0.5))
                softmax_exp(1)
                for c in range(2):
                    b = unit(14 + c)
                    used(A(rawB[:, 2 * c:2 * c + 2, :], b[:, :].rearrange("p (c s) -> p c s", c=2), ACT.Copy))
                softmax_exp(2)
                for c in range(TC):
                    b = unit(16 + c)
                    A(vgB[:, c, :], b[:, :], ACT.Copy)
                    used(A(eB[:, c, :], b[:, 256:512], ACT.Tanh, scale=0.5))
                softmax_exp(3)
            n_arg = [DEPTH * ARG_L]

            def arg2():
                n_arg[0] += 1
                act.wait_ge(act_arg, n_arg[0])

            def unit2(u):
                act.wait_ge(pj_ready, DEPTH * PJ_L + PJ_0 + u + 1)
                return PJ[u % 4]

            def used2(i):
                i.then_inc(pj_used, 1)

            act.wait_ge(lru_w_zero, 1)
            for g, name in enumerate(("lru_wa_2", "lru_wi_2")):
                for d in range(2):
                    for j in range(2):
                        act.dma_start(lru_w[HD * j:HD * (j + 1), 8 * d + 4 * g:8 * d + 4 * g + 4, HD * j:HD * (j + 1)],
                                      ins[name][0, d].rearrange("(c j) i o -> j i c o", j=2)[j]).then_inc(lru_w_in, 16)
            squares(x_ready, DEPTH + 1, x, hT_rows)
            squares(xw_ready, 1, xn, mem1[:, :].rearrange("p (c d) -> p c d", c=TC), 66)
            arg2()
            A(lam(1), lam(0), ACT.Exp).then_inc(act_res, 1)
            arg2()
            A(lam(3), lam(2), ACT.Ln).then_inc(act_res, 1)
            for c in range(2):
                b = unit2(c)
                used2(A(lraw[:, 2 * c:2 * c + 2, 2:2 + S], b[:, :].rearrange("p (c s) -> p c s", c=2), ACT.Copy))
            for c in range(TC):
                b = unit2(2 + c)
                A(qk[:, c, 8:10, :], b[:, 0:P].rearrange("p (g d) -> p g d", d=HD), ACT.Copy)
                used2(A(v2[:, c, :], b[:, P:2 * P], ACT.Copy))
            for d in range(2):
                for g in range(2):
                    for h in range(2):
                        b = unit2(4 + 4 * d + 2 * g + h)
                        for j in range(2):
                            c = 2 * h + j
                            i = A(gate[d][g][:, c, :], b[:, S * j:S * (j + 1)], ACT.Tanh, scale=0.5,
                                  bias=half_b[:, 8 * g + 4 * d + c:8 * g + 4 * d + c + 1])
                        used2(i)
            for d in range(2):
                arg2()
                A(decay2[d][:, :, :], gate[d][0][:, :, :], ACT.Exp)
                A(gate[d][0][:, :, :], gate[d][0][:, :, :], ACT.Tanh).then_inc(act_res, 1)
            for c in range(TC):
                b = unit2(12 + c)
                used2(A(qk[:, c, 0:8, :].rearrange("p (j g) d -> p g j d", g=2),
                        b[:, :].rearrange("p (g j d) -> p g j d", g=2, d=HD), ACT.Copy))
            for d in range(2):
                arg2()
                A(gate[d][0][:, :, :], gate[d][0][:, :, :], ACT.Sqrt, scale=-1.0).then_inc(act_res, 1)
            for c in range(2):
                b = unit2(14 + c)
                used2(A(gel[:, 2 * c:2 * c + 2, :], b[:, :].rearrange("p (c s) -> p c s", c=2), ACT.Gelu_apprx_tanh))
            for pair in range(4):
                arg2()
                for j in range(2):
                    for c in range(TC):
                        n = 2 * j + c
                        i = A(p2[:, 2 * (pair % 2) + j, S * c:S * (c + 1)], SC[j][:, S * c:S * (c + 1)], ACT.Exp,
                              scale=SCALE, bias=neg2[:, 4 * (pair % 2) + n:4 * (pair % 2) + n + 1],
                              accum_out=sum2[:, 4 * (pair % 2) + n:4 * (pair % 2) + n + 1])
                i.then_inc(act_res, 1)
            for dst, src in ((sqL, gate[0][0]), (sqA, ao)):
                arg2()
                A(dst[:, :, :], src[:, :, :], ACT.Square).then_inc(act_res, 1)
            squares(x_ready, DEPTH + 3, x, xn)
            arg2()
            for c in range(TC):
                i = A(expL[:, c, :], logits[:, c, :], ACT.Exp, bias=negL[:, c:c + 1])
            i.then_inc(act_res, 1)

            act.sem_inc(ex["y_out"], 1)
            act.wait_ge(ex["xs"], 1)
            by_chunk = lambda a: a.rearrange("q (p c) -> q c p", c=4)
            as_chunks = lambda a: a.rearrange("q (c p) -> q c p", c=4)
            A(as_chunks(xs_sb), by_chunk(XS[:, :]), ACT.Copy).then_inc(ex["xs_out"], 1)
            act.wait_ge(count_ready, 2)
            with act.Fori(0, E) as e:
                first = act.value_load(n_before[0:1, bass.ds(e, 1)], min_val=0, max_val=16)
                more = act.value_load(n_more[0:1, bass.ds(e, 1)], min_val=0, max_val=3)
                with act.If(more > 0):
                    with act.Fori(0, more) as b:
                        j = first + b
                        pe_at = lambda n: act.wait_ge(ex["pe"], j * 7 + n)
                        dve_at = lambda n: act.wait_ge(ex["dve"], j * 7 + n)
                        pe_at(1)
                        A(as_chunks(xs_sb), by_chunk(XS[:, :]), ACT.Copy).then_inc(ex["act"], 1)
                        dve_at(3)
                        A(tanh_g, g_sb, ACT.Tanh, scale=SWIGLU_ALPHA / 2).then_inc(ex["act"], 1)
                        pe_at(4)
                        A(hT_sb, HTB[:, :], ACT.Copy).then_inc(ex["act"], 1)
                        pe_at(5)
                        A(yx_sb, YB[:, :], ACT.Copy).then_inc(ex["act"], 1)
                act.wait_ge(ex["gc"], e + 1)
                A(tanh_g, g_sb, ACT.Tanh, scale=SWIGLU_ALPHA / 2).then_inc(ex["eg"], 1)
                act.wait_ge(ex["xs"], e + 2)
                A(as_chunks(xs_sb), by_chunk(XS[:, :]), ACT.Copy).then_inc(ex["xs_out"], 1)
                act.wait_ge(ex["ht"], e + 1)
                A(hT_sb, HTB[:, :], ACT.Copy).then_inc(ex["ht_out"], 1)
                act.wait_ge(w_used, e * EXPERT_TURNS + EXPERT_TURNS)
                act.wait_ge(ex["o"], e * 2 + 2)
                A(y_sb, YB[:, :], ACT.Copy).then_inc(ex["y_out"], 1)
            squares(x_ready, DEPTH + 4, x, hT_rows)

        @block.tensor
        def _(pe):
            mm = nc.tensor.matmul
            tp = nc.tensor.transpose

            def arrived(slot, n):
                pe.wait_ge(w_in_slot[slot], n * 16)

            def slot_cols(slot, n):
                return ring[:, slot, 0:KC * n].rearrange("p (k n) -> p k n", n=n)

            def project_T(b, w, c, n=2):
                for j in range(n):
                    for k in range(KC):
                        i = mm(b[:, S * j:S * j + S], w[:, k, P * (c + j):P * (c + j + 1)], hT[:, k, :],
                               start=(k == 0), stop=(k == KC - 1))
                return i

            def project(b, w, c, n):
                for k in range(KC):
                    i = mm(b[:, 0:n], hT[:, k, P * c:P * (c + 1)], w[:, k, 0:n], start=(k == 0), stop=(k == KC - 1))
                return i

            def causal_scores(b, stationary, moving, r):
                mm(b[:, 0:S], stationary[r:r + HD, 0:P], moving[r:r + HD, :], start=True, stop=True)
                return mm(b[:, S:CAUSAL], stationary[r:r + HD, P:S], moving[r:r + HD, P:S], start=True, stop=True,
                          skip_group_check=True)

            pe.sem_inc(pj_ready, PJ_0)
            pe.sem_inc(out_ready, OUT_0)
            pe.wait_ge(params_in, 16 * N_PARAM_LOADS)
            pe.wait_ge(ident_in, 16)
            tp(TR[1][:, 0:N_ROWS], rows[0:N_ROWS, :], ident[0:N_ROWS, 0:N_ROWS]).then_inc(tr_ready, 1)

            with pe.Fori(0, DEPTH) as l:
                def pj(u):
                    if u >= 4:
                        pe.wait_ge(pj_used, l * PJ_L + (u - 3))
                    return PJ[u % 4]

                def tr(u):
                    pe.wait_ge(tr_used, l * TR_L + max(u, 1))
                    return TR[u % 2]

                def sc(u):
                    if u >= 2:
                        pe.wait_ge(sc_used, l * SC_L + (u - 1))
                    return SC[u % 2]

                def group(g, kind):
                    slot, n = g % SLOTS, IN_GROUPS[g][1]
                    arrived(slot, l * in_loads[slot] + (g // SLOTS + 1))
                    w = slot_cols(slot, n)
                    for j in range(2):
                        b = pj(2 * g + j)
                        i = project_T(b, w, 2 * j) if kind == "T" else project(b, w, j, n)
                        i.then_inc(pj_ready, 1)

                def a_scores(pair):
                    u = [6, 10, 12, 15][pair]
                    banks = [sc(u), sc(u + 1)]
                    q, k = qkA[:, pair, :], qkA[:, 4 + pair, :]
                    for j in range(2):
                        for b, r in zip(banks, (0, HD)):
                            i = mm(b[:, P * j:CAUSAL if j else P], q[r:r + HD, P * j:P * (j + 1)],
                                   k[r:r + HD, 0:P * (j + 1)], start=True, stop=True, skip_group_check=True)
                            if j:
                                i.then_inc(sc_ready, 1)

                def a_turn(pair):
                    pe.wait_ge(probs_ready, l * 4 + (pair + 1))
                    for h in (2 * pair, 2 * pair + 1):
                        b = tr([6, 8, 10, 13][pair] + h % 2)
                        for j in range(3):
                            i = tp(b[:, P * j:P * (j + 1)], prob[:, h % 4, P * j:P * (j + 1)], ident)
                        i.then_inc(tr_ready, 1)

                def a_out(pair):
                    b = sc([14, 17, 24, 25][pair])
                    pe.wait_ge(tr_used, l * TR_L + [9, 11, 13, 16][pair])
                    for kc in range(2):
                        for j in range(2):
                            h = 2 * pair + j
                            src = probT[:, j, 0:S] if kc == 0 else probT[:, j, S:CAUSAL]
                            i = mm(b[HD * j:HD * (j + 1), P * kc:S], vA[:, kc, HD * h:HD * (h + 1)], src,
                                   start=(kc == 0), stop=(kc == 1), skip_group_check=True)
                    i.then_inc(sc_ready, 1)

                pe.wait_ge(xn_ready, l + 1)
                for u in range(4):
                    b = tr(u)
                    for k in (2 * u, 2 * u + 1):
                        for c in range(TC):
                            o = S * (k - 2 * u) + P * c
                            i = tp(b[:, o:o + P], xn[:, c, P * k:P * (k + 1)], ident)
                    i.then_inc(tr_ready, 1)
                pe.wait_ge(tr_used, l * TR_L + 5)
                group(0, "tok")
                group(1, "T")
                pe.wait_ge(pj_used, l * PJ_L + 2)
                b = tr(4)
                for g in range(2):
                    for c in range(TC):
                        i = tp(b[0:C_HEADS, S * g + P * c:S * g + P * (c + 1)],
                               cg[:, c, 256 + 4 * g:260 + 4 * g], ident)
                i.then_inc(tr_ready, 1)
                group(2, "T")
                group(3, "T")
                pe.wait_ge(act_res, l * RES_L + 5)
                pe.wait_ge(consts_in, 16)
                turned, b = tr(5), sc(0)
                row_head = K("row_head").rearrange("p (h n) -> p h n", h=C_HEADS)
                for pair in range(2):
                    b = sc(pair)
                    for j in range(2):
                        i = mm(b[:, S * j:S * (j + 1)], row_head[0:C_HEADS, 2 * pair + j, :], rw[:, 8, :],
                               start=True, stop=True, skip_group_check=True)
                    i.then_inc(sc_ready, 1)
                for g, row in enumerate((7, 1)):
                    for c in range(TC):
                        i = tp(turned[:, 8 * g + 4 * c:8 * g + 4 * c + 4], rw[:, row, P * c:P * (c + 1)],
                               ident[0:C_HEADS, 0:C_HEADS])
                i.then_inc(tr_ready, 1)
                group(4, "tok")
                pe.wait_ge(qkC_ready, l + 1)
                for h in range(C_HEADS):
                    causal_scores(sc(2 + h), qkC[:, 2 + h // 2, :], qkC[:, h // 2, :], HD * (h % 2)).then_inc(sc_ready, 1)
                pe.wait_ge(pj_used, l * PJ_L + 8)
                a_scores(0)
                group(5, "tok")
                pe.wait_ge(pj_used, l * PJ_L + 10)
                pe.wait_ge(sc_used, l * SC_L + 6)
                for c in range(TC):
                    b = sc(8 + c)
                    for h in range(C_HEADS):
                        o = b[:, (HD + 1) * h:(HD + 1) * (h + 1)]
                        lhs = [wC[:, h, 0:P]] if c == 0 else [wC[:, h, P:S], wC[:, h, S:CAUSAL]]
                        for s, w in enumerate(lhs):
                            i = mm(o, w, vC[:, s, h, :], start=(s == 0), stop=(s == len(lhs) - 1),
                                   skip_group_check=True)
                    i.then_inc(sc_ready, 1)
                a_scores(1)
                group(6, "T")
                a_turn(0)
                a_scores(2)
                group(7, "T")
                a_out(0)
                a_turn(1)
                a_scores(3)
                group(8, "tok")
                a_out(1)
                for c in range(2):
                    b = sc(18 + c)
                    for j in range(2):
                        i = mm(b[:, S * j:S * (j + 1)], K("swap"), rawB[:, 2 * c + j, :], start=True, stop=True,
                               skip_group_check=True)
                    i.then_inc(sc_ready, 1)
                a_turn(2)
                pe.wait_ge(yC_ready, l + 1)
                b = tr(12)
                for k in range(2):
                    for c in range(TC):
                        i = tp(b[:, S * k + P * c:S * k + P * (c + 1)], yBC[:, 4 * c + 2 * k:4 * c + 2 * k + 2, :], ident)
                i.then_inc(tr_ready, 1)
                pe.wait_ge(rotB_ready, l + 1)
                for h in range(B_HEADS):
                    causal_scores(sc(20 + h), rotB[:, 2 + h // 2, :], rotB[:, h // 2, :], HD * (h % 2)).then_inc(sc_ready, 1)
                a_out(2)
                a_turn(3)
                a_out(3)
                pe.wait_ge(sc_used, l * SC_L + 24)
                b = sc(26)
                for c in range(TC):
                    for h in range(B_HEADS):
                        o = b[:, 256 * c + HD * h:256 * c + HD * (h + 1)]
                        lhs = [sB[:, h, 0:P]] if c == 0 else [sB[:, h, P:S], sB[:, h, S:CAUSAL]]
                        for s, w in enumerate(lhs):
                            i = mm(o, w, vgB[:, s, HD * h:HD * (h + 1)], start=(s == 0), stop=(s == len(lhs) - 1),
                                   skip_group_check=True)
                i.then_inc(sc_ready, 1)

                pe.wait_ge(pj_used, l * PJ_L + 18)
                arrived(3, l * in_loads[3] + 2)
                arrived(4, l * in_loads[4] + 2)
                w = [slot_cols(3, 512), slot_cols(4, 512)]

                def out_rows(k, lhs, first=False, last=False):
                    for c in range(TC):
                        for h in range(2):
                            i = mm(PJ[2 * c + h][:, :], lhs[:, P * c:P * (c + 1)], w[h][:, k, :], start=first, stop=last)
                    return i

                pe.wait_ge(tr_used, l * TR_L + 14)
                for k in (6, 7):
                    out_rows(k, yT[:, k - 4, :], first=(k == 6))
                pe.wait_ge(sc_used, l * SC_L + 26)
                for k in range(4):
                    out_rows(k, agT[:, k, :])
                pe.wait_ge(yB_ready, l + 1)
                b = tr(15)
                for k in range(2):
                    for c in range(TC):
                        i = tp(b[:, S * k + P * c:S * k + P * (c + 1)], yBC[:, 4 * c + 2 * k:4 * c + 2 * k + 2, :], ident)
                i.then_inc(tr_ready, 1)
                pe.wait_ge(tr_used, l * TR_L + 17)
                out_rows(4, yT[:, 0, :])
                out_rows(5, yT[:, 1, :], last=True).then_inc(out_ready, 1)
            tr_n = [1 + DEPTH * TR_L]

            def tr2():
                pe.wait_ge(tr_used, tr_n[0] - 1)
                tr_n[0] += 1
                return TR[tr_n[0] % 2]

            def pj2(u):
                if u >= 4:
                    pe.wait_ge(pj_used, DEPTH * PJ_L + u - 3)
                return PJ[u % 4]

            def turn_tokens(s, ready, src):
                pe.wait_ge(s, ready)
                for u in range(4):
                    b = tr2()
                    for k in (2 * u, 2 * u + 1):
                        for c in range(TC):
                            o = S * (k - 2 * u) + P * c
                            i = tp(b[:, o:o + P], src[:, c, P * k:P * (k + 1)], ident)
                    i.then_inc(tr_ready, 1)
                pe.wait_ge(tr_used, tr_n[0])

            def group2(g, kind, u):
                slot, n = g, IN2_GROUPS[g][1]
                arrived(slot, DEPTH * in_loads[slot] + 1)
                w = slot_cols(slot, n)
                for j in range(2):
                    b = pj2(u + j)
                    i = project_T(b, w, 2 * j) if kind == "T" else project(b, w, j, n)
                    i.then_inc(pj_ready, 1)

            turn_tokens(xn_ready, DEPTH + 1, xn)
            group2(0, "T", 0)
            group2(1, "tok", 2)
            pe.wait_ge(lru_w_in, 16 * 8)
            pe.wait_ge(xc_ready, 1)
            for u in range(8):
                b = pj2(4 + u)
                for j in range(2):
                    i = mm(b[:, S * j:S * (j + 1)], lru_w[:, 2 * u + j, :], xc[:, 2 * (u % 2) + j, :], start=True,
                           stop=True, skip_group_check=True)
                i.then_inc(pj_ready, 1)
            group2(2, "tok", 12)
            group2(3, "T", 14)
            pe.wait_ge(qk_ready, 1)
            for chunks in ((4,), (0, 1), (2, 3)):
                b = tr2()
                for n, ch in enumerate(chunks):
                    for c in range(TC):
                        i = tp(b[:, S * n + P * c:S * n + P * (c + 1)], qk[:, c, 2 * ch:2 * ch + 2, :], ident)
                i.then_inc(tr_ready, 1)
            pe.wait_ge(tr_used, tr_n[0])

            def scores2(pair):
                if pair:
                    pe.wait_ge(act_res, DEPTH * RES_L + 8 + pair)
                for c in range(TC):
                    for j in range(2):
                        r = HD * j
                        i = mm(SC[j][:, S * c:S * (c + 1)], qkT[r:r + HD, pair, P * c:P * (c + 1)], qkT[r:r + HD, 4, :],
                               start=True, stop=True, skip_group_check=True)
                        if c:
                            i.then_inc(sc_ready, 1)

            def turn2(pair):
                pe.wait_ge(probs_ready, DEPTH * 4 + pair + 1)
                for j in range(2):
                    b = tr2()
                    for kc in range(2):
                        for c in range(TC):
                            i = tp(b[:, S * kc + P * c:S * kc + P * (c + 1)],
                                   p2[:, 2 * (pair % 2) + j, S * c + P * kc:S * c + P * (kc + 1)], ident)
                    i.then_inc(tr_ready, 1)

            def out2(pair):
                pe.wait_ge(tr_used, tr_n[0])
                b = tr2()
                r = HD * (pair % 2)
                for j in range(2):
                    for kc in range(2):
                        i = mm(b[r:r + HD, S * j:S * (j + 1)], v2[:, kc, HD * j:HD * (j + 1)],
                               pT2[:, j, S * kc:S * (kc + 1)], start=(kc == 0), stop=(kc == 1), skip_group_check=True)
                i.then_inc(tr_ready, 1)

            w = [slot_cols(4, 512), slot_cols(5, 512)]

            def attn_rows(ks, first):
                pe.wait_ge(y2_ready, 1 if first else 2)
                for n, k in enumerate(ks):
                    for c in range(TC):
                        for h in range(2):
                            i = mm(PJ[2 * c + h][:, :], yT[:, k, P * c:P * (c + 1)], w[h][:, k, :],
                                   start=(first and n == 0), stop=(not first and n == 1))
                return i

            scores2(0)
            scores2(1)
            turn2(0)
            scores2(2)
            out2(0)
            turn2(1)
            scores2(3)
            out2(1)
            turn2(2)
            arrived(4, DEPTH * in_loads[4] + 1)
            arrived(5, DEPTH * in_loads[5] + 1)
            pe.wait_ge(pj_used, DEPTH * PJ_L + 16)
            attn_rows((0, 2), True)
            out2(2)
            turn2(3)
            out2(3)
            attn_rows((1, 3), False).then_inc(out_ready, 1)
            pe.wait_ge(act_res, DEPTH * RES_L + 14)
            b = tr2()
            for s, sq in enumerate((sqA, sqL)):
                for c in range(TC):
                    for k in range(LC):
                        i = mm(b[:, 2 * s + c:2 * s + c + 1], sq[:, k, P * c:P * (c + 1)], ones[:, 0:1], start=(k == 0),
                               stop=(k == LC - 1), skip_group_check=True)
            i.then_inc(tr_ready, 1)
            pe.wait_ge(lru_ready, 1)
            for n, (c, h) in enumerate(((0, 0), (0, 1), (1, 0), (1, 1))):
                if n == 2:
                    pe.wait_ge(tr_used, tr_n[0])
                for k in range(4, 8):
                    i = mm(LB[n][:, :], yT[:, k, P * c:P * (c + 1)], w[h][:, k, :], start=(k == 4), stop=(k == 7))
                i.then_inc(out_ready, 1)

            turn_tokens(x_ready, DEPTH + 3, x)
            pe.wait_ge(wr_in, 16)
            for c in range(TC):
                for k in range(KC):
                    i = mm(PJ[0][:, E * c:E * (c + 1)], hT[:, k, P * c:P * (c + 1)], wr[:, k, :],
                           start=(k == 0), stop=(k == KC - 1), skip_group_check=True)
            i.then_inc(out_ready, 1)
            pe.wait_ge(mask_ready, 1)
            before = K("before")
            mm(PJ[1][:, 0:E], before, mask[:, 0, :], start=True, stop=True)
            mm(PJ[1][:, E:2 * E], ones, mask[:, 0, :], start=True, stop=False, skip_group_check=True)
            mm(PJ[1][:, E:2 * E], before, mask[:, 1, :], start=False, stop=True, skip_group_check=True)
            mm(PJ[1][:, 2 * E:3 * E], ones, mask[:, 0, :], start=True, stop=False, skip_group_check=True)
            mm(PJ[1][:, 2 * E:3 * E], ones, mask[:, 1, :], start=False, stop=True, skip_group_check=True).then_inc(out_ready, 1)
            pe.wait_ge(gates_ready, 1)
            b = tr2()
            for c in range(TC):
                i = tp(b[0:E, P * c:P * (c + 1)], gates[:, c, :], ident)
            i.then_inc(tr_ready, 1)
            pe.wait_ge(tr_used, tr_n[0])
            pe.wait_ge(bdown_in, 16)
            for c in range(TC):
                for h in range(2):
                    if (c, h) == (0, 1):
                        pe.wait_ge(gates_ready, 2)
                    i = mm(PJ[2 * c + h][:, :], gatesT[:, P * c:P * (c + 1)], bdown[:, 512 * h:512 * (h + 1)],
                           start=True, stop=True)
            i.then_inc(out_ready, 1)

            def halves(f):
                for n in range(2):
                    i = f(n, slice(T * n, T * (n + 1)))
                return i

            def gather(sel):
                for c in range(TC):
                    i = halves(lambda n, at: mm(XS[at, :], sel[:, c, :], xn[:, c, 512 * n:512 * (n + 1)],
                                                start=(c == 0), stop=(c == TC - 1), skip_group_check=True))
                return i

            def turn4(dst, src):
                for c in range(4):
                    i = tp(dst[:, P * c:P * (c + 1)], src[:, P * c:P * (c + 1)], ident)
                return i

            def product(dst, slot, lhs, h, done):
                w = ring[:, slot, :].rearrange("p (c n) -> p c n", c=4)
                for c in range(4):
                    i = halves(lambda n, at: mm(dst[at, :], lhs[:, c, T * h:T * (h + 1)], w[:, c, 512 * n:512 * (n + 1)],
                                                start=(h == 0 and c == 0), stop=(done and h == 1 and c == 3),
                                                skip_group_check=True))
                return i

            def biases():
                for m, dst in enumerate((GB, UB)):
                    i = halves(lambda n, at: mm(dst[at, :], bsel[:, :], bias[:, m, 512 * n:512 * (n + 1)],
                                                start=False, stop=True, skip_group_check=True))
                return i

            def add_up(c, gT, y):
                return halves(lambda n, at: mm(OB[n][:, :], gT[at, P * c:P * (c + 1)], y[at, :], start=True, stop=True))

            def turn_gates(i=None):
                for c in range(TC):
                    i = tp(XS[:, P * c:P * (c + 1)], selg[:, c, :], ident)
                return i

            chunked = lambda a: a.rearrange("p (c q) -> p c q", c=4)
            slot_base = [(DEPTH * in_loads[s] + 1) for s in range(SLOTS)]
            pe.wait_ge(ex["sel"], 1)
            gather(sel).then_inc(ex["xs"], 1)
            pe.wait_ge(ex["xs_out"], 1)
            turn4(XTB, xs_sb).then_inc(ex["xt"], 1)
            pe.wait_ge(count_ready, 2)
            pe.wait_ge(bias_in, 32)
            with pe.Fori(0, E) as e:
                first = pe.value_load(n_before[0:1, bass.ds(e, 1)], min_val=0, max_val=16)
                more = pe.value_load(n_more[0:1, bass.ds(e, 1)], min_val=0, max_val=3)

                def weights(turn):
                    arrived(turn, e + (slot_base[turn] + 1))

                with pe.If(more > 0):
                    with pe.Fori(0, more) as b:
                        j = first + b
                        up = lambda i: i.then_inc(ex["pe"], 1)
                        act_at = lambda n: pe.wait_ge(ex["act"], j * 4 + n)
                        dve_at = lambda n: pe.wait_ge(ex["dve"], j * 7 + n)
                        dve_at(1)
                        up(gather(sel))
                        act_at(1)
                        up(turn4(XTB, xs_sb))
                        dve_at(2)
                        pe.wait_ge(ex["bsel"], e + 1)
                        for turn in range(4):
                            weights(turn)
                            product((GB, UB)[turn % 2], turn, chunked(xTx), turn // 2, False)
                        up(biases())
                        dve_at(4)
                        turn_gates()
                        up(turn4(HTB, h_sb))
                        act_at(3)
                        pe.wait_ge(ex["y_out"], e + 1)
                        for h in range(2):
                            weights(4 + h)
                            i = product(YB, 4 + h, chunked(hT_sb), h, True)
                        up(i)
                        act_at(4)
                        dve_at(5)
                        up(add_up(0, gTx, yx_sb))
                        dve_at(6)
                        up(add_up(1, gTx, yx_sb))

                pe.wait_ge(ex["xt_out"], e + 1)
                pe.wait_ge(ex["bsel"], e + 1)
                for turn in range(4):
                    weights(turn)
                    product((GB, UB)[turn % 2], turn, chunked(xT), turn // 2, False).then_inc(w_used, 1)
                biases().then_inc(ex["gu"], 1)
                pe.wait_ge(ex["sel"], e + 2)
                gather(sel).then_inc(ex["xs"], 1)
                pe.wait_ge(ex["y_out"], e + 1)
                pe.wait_ge(ex["gt_out"], e + 1)
                add_up(0, gT, y_sb).then_inc(ex["o"], 1)
                pe.wait_ge(ex["xs_out"], e + 2)
                turn4(XTB, xs_sb).then_inc(ex["xt"], 1)
                pe.wait_ge(ex["h"], e + 1)
                turn4(HTB, h_sb).then_inc(ex["ht"], 1)
                pe.wait_ge(ex["ht_out"], e + 1)
                for h in range(2):
                    weights(4 + h)
                    product(YB, 4 + h, chunked(hT_sb), h, True).then_inc(w_used, 1)
                pe.wait_ge(ex["acc"], e * 2 + 1)
                add_up(1, gT, y_sb).then_inc(ex["o"], 1)
                pe.wait_ge(ex["selg"], e + 1)
                turn_gates().then_inc(ex["gt"], 1)
            pe.wait_ge(ex["y_out"], E + 1)
            pe.wait_ge(ex["gt_out"], E + 1)
            add_up(0, gT, y_sb).then_inc(ex["o"], 1)
            pe.wait_ge(ex["acc"], 2 * E + 1)
            add_up(1, gT, y_sb).then_inc(ex["o"], 1)

        @block.vector
        def _(v):
            tt, ts, stt = v.tensor_tensor, v.tensor_scalar, v.scalar_tensor_tensor

            def bc(a, n):
                return a.unsqueeze(2).to_broadcast([a.shape[0], a.shape[1], n])

            v.wait_ge(tr_ready, 1)
            v.tensor_copy(cols_all[:, 0:N_ROWS], TR[1][:, 0:N_ROWS]).then_inc(tr_used, 1)
            v.wait_ge(tr_used, 1)
            v.wait_ge(x_in, 16)
            v.sem_inc(x_ready, 1)

            with v.Fori(0, DEPTH) as l:
                st = Steps(v, dve_step, l * STEPS_L)

                def arg(i):
                    i.then_inc(act_arg, 1)

                def result(n):
                    v.wait_ge(act_res, l * RES_L + n)

                def tr(u):
                    v.wait_ge(tr_ready, l * TR_L + (u + 2))
                    return TR[u % 2]

                def tr_done(i):
                    i.then_inc(tr_used, 1)

                def sc(u):
                    v.wait_ge(sc_ready, l * SC_L + (u + 1))
                    return SC[u % 2]

                def sc_done(i):
                    i.then_inc(sc_used, 1)

                def gated(out, tanh, z):
                    return stt(out=out, in0=tanh, scalar=1.0, in1=z, op0=ALU.add, op1=ALU.mult)

                def head_norm(w, gate, nth, ready):
                    s = small[:, 128:136]
                    flat = yBC.rearrange("p (c h) d -> p c (h d)", c=TC)
                    st.do(v.tensor_reduce(s, yBC, AX, ALU.add))
                    st.do(ts(s, s, 1.0 / HD, None, ALU.mult))
                    st.do(tt(yBC, yBC, bc(s, HD), ALU.subtract))
                    st.do(tt(tmp, yBC, yBC, ALU.mult))
                    st.do(v.tensor_reduce(s, tmp, AX, ALU.add))
                    ts(small[:, 0:8], s, 1.0 / HD, HEAD_EPS, ALU.mult, ALU.add).then_inc(pow_arg, 1)
                    st.do(tt(flat, flat, w.unsqueeze(1).to_broadcast([P, TC, 256]), ALU.mult))
                    st.do(tt(flat, flat, gate, ALU.mult))
                    v.wait_ge(pow_res, l * POW_L + nth)
                    stt(out=yBC, in0=yBC, scalar=0.5, in1=bc(small[:, 32:40], HD), op0=ALU.mult,
                        op1=ALU.mult).then_inc(ready, 1)

                st.go(v.tensor_copy(cols[:, 0:N_ROWS1], cols_all[:, bass.ds(l * N_ROWS1, N_ROWS1)]))
                st.go(v.tensor_copy(gb[:, :], gb_all[:, bass.ds(l, 1), :].rearrange("p a b -> p (a b)")))
                st.go(v.tensor_copy(hw[:, :, :], hw_all[:, bass.ds(l, 1), :, :].rearrange("p a b c -> p (a b) c")))
                st.go(v.memset(rawC[:, :, 0:3], 0.0))
                result(1)
                ts(small[:, 0:2], small[:, 64:66], 1.0 / D, RMS_EPS, ALU.mult, ALU.add).then_inc(pow_arg, 1)
                v.wait_ge(pow_res, l * POW_L + 1)
                st.go(ts(xn[:, 0, :], x[:, 0, :], small[:, 32:33], None, ALU.mult))
                ts(xn[:, 1, :], x[:, 1, :], small[:, 33:34], None, ALU.mult).then_inc(xn_ready, 1)
                st.wait()
                for u in range(4):
                    b = tr(u)
                    st.go(ts(hT[:, 2 * u, :], b[:, 0:S], cols[:, 2 * u:2 * u + 1], None, ALU.mult))
                    tr_done(ts(hT[:, 2 * u + 1, :], b[:, S:512], cols[:, 2 * u + 1:2 * u + 2], None, ALU.mult))
                b = tr(4)
                st.go(ts(rw[:, 0, :], b[0:C_HEADS, 0:S], gb[:, 0:1], None, ALU.add))
                tr_done(ts(rw[:, 1, :], b[0:C_HEADS, S:512], gb[:, 1:2], None, ALU.add))
                v.wait_ge(tr_used, l * TR_L + 6)
                st.do(ts(rw[:, 2, :], rw[:, 1, :], -1.0, None, ALU.mult))
                arg(tt(rw[:, 2, :], rw[:, 1, :], rw[:, 2, :], ALU.min))
                result(2)
                arg(ts(rw[:, 4, :], rw[:, 3, :], 1.0, None, ALU.add))
                v.wait_ge(pj_used, l * PJ_L + 4)
                w = lambda j, c: cols[:, COL1["conv_w"] + 4 * j + c:COL1["conv_w"] + 4 * j + c + 1]
                for j in range(4):
                    for c in range(4):
                        if j == 0:
                            i = ts(qkC[:, c, :], rawC[:, c, 0:S], w(0, c),
                                   cols[:, COL1["conv_b"] + c:COL1["conv_b"] + c + 1], ALU.mult, ALU.add)
                        else:
                            i = stt(out=qkC[:, c, :], in0=rawC[:, c, j:j + S], scalar=w(j, c), in1=qkC[:, c, :],
                                    op0=ALU.mult, op1=ALU.add)
                        if (j, c) == (3, 3):
                            arg(i)
                        else:
                            st.go(i)
                    if j < 3:
                        st.wait()
                result(3)
                st.do(ts(rw[:, 6, :], rw[:, 4, :], -1.0, None, ALU.add))
                st.do(ts(rw[:, 7, :], rw[:, 6, :], 0.0, None, ALU.is_equal))
                st.go(tt(rw[:, 5, :], rw[:, 5, :], rw[:, 7, :], ALU.add))
                st.do(tt(rw[:, 6, :], rw[:, 6, :], rw[:, 7, :], ALU.add))
                st.go(tt(rw[:, 5, :], rw[:, 5, :], rw[:, 3, :], ALU.mult))
                st.go(v.memset(rw[:, 7, :], 1.0))
                st.do(v.reciprocal(rw[:, 6, :], rw[:, 6, :]))
                st.do(tt(rw[:, 5, :], rw[:, 5, :], rw[:, 6, :], ALU.mult))
                st.do(stt(out=rw[:, 5, :], in0=rw[:, 1, :], scalar=0.0, in1=rw[:, 5, :], op0=ALU.min, op1=ALU.subtract))
                st.do(v.tensor_tensor_scan(rw[:, 6, :], rw[:, 7, :], rw[:, 5, :], 0.0, ALU.mult, ALU.add))
                st.do(tt(rw[:, 7, :], rw[:, 0, :], rw[:, 6, :], ALU.subtract))
                st.do(v.tensor_tensor_scan(rw[:, 8, :], rw[:, 7, :], rw[:, 7, :], 0.0, ALU.max, ALU.max))
                arg(tt(rw[:, 2, :], rw[:, 6, :], rw[:, 8, :], ALU.add))
                result(4)
                gated(qkC[:, :, :], eg[:, :, :], qkC[:, :, :]).then_inc(qkC_ready, 1)
                acol, emcol = small[:, 80:88], small[:, 88:96]
                b = tr(5)
                tr_done(v.tensor_copy(small[:, 80:96], b[:, 0:16]))
                v.wait_ge(tr_used, l * TR_L + 7)
                for pair in range(2):
                    b = sc(pair)
                    for j in range(2):
                        h = 2 * pair + j
                        st.go(ts(wC[:, h, 0:S], b[:, S * j:S * (j + 1)], acol[:, h:h + 1], 0.0, ALU.subtract, ALU.max))
                        i = ts(wC[:, h, S:CAUSAL], b[:, S * j + P:S * (j + 1)], acol[:, 4 + h:5 + h], 0.0,
                               ALU.subtract, ALU.max)
                        if j:
                            sc_done(i)
                        else:
                            st.go(i)
                v.wait_ge(pj_used, l * PJ_L + 10)
                st.go(gated(cg[:, :, 0:256], eC[:, :, 256:512], cg[:, :, 0:256]))
                result(7)
                blocks = wC.rearrange("p h (j n) -> p h j n", j=3)[:, :, 0:3:2, :]
                tri = K("tri").unsqueeze(1).unsqueeze(1).to_broadcast([P, C_HEADS, 2, P])
                v.wait_ge(consts_in, 16)
                st.do(tt(blocks, blocks, tri, ALU.mult))
                for h in range(C_HEADS):
                    b = sc(2 + h)
                    sc_done(stt(out=wC[:, h, :], in0=b[:, 0:CAUSAL], scalar=SCALE / 4, in1=wC[:, h, :],
                                op0=ALU.mult, op1=ALU.mult))

                def a_softmax(pair):
                    neg = small[:, 96 + 4 * (pair % 2):100 + 4 * (pair % 2)]
                    for j in range(2):
                        h = 2 * pair + j
                        b = sc([6, 10, 12, 15][pair] + j)
                        sc_done(stt(out=prob[:, h % 4, :], in0=K("dist"), scalar=-(2.0 ** (-8.0 * (h + 1) / A_HEADS)),
                                    in1=b[:, 0:CAUSAL], op0=ALU.mult, op1=ALU.add))
                        v.wait_ge(sc_used, l * SC_L + ([6, 10, 12, 15][pair] + j + 1))
                        st.go(v.tensor_reduce(neg[:, 2 * j:2 * j + 1], prob[:, h % 4, 0:P], AX, ALU.max))
                        st.go(v.tensor_reduce(neg[:, 2 * j + 1:2 * j + 2], prob[:, h % 4, P:CAUSAL], AX, ALU.max))
                    st.wait()
                    arg(ts(neg, neg, -1.0, None, ALU.mult))

                def a_normalise(pair):
                    result(8 + pair)
                    s = small[:, 104 + 4 * (pair % 2):108 + 4 * (pair % 2)]
                    st.do(v.reciprocal(s, s))
                    for j in range(2):
                        h = (2 * pair + j) % 4
                        st.go(ts(prob[:, h, 0:P], prob[:, h, 0:P], s[:, 2 * j:2 * j + 1], None, ALU.mult))
                        i = ts(prob[:, h, P:CAUSAL], prob[:, h, P:CAUSAL], s[:, 2 * j + 1:2 * j + 2], None, ALU.mult)
                        if j:
                            i.then_inc(probs_ready, 1)
                        else:
                            st.go(i)

                def a_turned(pair):
                    for j in range(2):
                        b = tr([6, 8, 10, 13][pair] + j)
                        tr_done(v.tensor_copy(probT[:, j, :], b[:, 0:CAUSAL]))

                def a_gate(pair):
                    b = sc([14, 17, 24, 25][pair])
                    sc_done(stt(out=agT[:, pair, :], in0=b[:, 0:S], scalar=0.5, in1=agT[:, pair, :], op0=ALU.mult,
                                op1=ALU.mult))

                a_softmax(0)
                a_normalise(0)
                den, rden = small[:, 112:120], small[:, 120:128]
                o = [sc(8 + c)[:, 0:(HD + 1) * C_HEADS].rearrange("p (h n) -> p h n", h=C_HEADS) for c in range(TC)]
                for c in range(TC):
                    st.go(v.tensor_copy(den[:, 4 * c:4 * c + 4].unsqueeze(2), o[c][:, :, HD:HD + 1]))
                st.wait()
                st.do(stt(out=rden, in0=den, scalar=-1.0, in1=den, op0=ALU.mult, op1=ALU.max))
                st.do(tt(rden, rden, emcol, ALU.max))
                st.do(ts(rden, rden, 2.0, None, ALU.mult))
                st.do(v.reciprocal(rden, rden))
                for c in range(TC):
                    sc_done(tt(yBC[:, 4 * c:4 * c + 4, :], o[c][:, :, 0:HD], bc(rden[:, 4 * c:4 * c + 4], HD), ALU.mult))
                v.wait_ge(sc_used, l * SC_L + 10)
                flat = yBC.rearrange("p (c h) d -> p c (h d)", c=TC)
                st.do(gated(flat, eC[:, :, 0:256], flat))
                head_norm(hw[:, 1, :], cg[:, :, 0:256], 2, yC_ready)
                a_softmax(1)
                a_normalise(1)
                a_turned(0)
                a_softmax(2)
                v.wait_ge(pj_used, l * PJ_L + 14)
                st.do(gated(agT[:, :, :], eg[:, :, :], agT[:, :, :]))
                a_normalise(2)
                a_gate(0)
                a_turned(1)
                a_softmax(3)
                v.wait_ge(pj_used, l * PJ_L + 16)
                table = lambda n: K(n).unsqueeze(1)
                st.go(tt(rotB, rawB, table("ret_cos").to_broadcast([P, 4, S]), ALU.mult))
                a_normalise(3)
                a_gate(1)
                for c in range(2):
                    b = sc(18 + c)
                    turned = tmp.rearrange("p g d -> p (g d)").rearrange("p (c s) -> p c s", c=2)
                    sc_done(tt(turned, b[:, :].rearrange("p (c s) -> p c s", c=2),
                               table("ret_sin").to_broadcast([P, 2, S]), ALU.mult))
                    v.wait_ge(sc_used, l * SC_L + (19 + c))
                    i = tt(rotB[:, 2 * c:2 * c + 2, :], rotB[:, 2 * c:2 * c + 2, :], turned, ALU.add)
                    if c:
                        i.then_inc(rotB_ready, 1)
                    else:
                        st.do(i)
                v.wait_ge(rotB_ready, l + 1)
                a_turned(2)
                b = tr(12)
                tr_done(v.tensor_copy(yT[:, 2:4, :], b[:, :].rearrange("p (c s) -> p c s", c=2)))
                decay = K("decay").rearrange("p (h n) -> p h n", h=B_HEADS)
                for h in range(B_HEADS):
                    b = sc(20 + h)
                    sc_done(tt(sB[:, h, :], b[:, 0:CAUSAL], decay[:, h, :], ALU.mult))
                a_gate(2)
                a_turned(3)
                a_gate(3)
                v.wait_ge(pj_used, l * PJ_L + 18)
                st.go(gated(vgB[:, :, 256:512], eB[:, :, :], vgB[:, :, 256:512]))
                b = sc(26)
                sc_done(v.tensor_copy(yBC, b[:, :].rearrange("p (g d) -> p g d", d=HD)))
                v.wait_ge(sc_used, l * SC_L + 27)
                head_norm(hw[:, 0, :], vgB[:, :, 256:512], 3, yB_ready)
                b = tr(15)
                tr_done(v.tensor_copy(yT[:, 0:2, :], b[:, :].rearrange("p (c s) -> p c s", c=2)))
                v.wait_ge(out_ready, l + (OUT_0 + 1))
                for c in range(TC):
                    for h in range(2):
                        i = tt(x[:, c, 512 * h:512 * (h + 1)], x[:, c, 512 * h:512 * (h + 1)], PJ[2 * c + h][:, :], ALU.add)
                        if c and h:
                            i.then_inc(x_ready, 1)
                        else:
                            st.go(i)
                v.wait_ge(x_ready, l + 2)
                assert st.n == STEPS_L, f"STEPS_L = {st.n}"
            st = Steps(v, dve_step, DEPTH * STEPS_L)
            res = Steps(v, act_res, DEPTH * RES_L)
            n_pow, n_tr = [DEPTH * POW_L], [1 + DEPTH * TR_L]

            def arg2(i):
                i.then_inc(act_arg, 1)

            def result2():
                res.n += 1
                res.wait()

            def powered(i):
                i.then_inc(pow_arg, 1)
                n_pow[0] += 1
                v.wait_ge(pow_res, n_pow[0])

            def tr2():
                n_tr[0] += 1
                v.wait_ge(tr_ready, n_tr[0])
                return TR[n_tr[0] % 2]

            def tr2_done(i):
                i.then_inc(tr_used, 1)

            def rstd(eps):
                powered(ts(small[:, 0:2], small[:, 64:66], 1.0 / D, eps, ALU.mult, ALU.add))

            def turned_tokens(scale):
                for u in range(4):
                    b = tr2()
                    if scale is None:
                        tr2_done(v.tensor_copy(hT[:, 2 * u:2 * u + 2, :], b[:, :].rearrange("p (c s) -> p c s", c=2)))
                    else:
                        st.go(ts(hT[:, 2 * u, :], b[:, 0:S], scale(2 * u), None, ALU.mult))
                        tr2_done(ts(hT[:, 2 * u + 1, :], b[:, S:512], scale(2 * u + 1), None, ALU.mult))

            col = lambda key, i, n=1: cols_all[:, COL2[key] + i:COL2[key] + i + n]
            v.wait_ge(roww_in, 16)
            for c in range(TC):
                i = tt(xn[:, c, :], x[:, c, :], roww[:, :], ALU.mult)
                i.then_inc(xw_ready, 1) if c else st.go(i)
            st.go(v.memset(lraw[:, :, 0:2], 0.0))
            st.go(v.memset(lraw[:, :, 2 + S:3 + S], 0.0))
            st.go(ts(half_b, col("ba", 0, 16), 0.5, None, ALU.mult))
            st.go(ts(lam(0), col("lam", 0, 8), -1.0, None, ALU.mult))
            result2()
            st.do(ts(small[:, 0:2], small[:, 64:66], 1.0 / D, RMS_EPS, ALU.mult, ALU.add))
            st.do(v.reciprocal(small[:, 2:4], small[:, 0:2]))
            result2()
            st.do(tt(small[:, 2:4], small[:, 2:4], small[:, 66:68], ALU.mult))
            powered(ts(small[:, 2:4], small[:, 2:4], 1.0 / D, NORM_EPS, ALU.mult, ALU.add))
            st.do(tt(small[:, 68:70], small[:, 32:34], small[:, 34:36], ALU.mult))
            for c in range(TC):
                i = ts(xn[:, c, :], xn[:, c, :], small[:, 68 + c:69 + c], None, ALU.mult)
                i.then_inc(xn_ready, 1) if c else st.go(i)
            for c in range(TC):
                i = stt(out=x[:, c, :], in0=x[:, c, :], scalar=small[:, 32 + c:33 + c], in1=roww[:, :], op0=ALU.mult,
                        op1=ALU.mult)
                i.then_inc(x_ready, 1) if c else st.go(i)
            st.wait()
            turned_tokens(lambda k: col("norm1", k))
            arg2(tt(lam(0), lam(0), col("lam", 0, 8), ALU.min))
            result2()
            arg2(ts(lam(2), lam(1), 1.0, None, ALU.add))
            v.wait_ge(act_arg, DEPTH * ARG_L + 2)
            st.do(ts(lam(4), lam(2), -1.0, None, ALU.add))
            st.do(ts(lam(5), lam(4), 0.0, None, ALU.is_equal))
            result2()
            st.go(tt(lam(3), lam(3), lam(5), ALU.add))
            st.do(tt(lam(4), lam(4), lam(5), ALU.add))
            st.go(tt(lam(3), lam(3), lam(1), ALU.mult))
            st.do(v.reciprocal(lam(4), lam(4)))
            st.go(tt(lam(3), lam(3), lam(4), ALU.mult))
            st.do(ts(lam(5), col("lam", 0, 8), -1.0, 0.0, ALU.mult, ALU.max))
            st.do(tt(lam(3), lam(3), lam(5), ALU.add))
            st.do(ts(lam(5), lam(3), -LRU_C / 2, None, ALU.mult))
            v.wait_ge(pj_used, DEPTH * PJ_L + 2)
            for j in range(4):
                for c in range(LC):
                    if j == 0:
                        i = ts(xc[:, c, :], lraw[:, c, 0:S], col("conv_w", c), col("conv_b", c), ALU.mult, ALU.add)
                    else:
                        i = stt(out=xc[:, c, :], in0=lraw[:, c, j:j + S], scalar=col("conv_w", 4 * j + c), in1=xc[:, c, :],
                                op0=ALU.mult, op1=ALU.add)
                    i.then_inc(xc_ready, 1) if (j, c) == (3, 3) else st.go(i)
                if j < 3:
                    st.wait()
            v.wait_ge(xc_ready, 1)

            for d in range(2):
                v.wait_ge(pj_used, DEPTH * PJ_L + 8 + 4 * d)
                c8 = lam(5)[:, 4 * d:4 * d + 4].unsqueeze(2).to_broadcast([P, LC, S])
                arg2(stt(out=gate[d][0][:, :, :], in0=gate[d][0][:, :, :], scalar=1.0, in1=c8, op0=ALU.add, op1=ALU.mult))
                st.go(stt(out=gate[d][1][:, :, :], in0=gate[d][1][:, :, :], scalar=1.0, in1=xc[:, :, :], op0=ALU.add,
                          op1=ALU.mult))
            for d in range(2):
                t = gate[d][0][:, :, :]
                result2()
                st.do(tt(sq2[:, :, :], decay2[d][:, :, :], decay2[d][:, :, :], ALU.mult))
                arg2(stt(out=t, in0=sq2[:, :, :], scalar=1.0, in1=t, op0=ALU.add, op1=ALU.mult))
                v.wait_ge(act_arg, DEPTH * ARG_L + 5 + d)
            wr_in_norm = wr[:, :, :]
            v.wait_ge(wr_in, 16)
            st.do(tt(wr_in_norm, wr_in_norm, bc(col("norm2", 0, KC), E), ALU.mult))

            def recurrence(d):
                st.do(stt(out=gate[d][1][:, :, :], in0=gate[d][1][:, :, :], scalar=0.5, in1=gate[d][0][:, :, :],
                          op0=ALU.mult, op1=ALU.mult))
                way = (lambda a: a[:, ::-1]) if d else (lambda a: a)
                for c in range(LC):
                    st.go(v.tensor_tensor_scan(way(gate[d][0][:, c, :]), way(decay2[d][:, c, :]), way(gate[d][1][:, c, :]),
                                               0.0, ALU.mult, ALU.add))

            def weighted(src, key, chunks, first, ready):
                for n, c in enumerate(chunks):
                    i = ts(yT[:, first + c, :], src[:, c, :], col(key, c), None, ALU.mult)
                    i.then_inc(ready, 1) if n == len(chunks) - 1 else st.go(i)

            v.wait_ge(pj_used, DEPTH * PJ_L + 14)
            for c in range(TC):
                f = qk[:, c, :, :]
                st.do(tt(rot1, f, f, ALU.mult))
                st.do(v.tensor_reduce(small[:, 10 * c:10 * c + 10], rot1, AX, ALU.add))
            powered(ts(small[:, 0:20], small[:, 0:20], 1.0 / HD, 1e-6, ALU.mult, ALU.add))
            for c in range(TC):
                f = qk[:, c, :, :]
                st.do(tt(f, f, bc(small[:, 32 + 10 * c:42 + 10 * c], HD), ALU.mult))
                for a, n in ((0, Q_HEADS), (Q_HEADS, KV_HEADS)):
                    g = qk[:, c, a:a + n, :]
                    w = qkw[:, 1 if a else 0, :].unsqueeze(1).to_broadcast([P, n, HD])
                    st.go(tt(g, g, w, ALU.mult))
                st.wait()
                table = lambda name: K(name)[:, HD * c:HD * (c + 1)]
                st.go(tt(rot1, f, table("rope_cos").unsqueeze(1).to_broadcast([P, 10, HD]), ALU.mult))
                pairs = lambda a: a.rearrange("p h (a t i) -> p h a t i", a=2, t=2)
                sin = table("rope_sin").rearrange("p (a t i) -> p a t i", a=2, t=2)
                for t in range(2):
                    for a in range(2):
                        st.go(tt(pairs(rot2)[:, :, a, t, :], pairs(f)[:, :, a, 1 - t, :],
                                 sin[:, a, t, :].unsqueeze(1).to_broadcast([P, 10, 16]), ALU.mult))
                st.wait()
                i = tt(f, rot1, rot2, ALU.add)
                i.then_inc(qk_ready, 1) if c else st.do(i)
            b = tr2()
            tr2_done(v.tensor_copy(qkT[:, 4, :], b[:, 0:S]))
            for n in range(2):
                b = tr2()
                tr2_done(v.tensor_copy(qkT[:, 2 * n:2 * n + 2, :], b[:, :].rearrange("p (c s) -> p c s", c=2)))

            def maxima2(pair):
                neg = neg2[:, 4 * (pair % 2):4 * (pair % 2) + 4]
                v.wait_ge(sc_ready, DEPTH * SC_L + 2 * pair + 2)
                for j in range(2):
                    st.go(v.tensor_reduce(neg[:, 2 * j:2 * j + 2], SC[j][:, :].rearrange("p (c k) -> p c k", c=2), AX, ALU.max))
                st.wait()
                arg2(ts(neg, neg, -SCALE, None, ALU.mult))

            def normalise2(pair):
                result2()
                s = sum2[:, 4 * (pair % 2):4 * (pair % 2) + 4]
                st.do(v.reciprocal(s, s))
                for j in range(2):
                    a = p2[:, 2 * (pair % 2) + j, :].rearrange("p (c k) -> p c k", c=2)
                    i = tt(a, a, bc(s[:, 2 * j:2 * j + 2], S), ALU.mult)
                    i.then_inc(probs_ready, 1) if j else st.go(i)

            def turned2(pair):
                for j in range(2):
                    b = tr2()
                    tr2_done(v.tensor_copy(pT2[:, j, :], b[:, :]))

            def out2(pair):
                b = tr2()
                r, c = HD * (pair % 2), pair // 2
                tr2_done(v.tensor_copy(ao[r:r + HD, c:c + 3:2, :], b[r:r + HD, :].rearrange("p (j s) -> p j s", j=2)))

            maxima2(0)
            result2()
            result2()
            recurrence(0)
            normalise2(0)
            maxima2(1)
            turned2(0)
            normalise2(1)
            maxima2(2)
            out2(0)
            turned2(1)
            recurrence(1)
            normalise2(2)
            maxima2(3)
            out2(1)
            v.wait_ge(pj_used, DEPTH * PJ_L + 16)
            v.wait_ge(tr_used, n_tr[0])
            weighted(ao, "attn_g", (0, 2), 0, y2_ready)
            turned2(2)
            normalise2(3)
            lru = gate[0][0]
            st.wait()
            st.do(tt(lru[:, :, :], lru[:, :, :], gate[1][0][:, :, :], ALU.add))
            arg2(tt(lru[:, :, :], lru[:, :, :], gel[:, :, :], ALU.mult))
            out2(2)
            turned2(3)
            v.wait_ge(act_arg, DEPTH * ARG_L + 11)
            weighted(lru, "lru_g", range(LC), 4, lru_ready)
            b = tr2()
            r, c = HD * (3 % 2), 3 // 2
            arg2(v.tensor_copy(ao[r:r + HD, c:c + 3:2, :], b[r:r + HD, :].rearrange("p (j s) -> p j s", j=2)))
            v.wait_ge(act_arg, DEPTH * ARG_L + 12)
            v.sem_inc(tr_used, 1)
            weighted(ao, "attn_g", (1, 3), 0, y2_ready)
            b = tr2()
            i = ts(small[:, 0:4], b[:, 0:4], 1.0 / LRU, NORM_EPS, ALU.mult, ALU.add)
            powered(i)
            v.sem_inc(tr_used, 1)
            v.wait_ge(out_ready, OUT_0 + DEPTH + 1)
            for banks, at, last in ((PJ, 32, False), (LB, 34, True)):
                for n in range(4):
                    c, h = n // 2, n % 2
                    if last:
                        v.wait_ge(out_ready, OUT_0 + DEPTH + 2 + n)
                    part = x[:, c, 512 * h:512 * (h + 1)]
                    i = stt(out=part, in0=banks[n][:, :], scalar=small[:, at + c:at + c + 1], in1=part, op0=ALU.mult,
                            op1=ALU.add)
                    i.then_inc(x_ready, 1) if last and n == 3 else st.go(i)
                st.wait()
            v.wait_ge(x_ready, DEPTH + 3)

            turned_tokens(None)
            res.n += 2
            result2()
            rstd(NORM_EPS)
            v.wait_ge(out_ready, OUT_0 + DEPTH + 6)
            for c in range(TC):
                st.go(stt(out=logits[:, c, :], in0=PJ[0][:, E * c:E * (c + 1)], scalar=small[:, 32 + c:33 + c],
                          in1=brout[:, :], op0=ALU.mult, op1=ALU.add))
            st.wait()
            for c in range(TC):
                st.go(v.max(out=top[:, c, :], in_=logits[:, c, :]))
            st.wait()
            arg2(ts(negL.unsqueeze(2), top[:, :, 0:1], -1.0, None, ALU.mult))
            for c in range(TC):
                st.go(v.max_index(top_at[:, c, :], top[:, c, :], logits[:, c, :]))
            st.wait()
            st.do(v.tensor_copy(top_atf, top_at[:, :, :]))
            for k in range(TOPK):
                for c in range(TC):
                    at = top_atf[:, c, k:k + 1]
                    if k == 0:
                        i = ts(mask[:, c, :], K("iota32"), at, None, ALU.is_equal)
                    else:
                        i = stt(out=mask[:, c, :], in0=K("iota32"), scalar=at, in1=mask[:, c, :], op0=ALU.is_equal, op1=ALU.add)
                    i.then_inc(mask_ready, 1) if (k, c) == (TOPK - 1, TC - 1) else st.go(i)
                if k < TOPK - 1:
                    st.wait()
            v.wait_ge(roww_in, 32)
            for c in range(TC):
                i = stt(out=xn[:, c, :], in0=x[:, c, :], scalar=small[:, 32 + c:33 + c], in1=roww[:, :], op0=ALU.mult,
                        op1=ALU.mult)
                i.then_inc(xn_ready, 1) if c else st.go(i)
            result2()
            v.wait_ge(mask_ready, 1)
            st.do(tt(gates, expL, mask, ALU.mult))
            st.do(v.tensor_reduce(rsum, gates, AX, ALU.add))
            st.do(v.reciprocal(rsum, rsum))
            tt(gates, gates, bc(rsum, E), ALU.mult).then_inc(gates_ready, 1)
            v.wait_ge(gates_ready, 1)
            st.go(ts(half_gates, gates, 0.5, None, ALU.mult))
            v.wait_ge(out_ready, OUT_0 + DEPTH + 7)
            st.go(v.memset(place[:, :, E:E + 1], -1.0))
            st.do(stt(out=place[:, :, 0:E], in0=PJ[1][:, 0:2 * E].rearrange("p (c e) -> p c e", c=2), scalar=1.0, in1=mask,
                      op0=ALU.add, op1=ALU.mult))
            st.do(ts(place[:, :, 0:E], place[:, :, 0:E], -1.0, None, ALU.add))
            st.do(ts(nblk, PJ[1][:, 2 * E:3 * E], float(T), None, ALU.is_gt))
            for b in range(2, S // T):
                st.do(stt(out=nblk, in0=PJ[1][:, 2 * E:3 * E], scalar=float(T * b), in1=nblk, op0=ALU.is_gt, op1=ALU.add))
            st.do(v.tensor_tensor_scan(ncum, ones[:, 0:E], nblk, 0.0, ALU.mult, ALU.add))
            v.tensor_copy(n_more[:, :], nblk).then_inc(count_ready, 1)
            tt(n_before[:, :], ncum, nblk, ALU.subtract).then_inc(count_ready, 1)
            v.sem_inc(gates_ready, 1)
            b = tr2()
            tr2_done(v.tensor_copy(gatesT, b[0:E, 0:S]))
            v.wait_ge(out_ready, OUT_0 + DEPTH + 8)
            for c in range(TC):
                for h in range(2):
                    st.go(tt(x[:, c, 512 * h:512 * (h + 1)], x[:, c, 512 * h:512 * (h + 1)], PJ[2 * c + h][:, :], ALU.add))

            iota = K("iota64")

            def select(at0, at1, ready):
                st2.go(ts(sel[:, 0, :], iota[:, 0:T], at0, None, ALU.is_equal))
                ts(sel[:, 1, :], iota[:, 0:T], at1, None, ALU.is_equal).then_inc(ready, 1)

            def select_gates(at, e):
                for c in range(TC):
                    i = ts(selg[:, c, :], iota, at[c], half_gates[:, c, bass.ds(e, 1)], ALU.is_equal, ALU.mult)
                    yield i

            def hidden(ready, gc_ready, tanh_ready):
                i = ts(g_sb, GB[:, :], SWIGLU_LIMIT, None, ALU.min)
                gc_ready(i)
                st2.go(ts(u_sb, UB[:, :], SWIGLU_LIMIT, -SWIGLU_LIMIT, ALU.min, ALU.max))
                tanh_ready()
                st2.do(gated(g_sb, tanh_g, g_sb))
                stt(out=h_sb.rearrange("q (c p) -> q p c", c=4), in0=u_sb.rearrange("q (p c) -> q p c", c=4), scalar=1.0,
                    in1=g_sb.rearrange("q (p c) -> q p c", c=4), op0=ALU.add, op1=ALU.mult).then_inc(ready, 1)

            def add_sums(c, ready):
                for n in range(2):
                    i = tt(x[:, c, 512 * n:512 * (n + 1)], x[:, c, 512 * n:512 * (n + 1)], OB[n][:, :], ALU.add)
                    i.then_inc(ready, 1) if n else st2.go(i)

            st2 = st
            st.go(v.memset(y_sb, 0.0))
            st.go(v.memset(gT, 0.0))
            st.wait()
            v.sem_inc(ex["gt_out"], 1)
            v.tensor_copy(bsel[:, :], ident[:, 0:1].to_broadcast([P, T])).then_inc(ex["bsel"], 1)
            select(place[:, 0, 0:1], place[:, 1, 0:1], ex["sel"])
            v.wait_ge(ex["xt"], 1)
            v.tensor_copy(xT, XTB[:, :]).then_inc(ex["xt_out"], 1)
            st_main = st.base + st.n
            with v.Fori(0, E) as e:
                first = v.value_load(n_before[0:1, bass.ds(e, 1)], min_val=0, max_val=16)
                more = v.value_load(n_more[0:1, bass.ds(e, 1)], min_val=0, max_val=3)
                st2 = Steps(v, ex_step, first * EX_STEPS + e * PRE_STEPS)
                st2.go(v.tensor_copy(rest, place[:, :, bass.ds(e, 1)].rearrange("p c a -> p (c a)")))
                assert st2.n == PRE_STEPS
                with v.If(more > 0):
                    with v.Fori(0, more) as b:
                        j = first + b
                        st2 = Steps(v, ex_step, j * EX_STEPS + (e * PRE_STEPS + PRE_STEPS))
                        done = ex["dve"]
                        pe_at = lambda n: v.wait_ge(ex["pe"], j * 7 + n)
                        act_at = lambda n: v.wait_ge(ex["act"], j * 4 + n)
                        st2.wait()
                        st2.do(ts(rest, rest, -float(T), None, ALU.add))
                        for i in select_gates([rest[:, 0:1], rest[:, 1:2]], e):
                            st2.go(i)
                        select(rest[:, 0:1], rest[:, 1:2], done)
                        pe_at(2)
                        v.tensor_copy(xTx, XTB[:, :]).then_inc(done, 1)
                        pe_at(3)
                        hidden(done, lambda i: i.then_inc(done, 1), lambda: (act_at(2), st2.wait()))
                        pe_at(4)
                        v.tensor_copy(gTx, XS[:, 0:S]).then_inc(done, 1)
                        pe_at(6)
                        add_sums(0, done)
                        pe_at(7)
                        add_sums(1, done)
                        assert st2.n == EX_STEPS, f"EX_STEPS = {st2.n}"

                v.wait_ge(ex_step, (first + more) * EX_STEPS + (e * PRE_STEPS + PRE_STEPS))
                st2 = Steps(v, dve_step, e * MAIN_STEPS + st_main)
                v.wait_ge(ex["xs"], e + 1)
                select(place[:, 0, bass.ds(e + 1, 1)], place[:, 1, bass.ds(e + 1, 1)], ex["sel"])
                for c, i in enumerate(select_gates([place[:, 0, bass.ds(e, 1)], place[:, 1, bass.ds(e, 1)]], e)):
                    i.then_inc(ex["selg"], 1) if c else st2.go(i)
                v.wait_ge(ex["gu"], e + 1)
                hidden(ex["h"], lambda i: i.then_inc(ex["gc"], 1), lambda: (v.wait_ge(ex["eg"], e + 1), st2.wait()))
                v.tensor_copy(bsel[:, :], ident[:, bass.ds(e + 1, 1)].to_broadcast([P, T])).then_inc(ex["bsel"], 1)
                v.wait_ge(ex["xt"], e + 2)
                v.tensor_copy(xT, XTB[:, :]).then_inc(ex["xt_out"], 1)
                v.wait_ge(ex["o"], e * 2 + 1)
                add_sums(0, ex["acc"])
                v.wait_ge(ex["o"], e * 2 + 2)
                add_sums(1, ex["acc"])
                v.wait_ge(ex["gt"], e + 1)
                v.tensor_copy(gT, XS[:, 0:S]).then_inc(ex["gt_out"], 1)
                assert st2.n == MAIN_STEPS, f"MAIN_STEPS = {st2.n}"
            st = Steps(v, dve_step, st_main + E * MAIN_STEPS)
            st2 = st
            v.wait_ge(ex["o"], 2 * E + 1)
            add_sums(0, ex["acc"])
            v.wait_ge(ex["o"], 2 * E + 2)
            add_sums(1, ex["acc"])
            v.wait_ge(ex["acc"], 2 * E + 2)
            v.sem_inc(x_ready, 1)
            result2()
            rstd(NORM_EPS)
            v.wait_ge(roww_in, 48)
            for c in range(TC):
                i = stt(out=xn[:, c, :], in0=x[:, c, :], scalar=small[:, 32 + c:33 + c], in1=roww[:, :], op0=ALU.mult,
                        op1=ALU.mult)
                i.then_inc(x_ready, 1) if c else st.go(i)


_INS = ['x', 'norm_w', 'w_in', 'conv_w', 'conv_b', 'gate_bias', 'ret_norm_w', 'mlstm_norm_w', 'w_out', 'final_norm_w',
        'norm1_g_2', 'w_in_2', 'q_norm_g_2', 'k_norm_g_2', 'conv_w_2', 'conv_b_2', 'lru_wa_2', 'lru_ba_2', 'lru_wi_2',
        'lru_bi_2', 'lru_lam_2', 'attn_out_g_2', 'lru_out_g_2', 'w_out_2', 'norm2_g_2', 'w_router_2', 'b_router_2',
        'w_gate_2', 'b_gate_2', 'w_up_2', 'b_up_2', 'w_down_2', 'b_down_2', 'final_g_2']


def kernel(**inputs):
    import concourse.bacc as _bacc
    from concourse.bass_utils import run_bass_kernel_spmd as _run

    nc = _bacc.Bacc("TRN2", target_bir_lowering=False, num_devices=1)
    arrays, args = {}, {}
    tables, where = shape_constants()
    for name in _INS + ["consts"]:
        a = np.ascontiguousarray(tables if name == "consts" else inputs[name])
        arrays[f"in_{name}_dram"] = a
        args[name] = nc.dram_tensor(f"in_{name}_dram", a.shape, mybir.dt.from_np(a.dtype), kind="ExternalInput").ap()
    args["consts_at"] = where
    out = nc.dram_tensor("out_0_dram", (1, S, D), F32, kind="ExternalOutput").ap()
    build(nc, args, out)
    r = _run(nc, [arrays], core_ids=[0])
    return r.results[0]["out_0_dram"]
```

```python
from contextlib import ExitStack

import numpy as np

import concourse.bass as bass
from concourse import mybir

F32 = mybir.dt.float32
I32 = mybir.dt.int32
U32 = mybir.dt.uint32
ALU = mybir.AluOpType
ACT = mybir.ActivationFunctionType
AX = mybir.AxisListType.X

P = 128
D = 1024
S = 256
TC = S // P
KC = D // P
HD = 64
DEPTH = 2
A_HEADS, B_HEADS, C_HEADS = 8, 4, 4
LRU = 512
LC = LRU // P
Q_HEADS, KV_HEADS = 8, 2
E = 32
TOPK = 4
T = 64
SLOTS = 6
SLOT = 4096
CAUSAL = 3 * P
LRU_C, SWIGLU_ALPHA, SWIGLU_LIMIT = 8.0, 1.702, 7.0
RMS_EPS, HEAD_EPS, NORM_EPS = 1e-6, 1e-5, 1e-5
SCALE = HD ** -0.5

IN_GROUPS = [(4096, 264), (3072, 512), (0, 512), (512, 512), (3584, 512),
             (1024, 512), (1536, 512), (2048, 512), (2560, 512)]
LAYER_TURNS = 12
IN2_GROUPS = [(768, 512), (512, 256), (0, 512), (1280, 512)]
BLOCK2_TURNS = 6
EXPERT_LOADS = [("w_gate_2", 0), ("w_gate_2", 1), ("w_up_2", 0), ("w_up_2", 1), ("w_down_2", 0), ("w_down_2", 1)]
EXPERT_TURNS = len(EXPERT_LOADS)

TR_L, PJ_L, SC_L = 16, 18, 27
ARG_L, RES_L, POW_L = 8, 11, 3
OUT_L = 4
PJ_0, OUT_0 = 5, 2
STEPS_L = 105
MAIN_STEPS, PRE_STEPS, EX_STEPS = 6, 1, 8

N_ROWS1 = 28
COL1 = {"norm": 0, "conv_w": 8, "conv_b": 24}
COL2 = {k: DEPTH * N_ROWS1 + v for k, v in
        {"norm1": 0, "conv_w": 8, "conv_b": 24, "ba": 28, "bi": 36, "lam": 44, "attn_g": 52, "lru_g": 56, "norm2": 60}.items()}
N_ROWS = DEPTH * N_ROWS1 + 68
N_PARAM_LOADS = 3 * DEPTH + 9 + 6


def shape_constants():
    f = np.float32
    p = np.arange(P)
    t = {}
    t["ident"] = np.eye(P, dtype=f)
    t["ones"] = np.ones((P, P), f)
    swap = (p // HD) * HD + (p % HD + HD // 2) % HD
    t["swap"] = np.eye(P, dtype=f)[:, swap]
    half = HD // 2
    theta = (1.0 / (f(10000.0) ** np.linspace(0.0, 1.0, half, dtype=f))).astype(f)
    ang = (np.arange(S, dtype=f)[None, :] * theta[p % half][:, None]).astype(f)
    sign = np.where(p % HD < half, -1.0, 1.0).astype(f)
    t["ret_cos"] = np.cos(ang).astype(f)
    t["ret_sin"] = (np.sin(ang) * sign[:, None]).astype(f)
    lg = np.log(1.0 - 2.0 ** (-5.0 - np.arange(B_HEADS, dtype=f))).astype(f)
    dec = []
    for h in range(B_HEADS):
        for m0, n0, n1 in ((0, 0, 256), (128, 128, 256)):
            diff = (np.arange(n0, n1)[None, :] - (m0 + p)[:, None]).astype(f)
            dec.append(np.where(diff >= 0, np.exp(lg[h] * np.maximum(diff, 0)), 0.0) * SCALE)
    t["decay"] = np.concatenate(dec, 1).astype(f)
    dist = [(q0 + p)[:, None] - np.arange(n)[None, :] for q0, n in ((0, 128), (128, 256))]
    dist = np.concatenate(dist, 1).astype(f)
    t["dist"] = np.where(dist >= 0, dist, 1e30).astype(f)
    t["tri"] = (p[:, None] <= p[None, :]).astype(f)
    t["before"] = (p[:, None] < p[None, :]).astype(f)
    inv = (f(10000.0) ** (-np.arange(16, dtype=f) / 16)).astype(f)
    for name, fn in (("rope_cos", np.cos), ("rope_sin", np.sin)):
        cols = []
        for c in range(TC):
            tok = 128 * c + p
            for pos in (tok // 64, tok % 64):
                a = (pos.astype(f)[:, None] * inv[None, :]).astype(f)
                v = fn(a).astype(f)
                cols += [-v, v] if name == "rope_sin" else [v, v]
        t[name] = np.concatenate(cols, 1)
    t["iota64"] = np.tile(np.arange(T, dtype=f), (P, 2))
    t["iota32"] = np.tile(np.arange(E, dtype=f), (P, 1))
    t["row_head"] = np.concatenate([np.repeat((p == h).astype(f)[:, None], P, 1) for h in range(C_HEADS)], 1)
    at, pos = {}, 0
    for k, v in t.items():
        at[k] = (pos, v.shape[1])
        pos += v.shape[1]
    return np.concatenate([v.astype(f) for v in t.values()], 1), at


def build(nc, ins, out):
    consts_at = ins["consts_at"]
    ctx = ExitStack()
    with ctx:
        def sb(name, shape, dt=F32):
            return ctx.enter_context(nc.sbuf_tensor(name, shape, dt))

        def sem(name):
            return ctx.enter_context(nc.semaphore(name))

        ring = sb("ring", [P, SLOTS + 2, SLOT])

        def before(slot, at, shape):
            n = int(np.prod(shape))
            a = ring[:, SLOTS + slot, at:at + n]
            dims = "abc"[:len(shape)]
            return a.rearrange(f"p ({' '.join(dims)}) -> p {' '.join(dims)}", **dict(zip(dims, shape)))

        const = sb("const", [P, ins["consts"].shape[1]])

        def K(name):
            a, n = consts_at[name]
            return const[:, a:a + n]

        ident, ones = K("ident"), K("ones")
        x = sb("x", [P, TC, D])
        xn = sb("xn", [P, TC, D])
        hT = before(1, 0, (KC, S))
        yT = hT
        rows = sb("rows", [P, P])
        cols_all = sb("cols_all", [P, P])
        cols = sb("cols", [P, 32])
        gb_all = sb("gb_all", [C_HEADS, DEPTH, 2])
        gb = sb("gb", [C_HEADS, 2])
        hw_all = before(1, 3072, (DEPTH, 2, 256))
        hw = before(0, 3584, (2, 256))
        roww = sb("roww", [P, D])
        qkw = sb("qkw", [P, 2, HD])
        brout = sb("brout", [P, E])
        small = sb("small", [P, 256])
        wr = sb("wr", [P, KC, E])

        mem1 = sb("mem1", [P, 8 * S])
        mem2 = sb("mem2", [P, 4 * 260])
        mem3 = sb("mem3", [P, 8 * S])
        mem4 = sb("mem4", [P, C_HEADS * CAUSAL])
        mem5 = sb("mem5", [P, 6 * CAUSAL])
        vA = before(1, 2048, (TC, 512))
        vC = sb("vC", [P, TC, C_HEADS, HD + 1])
        cg = sb("cg", [P, TC, 264])
        vgB = before(0, 2048, (TC, 512))
        agT = before(0, 0, (4, S))
        eg = before(0, 1024, (4, S))
        eB = before(0, 3072, (TC, 256))
        qkA = mem1[:, :].rearrange("p (c s) -> p c s", c=8)
        rawC = mem2[:, :].rearrange("p (c s) -> p c s", c=4)
        rawB = mem2[:, 0:4 * S].rearrange("p (c s) -> p c s", c=4)
        rotB = mem3[:, 0:4 * S].rearrange("p (c s) -> p c s", c=4)
        qkC = mem3[:, 4 * S:].rearrange("p (c s) -> p c s", c=4)
        wC = mem4[:, :].rearrange("p (h n) -> p h n", h=C_HEADS)
        sB = wC
        prob = mem5[:, 0:4 * CAUSAL].rearrange("p (h n) -> p h n", h=4)
        probT = mem5[:, 4 * CAUSAL:].rearrange("p (h n) -> p h n", h=2)
        rw = mem5[0:C_HEADS, :].rearrange("p (r n) -> p r n", r=9)
        xn_flat = xn[:, :, :].rearrange("p c d -> p (c d)")
        yBC = xn_flat[:, 0:512].rearrange("p (g d) -> p g d", d=HD)
        tmp = xn_flat[:, 512:1024].rearrange("p (g d) -> p g d", d=HD)
        eC = xn_flat[:, 1024:2048].rearrange("p (c n) -> p c n", c=TC)


        def four(a):
            return a.rearrange("p (c s) -> p c s", c=4)

        free_at = consts_at["swap"][0]
        lraw = mem2[:, :].rearrange("p (c s) -> p c s", c=4)
        xc, sq2 = four(mem3[:, 0:4 * S]), four(mem3[:, 4 * S:8 * S])
        flat2 = lambda a: a[:, :, :].rearrange("p c n -> p (c n)")
        gate = [[four(mem1[:, 0:4 * S]), four(mem1[:, 4 * S:8 * S])], [four(flat2(vA)), four(flat2(vgB))]]
        decay2 = [agT, eg]
        gel = four(xn_flat[:, 0:4 * S])
        lru_w = mem5[:, 0:2048].rearrange("p (u n) -> p u n", u=16)
        p2 = mem5[:, 0:2048].rearrange("p (h n) -> p h n", h=4)
        qk = mem4[:, 0:1280].rearrange("p (c h d) -> p c h d", c=TC, h=Q_HEADS + KV_HEADS)
        v2 = vC[:, :, :, :].rearrange("p c h d -> p (c h d)")[:, 0:2 * P].rearrange("p (c n) -> p c n", c=TC)
        rot1 = xn_flat[:, 1024:1664].rearrange("p (h d) -> p h d", d=HD)
        rot2 = mem2[:, 0:640].rearrange("p (h d) -> p h d", d=HD)
        qkT = const[:, free_at:free_at + 5 * S].rearrange("p (c s) -> p c s", c=5)
        pT2 = const[:, free_at + 5 * S:free_at + 9 * S].rearrange("p (j n) -> p j n", j=2)
        ao = four(xn_flat[:, 4 * S:8 * S])
        sqL, sqA = gate[1][1], sq2
        neg2, sum2, half_b = small[:, 80:88], small[:, 88:96], small[:, 192:208]

        def score_banks(pair):
            return PJ[0:2] if pair == 1 else SC

        def lam(i):
            return small[:, 136 + 8 * i:144 + 8 * i]

        top_at = sb("top_at", [P, TC, 8], U32)
        n_more, n_before = sb("n_more", [P, E], I32), sb("n_before", [P, E], I32)
        at = [0]

        def piece(*shape):
            n = int(np.prod(shape))
            a = mem2[:, at[0]:at[0] + n]
            at[0] += n
            return a if len(shape) == 1 else a.rearrange("p (c n) -> p c n", c=shape[0])

        logits, mask, expL, gates, half_gates = (piece(TC, E) for _ in range(5))
        top, top_atf, place = piece(TC, 8), piece(TC, 8), piece(TC, E + 1)
        negL, rsum, rest = piece(TC), piece(TC), piece(TC)
        nblk, ncum = piece(E), piece(E)
        gatesT = mem4[0:E, D:D + S]
        bdown = mem4[0:E, 0:D]
        bias = const[:, free_at:free_at + 2 * D].rearrange("p (m n) -> p m n", m=2)
        xs_sb, xT, g_sb, tanh_g = (mem1[:, 512 * i:512 * (i + 1)] for i in range(4))
        u_sb, h_sb, hT_sb, y_sb = (mem3[:, 512 * i:512 * (i + 1)] for i in range(4))
        xTx, yx_sb = mem5[:, 0:512], mem5[:, 512:1024]
        gT, gTx = mem5[:, 1024:1280], mem5[:, 1280:1536]
        sel = mem5[:, 1536:1664].rearrange("p (c n) -> p c n", c=TC)
        selg = mem5[:, 1664:1920].rearrange("p (c n) -> p c n", c=TC)
        bsel = mem5[:, 1920:1984]

        bank = [ctx.enter_context(nc.psum_tensor(f"bank{i}", [P, 512], F32)) for i in range(8)]
        PJ, TR, SC = bank[0:4], bank[4:6], bank[6:8]
        LB = [bank[6], bank[7], bank[4], bank[5]]
        DB = [bank[0], bank[2], bank[6], bank[7]]
        GB, UB, YB, XS, XTB, HTB, OB = bank[0], bank[1], bank[2], bank[3], bank[4], bank[5], bank[6:8]

        x_in, consts_in = sem("x_in"), sem("consts_in")
        ident_in = sem("ident_in")
        params_in, roww_in = sem("params_in"), sem("roww_in")
        w_in_slot = [sem(f"w_in_slot{i}") for i in range(SLOTS + 2)]
        w_used = sem("w_used")
        load_begun = sem("load_begun")
        x_ready = sem("x_ready")
        xn_ready = sem("xn_ready")
        xw_ready = sem("xw_ready")
        tr_ready, tr_used = sem("tr_ready"), sem("tr_used")
        pj_ready, pj_used = sem("pj_ready"), sem("pj_used")
        sc_ready, sc_used = sem("sc_ready"), sem("sc_used")
        out_ready = sem("out_ready")
        act_arg, act_res = sem("act_arg"), sem("act_res")
        pow_arg, pow_res = sem("pow_arg"), sem("pow_res")
        probs_ready = sem("probs_ready")
        qkC_ready, rotB_ready = sem("qkC_ready"), sem("rotB_ready")
        yC_ready, yB_ready = sem("yC_ready"), sem("yB_ready")
        fills = sem("fills")
        dve_step = sem("dve_step")
        ex_step = sem("ex_step")
        xc_ready, lru_w_in, lru_w_zero = sem("xc_ready"), sem("lru_w_in"), sem("lru_w_zero")
        qk_ready, lru_ready, y2_ready = sem("qk_ready"), sem("lru_ready"), sem("y2_ready")
        bias_zero, bias_in, bdown_in, wr_in = sem("bias_zero"), sem("bias_in"), sem("bdown_in"), sem("wr_in")
        mask_ready, gates_ready, count_ready = sem("mask_ready"), sem("gates_ready"), sem("count_ready")
        out_done = sem("out_done")
        ex = {n: sem("ex_" + n) for n in
              ("sel", "xs", "xs_out", "xt", "xt_out", "gu", "gc", "eg", "h", "ht", "ht_out", "y", "y_out",
               "selg", "gt", "gt_out", "o", "acc", "pe", "dve", "act", "bsel")}

        class Steps:

            def __init__(self, eng, s, base=0):
                self.eng, self.s, self.base, self.n = eng, s, base, 0

            def go(self, i):
                i.then_inc(self.s, 1)
                self.n += 1

            def wait(self):
                self.eng.wait_ge(self.s, self.base + self.n)

            def do(self, i):
                self.go(i)
                self.wait()

        param_loads = []

        def param(dst, src):
            param_loads.append((dst, src))


        for l in range(DEPTH):
            r = N_ROWS1 * l
            param(rows[r:r + 8, :], ins["norm_w"][l].rearrange("(c p) -> c p", p=P))
            param(rows[r + 8:r + 24, :], ins["conv_w"][l].rearrange("t (c p) -> (t c) p", p=P))
            param(rows[r + 24:r + 28, :], ins["conv_b"][l].rearrange("(c p) -> c p", p=P))
        for name, key, pat in (("norm1_g_2", "norm1", "(c p) -> c p"), ("conv_w_2", "conv_w", "t (c p) -> (t c) p"),
                               ("conv_b_2", "conv_b", "(c p) -> c p"), ("lru_ba_2", "ba", "d (c p) -> (d c) p"),
                               ("lru_bi_2", "bi", "d (c p) -> (d c) p"), ("lru_lam_2", "lam", "d (c p) -> (d c) p"),
                               ("attn_out_g_2", "attn_g", "(c p) -> c p"), ("lru_out_g_2", "lru_g", "(c p) -> c p"),
                               ("norm2_g_2", "norm2", "(c p) -> c p")):
            src = ins[name][0].rearrange(pat, p=P)
            param(rows[COL2[key]:COL2[key] + src.shape[0], :], src)
        param(hw_all[:, :, 0, :], ins["ret_norm_w"].partition_broadcast(P))
        param(hw_all[:, :, 1, :], ins["mlstm_norm_w"].partition_broadcast(P))
        param(qkw[:, 0, :], ins["q_norm_g_2"][0].partition_broadcast(P))
        param(qkw[:, 1, :], ins["k_norm_g_2"][0].partition_broadcast(P))
        param(brout[:, :], ins["b_router_2"][0].partition_broadcast(P))

        block = ctx.enter_context(nc.Block())
        in_loads = [len([t for t in range(LAYER_TURNS - 1) if t % SLOTS == s]) for s in range(SLOTS)]

        slot_base = [DEPTH * n + 1 for n in in_loads]

        @block.sync
        def _(sp):
            sp.dma_start(const[:, 0:2 * P], ins["consts"][:, 0:2 * P]).then_inc(ident_in, 16)
            sp.dma_start(x[:, :, :], ins["x"][0].rearrange("(c p) d -> p c d", p=P)).then_inc(x_in, 16)

            for dst, src in param_loads[0::2]:
                sp.dma_start(dst, src).then_inc(params_in, 16)
            sp.wait_ge(params_in, 16 * N_PARAM_LOADS)
            sp.dma_start(const[:, 2 * P:], ins["consts"][:, 2 * P:]).then_inc(consts_in, 16)

            def load(slot, dst, src):
                sp.dma_start(dst, src).then_inc(w_in_slot[slot], 16)

            def load_cols(slot, w, c0, n):
                load(slot, ring[:, slot, 0:KC * n].rearrange("p (k n) -> p k n", n=n),
                     w[:, c0:c0 + n].rearrange("(k p) n -> p k n", p=P))

            def slot_free(turn, l):
                if turn >= SLOTS:
                    sp.wait_ge(pj_ready, l * PJ_L + (PJ_0 + 2 * (turn - SLOTS + 1)))
                elif turn in (3, 4):
                    sp.wait_ge(out_ready, l * OUT_L + (OUT_0 - 4 + turn))
                else:
                    sp.wait_ge(pj_ready, l * PJ_L + [1, 3, 5, 0, 0, 1][turn])
                sp.sem_inc(load_begun, 1)

            with sp.Fori(0, DEPTH) as l:
                w_in = ins["w_in"][bass.ds(l, 1)].rearrange("a k n -> (a k) n")
                w_out = ins["w_out"][bass.ds(l, 1)].rearrange("a k n -> (a k) n")
                for turn in range(LAYER_TURNS - 1):
                    slot_free(turn, l)
                    if turn < len(IN_GROUPS):
                        load_cols(turn % SLOTS, w_in, *IN_GROUPS[turn])
                    else:
                        load_cols(turn % SLOTS, w_out, 512 * (turn - len(IN_GROUPS)), 512)

            for turn in range(BLOCK2_TURNS):
                slot_free(turn, DEPTH)
                if turn < len(IN2_GROUPS):
                    load_cols(turn, ins["w_in_2"][0], *IN2_GROUPS[turn])
                else:
                    load_cols(turn, ins["w_out_2"][0], 512 * (turn - len(IN2_GROUPS)), 512)

            def load_expert(e, free, odd):
                for turn, (name, h) in enumerate(EXPERT_LOADS):
                    free(turn)
                    src = ins[name][0, e, 512 * h:512 * h + 512, :]
                    slot = turn + (SLOTS if odd and turn < 2 else 0)
                    load(slot, ring[:, slot, :], src.rearrange("a (p c) n -> p (a c n)", p=P))

            def free_of_block2(turn):
                if turn < 4:
                    sp.wait_ge(pj_ready, PJ_0 + DEPTH * PJ_L + [2, 4, 6, 16][turn])
                else:
                    sp.wait_ge(out_ready, OUT_0 + OUT_L * DEPTH + turn)

            def free_of_layers(turn):
                if turn == 0:
                    sp.wait_ge(x_ready, 2 * DEPTH + 6)
                elif turn == 1:
                    sp.wait_ge(out_ready, OUT_0 + OUT_L * DEPTH + 6)
                else:
                    sp.wait_ge(w_used, turn + 1)

            def expert_free(e, turn):
                if turn < 2:
                    sp.wait_ge(w_used, (e - 2) * EXPERT_TURNS + (turn + 1))
                else:
                    sp.wait_ge(w_used, (e - 1) * EXPERT_TURNS + (turn + 1))
                sp.sem_inc(load_begun, 1)

            load_expert(slice(0, 1), free_of_block2, 0)
            load_expert(slice(1, 2), free_of_layers, 1)
            with sp.Fori(0, E // 2 - 1) as pair:
                for odd in range(2):
                    e = pair * 2 + (2 + odd)
                    load_expert(bass.ds(e, 1), lambda turn: expert_free(e, turn), odd)

            for c in range(TC):
                sp.wait_ge(x_ready, 2 * DEPTH + 9 + c)
                sp.dma_start(out[0, P * c:P * (c + 1), :], xn[:, c, :]).then_inc(out_done, 16)
            sp.wait_ge(out_done, 16 * TC)

        @block.gpsimd
        def _(pool):
            def load(dst, src, s):
                pool.dma_start(dst, src).then_inc(s, 16)

            load(wr[:, :, :], ins["w_router_2"][0].rearrange("(k p) n -> p k n", p=P), wr_in)
            load(roww[:, :], ins["final_norm_w"].partition_broadcast(P), roww_in)
            pool.memset(vC[:, :, :, HD:HD + 1], 1.0).then_inc(fills, 1)
            minus_half = small[:, 224:256]
            pool.memset(minus_half, -0.5).then_inc(fills, 1)

            def power(n, count):
                pool.wait_ge(pow_arg, count)
                pool.tensor_tensor(small[:, 32:32 + n], small[:, 0:n], minus_half[:, 0:n], ALU.pow).then_inc(pow_res, 1)

            pool.wait_ge(fills, 2)
            with pool.Fori(0, DEPTH) as l:
                for i, n in enumerate((2, 8, 8)):
                    power(n, l * POW_L + (i + 1))
            base_pow = DEPTH * POW_L
            pow_count = [base_pow]

            def power2(n):
                pow_count[0] += 1
                power(n, pow_count[0])

            pool.wait_ge(sc_ready, DEPTH * SC_L)
            pool.memset(lru_w[:, :, :], 0.0).then_inc(lru_w_zero, 1)
            power2(4)
            pool.wait_ge(x_ready, 2 * DEPTH + 4)
            load(roww[:, :], ins["norm2_g_2"][0].partition_broadcast(P), roww_in)
            power2(20)
            power2(4)
            pool.wait_ge(x_ready, 2 * DEPTH + 6)
            pool.memset(bias[:, :, :], 0.0).then_inc(bias_zero, 1)
            pool.wait_ge(bias_zero, 1)
            load(bias[0:E, 0, :], ins["b_gate_2"][0], bias_in)
            load(bias[0:E, 1, :], ins["b_up_2"][0], bias_in)
            load(bdown[:, :], ins["b_down_2"][0], bdown_in)
            power2(2)
            pool.wait_ge(xn_ready, DEPTH + 2)
            load(roww[:, :], ins["final_g_2"].partition_broadcast(P), roww_in)
            power2(2)

        @block.scalar
        def _(act):
            A = nc.scalar.activation
            for dst, src in param_loads[1::2]:
                act.dma_start(dst, src).then_inc(params_in, 16)
            act.dma_start(gb_all[:, :, :], ins["gate_bias"].rearrange("l (g h) -> h l g", g=2),
                          allow_slow_non_contiguous=True).then_inc(params_in, 16)
            act.wait_ge(x_in, 16)
            act.wait_ge(fills, 2)

            def squares(s, ready, src, unread, at=64):
                for c in range(TC):
                    act.wait_ge(s, ready + (c + 1))
                    i = A(unread[:, c, :], src[:, c, :], ACT.Square, accum_out=small[:, at + c:at + 1 + c])
                i.then_inc(act_res, 1)

            with act.Fori(0, DEPTH) as l:
                def unit(u):
                    act.wait_ge(pj_ready, l * PJ_L + (PJ_0 + u + 1))
                    return PJ[u % 4]

                def used(i):
                    i.then_inc(pj_used, 1)

                def arg(n):
                    act.wait_ge(act_arg, l * ARG_L + n)

                def result(i):
                    i.then_inc(act_res, 1)

                def softmax_exp(pair):
                    arg(5 + pair)
                    for h in (2 * pair, 2 * pair + 1):
                        for j, (a, b) in enumerate(((0, P), (P, CAUSAL))):
                            n = 2 * (h % 4) + j
                            i = A(prob[:, h % 4, a:b], prob[:, h % 4, a:b], ACT.Exp, bias=small[:, 96 + n:97 + n],
                                  accum_out=small[:, 104 + n:105 + n])
                    result(i)

                squares(x_ready, 2 * l, x, xn)
                for c in range(TC):
                    b = unit(c)
                    A(cg[:, c, :], b[:, 0:264], ACT.Copy)
                    used(A(eC[:, c, 256:512], b[:, 0:256], ACT.Tanh, scale=0.5))
                for c in range(2):
                    b = unit(2 + c)
                    used(A(rawC[:, 2 * c:2 * c + 2, 3:3 + S], b[:, :].rearrange("p (c s) -> p c s", c=2), ACT.Copy))
                arg(1)
                result(A(rw[:, 3, :], rw[:, 2, :], ACT.Exp))
                arg(2)
                result(A(rw[:, 5, :], rw[:, 4, :], ACT.Ln))
                for c in range(2):
                    b = unit(4 + c)
                    used(A(qkA[:, 2 * c:2 * c + 2, :], b[:, :].rearrange("p (c s) -> p c s", c=2), ACT.Copy, scale=SCALE))
                    if c == 0:
                        arg(3)
                        result(A(eg[:, :, :], qkC[:, :, :], ACT.Tanh, scale=0.5))
                arg(4)
                result(A(rw[:, 1, :], rw[:, 2, :], ACT.Exp, scale=-1.0))
                for c in range(2):
                    b = unit(6 + c)
                    used(A(qkA[:, 4 + 2 * c:6 + 2 * c, :], b[:, :].rearrange("p (c s) -> p c s", c=2), ACT.Copy))
                for pair in range(2):
                    act.wait_ge(sc_used, l * SC_L + (pair + 1))
                    w = wC[:, 2 * pair:2 * pair + 2, :]
                    result(A(w, w, ACT.Exp, scale=-1.0))
                for c in range(TC):
                    b = unit(8 + c)
                    A(vC[:, c, :, 0:HD], b[:, 0:256].rearrange("p (h d) -> p h d", d=HD), ACT.Copy)
                    used(A(eC[:, c, 0:256], b[:, 256:512], ACT.Tanh, scale=0.5))
                softmax_exp(0)
                for c in range(TC):
                    b = unit(10 + c)
                    used(A(vA[:, c, :], b[:, :], ACT.Copy))
                softmax_exp(1)
                act.wait_ge(qkC_ready, l + 1)
                for c in range(2):
                    b = unit(12 + c)[:, :].rearrange("p (c s) -> p c s", c=2)
                    A(agT[:, 2 * c:2 * c + 2, :], b, ACT.Copy)
                    used(A(eg[:, 2 * c:2 * c + 2, :], b, ACT.Tanh, scale=0.5))
                softmax_exp(2)
                for c in range(2):
                    b = unit(14 + c)
                    used(A(rawB[:, 2 * c:2 * c + 2, :], b[:, :].rearrange("p (c s) -> p c s", c=2), ACT.Copy))
                softmax_exp(3)
                for c in range(TC):
                    b = unit(16 + c)
                    A(vgB[:, c, :], b[:, :], ACT.Copy)
                    used(A(eB[:, c, :], b[:, 256:512], ACT.Tanh, scale=0.5))
            n_arg = [DEPTH * ARG_L]

            def arg2():
                n_arg[0] += 1
                act.wait_ge(act_arg, n_arg[0])

            def unit2(u):
                act.wait_ge(pj_ready, DEPTH * PJ_L + PJ_0 + u + 1)
                return PJ[u % 4]

            def used2(i):
                i.then_inc(pj_used, 1)

            act.wait_ge(lru_w_zero, 1)
            for g, name in enumerate(("lru_wa_2", "lru_wi_2")):
                for d in range(2):
                    for j in range(2):
                        act.dma_start(lru_w[HD * j:HD * (j + 1), 8 * d + 4 * g:8 * d + 4 * g + 4, HD * j:HD * (j + 1)],
                                      ins[name][0, d].rearrange("(c j) i o -> j i c o", j=2)[j]).then_inc(lru_w_in, 16)
            squares(x_ready, 2 * DEPTH, x, mem3[:, :].rearrange("p (c d) -> p c d", c=TC))
            squares(xw_ready, 0, xn, mem1[:, :].rearrange("p (c d) -> p c d", c=TC), 66)
            arg2()
            A(lam(1), lam(0), ACT.Exp).then_inc(act_res, 1)
            arg2()
            A(lam(3), lam(2), ACT.Ln).then_inc(act_res, 1)
            for c in range(2):
                b = unit2(c)
                used2(A(lraw[:, 2 * c:2 * c + 2, 2:2 + S], b[:, :].rearrange("p (c s) -> p c s", c=2), ACT.Copy))
            for c in range(TC):
                b = unit2(2 + c)
                A(qk[:, c, 8:10, :], b[:, 0:P].rearrange("p (g d) -> p g d", d=HD), ACT.Copy)
                used2(A(v2[:, c, :], b[:, P:2 * P], ACT.Copy))
            for c in range(TC):
                b = unit2(4 + c)
                used2(A(qk[:, c, 0:8, :].rearrange("p (j g) d -> p g j d", g=2),
                        b[:, :].rearrange("p (g j d) -> p g j d", g=2, d=HD), ACT.Copy))
            for d in range(2):
                for g in range(2):
                    for h in range(2):
                        b = unit2(6 + 4 * d + 2 * g + h)
                        for j in range(2):
                            c = 2 * h + j
                            i = A(gate[d][g][:, c, :], b[:, S * j:S * (j + 1)], ACT.Tanh, scale=0.5,
                                  bias=half_b[:, 8 * g + 4 * d + c:8 * g + 4 * d + c + 1])
                        used2(i)
            for d in range(2):
                arg2()
                A(decay2[d][:, :, :], gate[d][0][:, :, :], ACT.Exp)
                A(gate[d][0][:, :, :], gate[d][0][:, :, :], ACT.Tanh).then_inc(act_res, 1)
            for pair in range(4):
                if pair == 2:
                    for d in range(2):
                        arg2()
                        A(gate[d][0][:, :, :], gate[d][0][:, :, :], ACT.Sqrt, scale=-1.0).then_inc(act_res, 1)
                    for c in range(2):
                        b = unit2(14 + c)
                        used2(A(gel[:, 2 * c:2 * c + 2, :], b[:, :].rearrange("p (c s) -> p c s", c=2),
                                ACT.Gelu_apprx_tanh))
                arg2()
                for j in range(2):
                    for c in range(TC):
                        n = 2 * j + c
                        i = A(p2[:, 2 * (pair % 2) + j, S * c:S * (c + 1)], score_banks(pair)[j][:, S * c:S * (c + 1)], ACT.Exp,
                              scale=SCALE, bias=neg2[:, 4 * (pair % 2) + n:4 * (pair % 2) + n + 1],
                              accum_out=sum2[:, 4 * (pair % 2) + n:4 * (pair % 2) + n + 1])
                i.then_inc(act_res, 1)
            for dst, src in ((sqL, gate[0][0]), (sqA, ao)):
                arg2()
                A(dst[:, :, :], src[:, :, :], ACT.Square).then_inc(act_res, 1)
            squares(x_ready, 2 * DEPTH + 4, x, xn)
            arg2()
            for c in range(TC):
                i = A(expL[:, c, :], logits[:, c, :], ACT.Exp, bias=negL[:, c:c + 1])
            i.then_inc(act_res, 1)

            act.sem_inc(ex["y_out"], 1)
            act.wait_ge(ex["xs"], 1)
            by_chunk = lambda a: a.rearrange("q (p c) -> q c p", c=4)
            as_chunks = lambda a: a.rearrange("q (c p) -> q c p", c=4)
            A(as_chunks(xs_sb), by_chunk(XS[:, :]), ACT.Copy).then_inc(ex["xs_out"], 1)
            act.wait_ge(count_ready, 2)
            with act.Fori(0, E) as e:
                first = act.value_load(n_before[0:1, bass.ds(e, 1)], min_val=0, max_val=16)
                more = act.value_load(n_more[0:1, bass.ds(e, 1)], min_val=0, max_val=3)
                with act.If(more > 0):
                    with act.Fori(0, more) as b:
                        j = first + b
                        pe_at = lambda n: act.wait_ge(ex["pe"], j * 8 + n)
                        dve_at = lambda n: act.wait_ge(ex["dve"], j * 7 + n)
                        pe_at(1)
                        A(as_chunks(xs_sb), by_chunk(XS[:, :]), ACT.Copy).then_inc(ex["act"], 1)
                        dve_at(3)
                        A(tanh_g, g_sb, ACT.Tanh, scale=SWIGLU_ALPHA / 2).then_inc(ex["act"], 1)
                        pe_at(5)
                        A(hT_sb, HTB[:, :], ACT.Copy).then_inc(ex["act"], 1)
                        pe_at(6)
                        A(yx_sb, YB[:, :], ACT.Copy).then_inc(ex["act"], 1)
                act.wait_ge(ex["gc"], e + 1)
                A(tanh_g, g_sb, ACT.Tanh, scale=SWIGLU_ALPHA / 2).then_inc(ex["eg"], 1)
                act.wait_ge(ex["xs"], e + 2)
                A(as_chunks(xs_sb), by_chunk(XS[:, :]), ACT.Copy).then_inc(ex["xs_out"], 1)
                act.wait_ge(ex["ht"], e + 1)
                A(hT_sb, HTB[:, :], ACT.Copy).then_inc(ex["ht_out"], 1)
                act.wait_ge(w_used, e * EXPERT_TURNS + EXPERT_TURNS)
                act.wait_ge(ex["o"], e * 2 + 2)
                A(y_sb, YB[:, :], ACT.Copy).then_inc(ex["y_out"], 1)
            squares(x_ready, 2 * DEPTH + 6, x, ring[:, 0, 0:2 * D].rearrange("p (c d) -> p c d", c=TC))

        @block.tensor
        def _(pe):
            mm = nc.tensor.matmul
            tp = nc.tensor.transpose

            def arrived(slot, n):
                pe.wait_ge(w_in_slot[slot], n * 16)

            def slot_cols(slot, n):
                return ring[:, slot, 0:KC * n].rearrange("p (k n) -> p k n", n=n)

            def project_T(b, w, c, n=2):
                for j in range(n):
                    for k in range(KC):
                        i = mm(b[:, S * j:S * j + S], w[:, k, P * (c + j):P * (c + j + 1)], hT[:, k, :],
                               start=(k == 0), stop=(k == KC - 1))
                return i

            def project(b, w, c, n):
                for k in range(KC):
                    i = mm(b[:, 0:n], hT[:, k, P * c:P * (c + 1)], w[:, k, 0:n], start=(k == 0), stop=(k == KC - 1))
                return i

            def causal_scores(b, stationary, moving, r):
                mm(b[:, 0:S], stationary[r:r + HD, 0:P], moving[r:r + HD, :], start=True, stop=True)
                return mm(b[:, S:CAUSAL], stationary[r:r + HD, P:S], moving[r:r + HD, P:S], start=True, stop=True,
                          skip_group_check=True)

            pe.sem_inc(pj_ready, PJ_0)
            pe.sem_inc(out_ready, OUT_0)
            pe.wait_ge(params_in, 16 * N_PARAM_LOADS)
            pe.wait_ge(ident_in, 16)
            tp(TR[1][:, 0:N_ROWS], rows[0:N_ROWS, :], ident[0:N_ROWS, 0:N_ROWS]).then_inc(tr_ready, 1)

            with pe.Fori(0, DEPTH) as l:
                def pj(u):
                    if u >= 4:
                        pe.wait_ge(pj_used, l * PJ_L + (u - 3))
                    return PJ[u % 4]

                def tr(u):
                    pe.wait_ge(tr_used, l * TR_L + max(u, 1))
                    return TR[u % 2]

                def sc(u):
                    if u >= 2:
                        pe.wait_ge(sc_used, l * SC_L + (u - 1))
                    return SC[u % 2]

                def group(g, kind, parts=(0, 1)):
                    slot, n = g % SLOTS, IN_GROUPS[g][1]
                    arrived(slot, l * in_loads[slot] + (g // SLOTS + 1))
                    w = slot_cols(slot, n)
                    for j in parts:
                        b = pj(2 * g + j)
                        i = project_T(b, w, 2 * j) if kind == "T" else project(b, w, j, n)
                        i.then_inc(pj_ready, 1)

                def a_scores(pair):
                    u = [6, 10, 12, 15][pair]
                    banks = [sc(u), sc(u + 1)]
                    q, k = qkA[:, pair, :], qkA[:, 4 + pair, :]
                    for j in range(2):
                        for b, r in zip(banks, (0, HD)):
                            i = mm(b[:, P * j:CAUSAL if j else P], q[r:r + HD, P * j:P * (j + 1)],
                                   k[r:r + HD, 0:P * (j + 1)], start=True, stop=True, skip_group_check=True)
                            if j:
                                i.then_inc(sc_ready, 1)

                def a_turn(pair):
                    pe.wait_ge(probs_ready, l * 4 + (pair + 1))
                    for h in (2 * pair, 2 * pair + 1):
                        b = tr([6, 8, 10, 13][pair] + h % 2)
                        for j in range(3):
                            i = tp(b[:, P * j:P * (j + 1)], prob[:, h % 4, P * j:P * (j + 1)], ident)
                        i.then_inc(tr_ready, 1)

                def a_out(pair):
                    b = sc([14, 17, 24, 25][pair])
                    pe.wait_ge(tr_used, l * TR_L + [9, 11, 13, 16][pair])
                    for kc in range(2):
                        for j in range(2):
                            h = 2 * pair + j
                            src = probT[:, j, 0:S] if kc == 0 else probT[:, j, S:CAUSAL]
                            i = mm(b[HD * j:HD * (j + 1), P * kc:S], vA[:, kc, HD * h:HD * (h + 1)], src,
                                   start=(kc == 0), stop=(kc == 1), skip_group_check=True)
                    i.then_inc(sc_ready, 1)

                pe.wait_ge(xn_ready, l + 1)
                for u in range(4):
                    b = tr(u)
                    for k in (2 * u, 2 * u + 1):
                        for c in range(TC):
                            o = S * (k - 2 * u) + P * c
                            i = tp(b[:, o:o + P], xn[:, c, P * k:P * (k + 1)], ident)
                    i.then_inc(tr_ready, 1)
                pe.wait_ge(tr_used, l * TR_L + 5)
                group(0, "tok")
                group(1, "T")
                pe.wait_ge(pj_used, l * PJ_L + 2)
                b = tr(4)
                for g in range(2):
                    for c in range(TC):
                        i = tp(b[0:C_HEADS, S * g + P * c:S * g + P * (c + 1)],
                               cg[:, c, 256 + 4 * g:260 + 4 * g], ident)
                i.then_inc(tr_ready, 1)
                group(2, "T")
                group(3, "T")
                pe.wait_ge(act_res, l * RES_L + 5)
                pe.wait_ge(consts_in, 16)
                turned = tr(5)
                row_head = K("row_head").rearrange("p (h n) -> p h n", h=C_HEADS)
                for pair in range(2):
                    b = sc(pair)
                    for j in range(2):
                        i = mm(b[:, S * j:S * (j + 1)], row_head[0:C_HEADS, 2 * pair + j, :], rw[:, 8, :],
                               start=True, stop=True, skip_group_check=True)
                    i.then_inc(sc_ready, 1)
                for g, row in enumerate((7, 1)):
                    for c in range(TC):
                        i = tp(turned[:, 8 * g + 4 * c:8 * g + 4 * c + 4], rw[:, row, P * c:P * (c + 1)],
                               ident[0:C_HEADS, 0:C_HEADS])
                i.then_inc(tr_ready, 1)
                group(4, "tok")
                pe.wait_ge(qkC_ready, l + 1)
                for h in range(C_HEADS):
                    causal_scores(sc(2 + h), qkC[:, 2 + h // 2, :], qkC[:, h // 2, :], HD * (h % 2)).then_inc(sc_ready, 1)
                pe.wait_ge(pj_used, l * PJ_L + 8)
                a_scores(0)
                group(5, "tok")
                pe.wait_ge(pj_used, l * PJ_L + 10)
                pe.wait_ge(sc_used, l * SC_L + 6)
                for c in range(TC):
                    b = sc(8 + c)
                    for h in range(C_HEADS):
                        o = b[:, (HD + 1) * h:(HD + 1) * (h + 1)]
                        lhs = [wC[:, h, 0:P]] if c == 0 else [wC[:, h, P:S], wC[:, h, S:CAUSAL]]
                        for s, w in enumerate(lhs):
                            i = mm(o, w, vC[:, s, h, :], start=(s == 0), stop=(s == len(lhs) - 1),
                                   skip_group_check=True)
                    i.then_inc(sc_ready, 1)
                group(6, "T", (0,))
                a_scores(1)
                group(6, "T", (1,))
                a_turn(0)
                a_scores(2)
                group(7, "T")
                a_out(0)
                a_turn(1)
                a_scores(3)
                group(8, "tok")
                a_out(1)
                pe.wait_ge(pj_used, l * PJ_L + 16)
                for c in range(2):
                    b = sc(18 + c)
                    for j in range(2):
                        i = mm(b[:, S * j:S * (j + 1)], K("swap"), rawB[:, 2 * c + j, :], start=True, stop=True,
                               skip_group_check=True)
                    i.then_inc(sc_ready, 1)
                a_turn(2)
                arrived(3, l * in_loads[3] + 2)
                arrived(4, l * in_loads[4] + 2)
                w_out = [slot_cols(3, 512), slot_cols(4, 512)]

                def out_rows(k, lhs, first=False):
                    for c in range(TC):
                        for h in range(2):
                            mm(PJ[2 * c + h][:, :], lhs[:, P * c:P * (c + 1)], w_out[h][:, k, :], start=first, stop=False)

                pe.wait_ge(pj_used, l * PJ_L + 18)
                pe.wait_ge(sc_used, l * SC_L + 18)
                out_rows(0, agT[:, 0, :], first=True)
                out_rows(1, agT[:, 1, :])
                pe.wait_ge(yC_ready, l + 1)
                b = tr(12)
                for k in range(2):
                    for c in range(TC):
                        i = tp(b[:, S * k + P * c:S * k + P * (c + 1)], yBC[:, 4 * c + 2 * k:4 * c + 2 * k + 2, :], ident)
                i.then_inc(tr_ready, 1)
                pe.wait_ge(rotB_ready, l + 1)
                for h in range(B_HEADS):
                    causal_scores(sc(20 + h), rotB[:, 2 + h // 2, :], rotB[:, h // 2, :], HD * (h % 2)).then_inc(sc_ready, 1)
                a_out(2)
                a_turn(3)
                a_out(3)
                pe.wait_ge(sc_used, l * SC_L + 24)
                b = sc(26)
                for c in range(TC):
                    for h in range(B_HEADS):
                        o = b[:, 256 * c + HD * h:256 * c + HD * (h + 1)]
                        lhs = [sB[:, h, 0:P]] if c == 0 else [sB[:, h, P:S], sB[:, h, S:CAUSAL]]
                        for s, w in enumerate(lhs):
                            i = mm(o, w, vgB[:, s, HD * h:HD * (h + 1)], start=(s == 0), stop=(s == len(lhs) - 1),
                                   skip_group_check=True)
                i.then_inc(sc_ready, 1)

                pe.wait_ge(tr_used, l * TR_L + 14)
                for k in (6, 7):
                    out_rows(k, yT[:, k - 4, :])
                pe.wait_ge(sc_used, l * SC_L + 26)
                out_rows(2, agT[:, 2, :])
                pe.wait_ge(yB_ready, l + 1)
                b = tr(15)
                for k in range(2):
                    for c in range(TC):
                        i = tp(b[:, S * k + P * c:S * k + P * (c + 1)], yBC[:, 4 * c + 2 * k:4 * c + 2 * k + 2, :], ident)
                i.then_inc(tr_ready, 1)
                out_rows(3, agT[:, 3, :])
                pe.wait_ge(tr_used, l * TR_L + 17)
                for c in range(TC):
                    for h in range(2):
                        for k in range(2):
                            i = mm(PJ[2 * c + h][:, :], yT[:, k, P * c:P * (c + 1)], w_out[h][:, 4 + k, :], start=False,
                                   stop=(k == 1))
                        i.then_inc(out_ready, 1)
            tr_n = [1 + DEPTH * TR_L]

            def tr2():
                pe.wait_ge(tr_used, tr_n[0] - 1)
                tr_n[0] += 1
                return TR[tr_n[0] % 2]

            def pj2(u):
                if u >= 4:
                    pe.wait_ge(pj_used, DEPTH * PJ_L + u - 3)
                return PJ[u % 4]

            def turn_tokens(s, ready, src):
                pe.wait_ge(s, ready)
                for u in range(4):
                    b = tr2()
                    for k in (2 * u, 2 * u + 1):
                        for c in range(TC):
                            o = S * (k - 2 * u) + P * c
                            i = tp(b[:, o:o + P], src[:, c, P * k:P * (k + 1)], ident)
                    i.then_inc(tr_ready, 1)
                pe.wait_ge(tr_used, tr_n[0])

            def group2(g, kind, u, parts=(0, 1)):
                slot, n = g, IN2_GROUPS[g][1]
                arrived(slot, DEPTH * in_loads[slot] + 1)
                w = slot_cols(slot, n)
                for j in parts:
                    b = pj2(u + j)
                    i = project_T(b, w, 2 * j) if kind == "T" else project(b, w, j, n)
                    i.then_inc(pj_ready, 1)

            turn_tokens(xn_ready, DEPTH + 1, xn)
            group2(0, "T", 0)
            group2(1, "tok", 2)
            group2(2, "tok", 4)
            pe.wait_ge(lru_w_in, 16 * 8)
            pe.wait_ge(xc_ready, 1)
            for u in range(8):
                b = pj2(6 + u)
                for j in range(2):
                    i = mm(b[:, S * j:S * (j + 1)], lru_w[:, 2 * u + j, :], xc[:, 2 * (u % 2) + j, :], start=True,
                           stop=True, skip_group_check=True)
                i.then_inc(pj_ready, 1)

            def scores2(pair):
                if pair == 1:
                    pe.wait_ge(pj_used, DEPTH * PJ_L + 14)
                elif pair > 1:
                    pe.wait_ge(act_res, DEPTH * RES_L + [7, 11][pair - 2])
                for c in range(TC):
                    for j in range(2):
                        r = HD * j
                        i = mm(score_banks(pair)[j][:, S * c:S * (c + 1)], qkT[r:r + HD, pair, P * c:P * (c + 1)],
                               qkT[r:r + HD, 4, :], start=True, stop=True, skip_group_check=True)
                        if c:
                            i.then_inc(sc_ready, 1)

            group2(3, "T", 14, (0,))
            pe.wait_ge(qk_ready, 1)
            for chunks in ((4,), (0, 1), (2, 3)):
                b = tr2()
                for n, ch in enumerate(chunks):
                    for c in range(TC):
                        i = tp(b[:, S * n + P * c:S * n + P * (c + 1)], qk[:, c, 2 * ch:2 * ch + 2, :], ident)
                i.then_inc(tr_ready, 1)
            pe.wait_ge(tr_used, tr_n[0])
            scores2(0)
            scores2(1)
            group2(3, "T", 14, (1,))

            def turn2(pair):
                pe.wait_ge(probs_ready, DEPTH * 4 + pair + 1)
                for j in range(2):
                    b = tr2()
                    for kc in range(2):
                        for c in range(TC):
                            i = tp(b[:, S * kc + P * c:S * kc + P * (c + 1)],
                                   p2[:, 2 * (pair % 2) + j, S * c + P * kc:S * c + P * (kc + 1)], ident)
                    i.then_inc(tr_ready, 1)

            def out2(pair):
                pe.wait_ge(tr_used, tr_n[0])
                b = tr2()
                r = HD * (pair % 2)
                for j in range(2):
                    for kc in range(2):
                        i = mm(b[r:r + HD, S * j:S * (j + 1)], v2[:, kc, HD * j:HD * (j + 1)],
                               pT2[:, j, S * kc:S * (kc + 1)], start=(kc == 0), stop=(kc == 1), skip_group_check=True)
                i.then_inc(tr_ready, 1)

            w = [slot_cols(4, 512), slot_cols(5, 512)]

            def attn_rows(ks, first):
                pe.wait_ge(y2_ready, 1 if first else 2)
                for n, k in enumerate(ks):
                    for c in range(TC):
                        for h in range(2):
                            i = mm(PJ[2 * c + h][:, :], yT[:, k, P * c:P * (c + 1)], w[h][:, k, :],
                                   start=(first and n == 0), stop=(not first and n == 1))
                return i

            turn2(0)
            scores2(2)
            out2(0)
            turn2(1)
            scores2(3)
            out2(1)
            turn2(2)
            arrived(4, DEPTH * in_loads[4] + 1)
            arrived(5, DEPTH * in_loads[5] + 1)
            pe.wait_ge(pj_used, DEPTH * PJ_L + 16)
            attn_rows((0, 2), True)
            out2(2)
            turn2(3)
            out2(3)

            def lru_rows(n):
                c, h = n // 2, n % 2
                for k in range(4, 8):
                    i = mm(LB[n][:, :], yT[:, k, P * c:P * (c + 1)], w[h][:, k, :], start=(k == 4), stop=(k == 7))
                i.then_inc(out_ready, 1)

            pe.wait_ge(lru_ready, 1)
            lru_rows(0)
            lru_rows(1)
            attn_rows((1, 3), False).then_inc(out_ready, 1)
            pe.wait_ge(act_res, DEPTH * RES_L + 14)
            b = tr2()
            for s, sq in enumerate((sqA, sqL)):
                for c in range(TC):
                    for k in range(LC):
                        i = mm(b[:, 2 * s + c:2 * s + c + 1], sq[:, k, P * c:P * (c + 1)], ones[:, 0:1], start=(k == 0),
                               stop=(k == LC - 1), skip_group_check=True)
            i.then_inc(tr_ready, 1)
            pe.wait_ge(tr_used, tr_n[0])
            lru_rows(2)
            lru_rows(3)

            def halves(f):
                for n in range(2):
                    i = f(n, slice(T * n, T * (n + 1)))
                return i

            def gather(sel):
                for c in range(TC):
                    i = halves(lambda n, at: mm(XS[at, :], sel[:, c, :], xn[:, c, 512 * n:512 * (n + 1)],
                                                start=(c == 0), stop=(c == TC - 1), skip_group_check=True))
                return i

            def turn4(dst, src):
                for c in range(4):
                    i = tp(dst[:, P * c:P * (c + 1)], src[:, P * c:P * (c + 1)], ident)
                return i

            def product(dst, slot, lhs, h, done, odd):
                w = ring[:, slot + (SLOTS if odd and slot < 2 else 0), :].rearrange("p (c n) -> p c n", c=4)
                for c in range(4):
                    i = halves(lambda n, at: mm(dst[at, :], lhs[:, c, T * h:T * (h + 1)], w[:, c, 512 * n:512 * (n + 1)],
                                                start=(h == 0 and c == 0), stop=(done and h == 1 and c == 3),
                                                skip_group_check=True))
                return i

            def biases(m):
                return halves(lambda n, at: mm((GB, UB)[m][at, :], bsel[:, :], bias[:, m, 512 * n:512 * (n + 1)],
                                               start=False, stop=True, skip_group_check=True))

            def add_up(c, gT, y, banks=OB):
                return halves(lambda n, at: mm(banks[n][:, :], gT[at, P * c:P * (c + 1)], y[at, :], start=True, stop=True))

            def turn_gates(i=None):
                for c in range(TC):
                    i = tp(XS[:, P * c:P * (c + 1)], selg[:, c, :], ident)
                return i

            chunked = lambda a: a.rearrange("p (c q) -> p c q", c=4)
            turn_tokens(x_ready, 2 * DEPTH + 6, x)
            pe.wait_ge(wr_in, 16)
            for c in range(TC):
                for k in range(KC):
                    i = mm(PJ[0][:, E * c:E * (c + 1)], hT[:, k, P * c:P * (c + 1)], wr[:, k, :],
                           start=(k == 0), stop=(k == KC - 1), skip_group_check=True)
            i.then_inc(out_ready, 1)
            pe.wait_ge(mask_ready, 1)
            before = K("before")
            mm(PJ[1][:, 0:E], before, mask[:, 0, :], start=True, stop=True)
            mm(PJ[1][:, E:2 * E], ones, mask[:, 0, :], start=True, stop=False, skip_group_check=True)
            mm(PJ[1][:, E:2 * E], before, mask[:, 1, :], start=False, stop=True, skip_group_check=True)
            mm(PJ[1][:, 2 * E:3 * E], ones, mask[:, 0, :], start=True, stop=False, skip_group_check=True)
            mm(PJ[1][:, 2 * E:3 * E], ones, mask[:, 1, :], start=False, stop=True, skip_group_check=True).then_inc(out_ready, 1)
            pe.wait_ge(gates_ready, 1)
            b = tr2()
            for c in range(TC):
                i = tp(b[0:E, P * c:P * (c + 1)], gates[:, c, :], ident)
            i.then_inc(tr_ready, 1)
            pe.wait_ge(ex["sel"], 1)
            gather(sel).then_inc(ex["xs"], 1)
            pe.wait_ge(tr_used, tr_n[0])
            pe.wait_ge(bdown_in, 16)
            for c in range(TC):
                for h in range(2):
                    i = mm(DB[2 * c + h][:, :], gatesT[:, P * c:P * (c + 1)], bdown[:, 512 * h:512 * (h + 1)],
                           start=True, stop=True)
                i.then_inc(out_ready, 1)
                if c == 0:
                    pe.wait_ge(ex["xs_out"], 1)
                    turn4(XTB, xs_sb).then_inc(ex["xt"], 1)

            pe.wait_ge(count_ready, 2)
            pe.wait_ge(bias_in, 32)
            with pe.Fori(0, E // 2) as pair:
                for odd in range(2):
                    e = pair * 2 + odd
                    first = pe.value_load(n_before[0:1, bass.ds(e, 1)], min_val=0, max_val=16)
                    more = pe.value_load(n_more[0:1, bass.ds(e, 1)], min_val=0, max_val=3)

                    def weights(turn):
                        if turn >= 2:
                            arrived(turn, e + (slot_base[turn] + 1))
                        elif odd:
                            arrived(SLOTS + turn, pair + 1)
                        else:
                            arrived(turn, pair + (slot_base[turn] + 1))

                    with pe.If(more > 0):
                        with pe.Fori(0, more) as b:
                            j = first + b
                            up = lambda i: i.then_inc(ex["pe"], 1)
                            act_at = lambda n: pe.wait_ge(ex["act"], j * 4 + n)
                            dve_at = lambda n: pe.wait_ge(ex["dve"], j * 7 + n)
                            dve_at(1)
                            up(gather(sel))
                            act_at(1)
                            up(turn4(XTB, xs_sb))
                            dve_at(2)
                            pe.wait_ge(ex["bsel"], e + 1)
                            for turn in range(4):
                                weights(turn)
                                product((GB, UB)[turn // 2], turn, chunked(xTx), turn % 2, False, odd)
                                if turn % 2:
                                    up(biases(turn // 2))
                            turn_gates()
                            dve_at(4)
                            up(turn4(HTB, h_sb))
                            act_at(3)
                            pe.wait_ge(ex["y_out"], e + 1)
                            for h in range(2):
                                weights(4 + h)
                                i = product(YB, 4 + h, chunked(hT_sb), h, True, odd)
                            up(i)
                            act_at(4)
                            dve_at(5)
                            up(add_up(0, gTx, yx_sb))
                            up(add_up(1, gTx, yx_sb, (XTB, HTB)))

                    pe.wait_ge(ex["xt_out"], e + 1)
                    pe.wait_ge(ex["bsel"], e + 1)
                    for turn in range(4):
                        weights(turn)
                        product((GB, UB)[turn // 2], turn, chunked(xT), turn % 2, False, odd).then_inc(w_used, 1)
                        if turn == 1:
                            biases(0)
                    biases(1).then_inc(ex["gu"], 1)
                    pe.wait_ge(ex["sel"], e + 2)
                    gather(sel).then_inc(ex["xs"], 1)
                    pe.wait_ge(ex["y_out"], e + 1)
                    pe.wait_ge(ex["gt_out"], e + 1)
                    add_up(0, gT, y_sb).then_inc(ex["o"], 1)
                    pe.wait_ge(ex["xs_out"], e + 2)
                    turn4(XTB, xs_sb).then_inc(ex["xt"], 1)
                    pe.wait_ge(ex["h"], e + 1)
                    turn4(HTB, h_sb).then_inc(ex["ht"], 1)
                    pe.wait_ge(ex["ht_out"], e + 1)
                    for h in range(2):
                        weights(4 + h)
                        product(YB, 4 + h, chunked(hT_sb), h, True, odd).then_inc(w_used, 1)
                        if h == 0:
                            pe.wait_ge(ex["acc"], e * 2 + 1)
                            add_up(1, gT, y_sb).then_inc(ex["o"], 1)
                            pe.wait_ge(ex["selg"], e + 1)
                            turn_gates().then_inc(ex["gt"], 1)
            pe.wait_ge(ex["y_out"], E + 1)
            pe.wait_ge(ex["gt_out"], E + 1)
            add_up(0, gT, y_sb).then_inc(ex["o"], 1)
            pe.wait_ge(ex["acc"], 2 * E + 1)
            add_up(1, gT, y_sb).then_inc(ex["o"], 1)

        @block.vector
        def _(v):
            tt, ts, stt = v.tensor_tensor, v.tensor_scalar, v.scalar_tensor_tensor

            def bc(a, n):
                return a.unsqueeze(2).to_broadcast([a.shape[0], a.shape[1], n])

            v.wait_ge(x_in, 16)
            v.sem_inc(x_ready, 2)
            v.wait_ge(tr_ready, 1)
            v.tensor_copy(cols_all[:, 0:N_ROWS], TR[1][:, 0:N_ROWS]).then_inc(tr_used, 1)
            v.wait_ge(tr_used, 1)

            with v.Fori(0, DEPTH) as l:
                st = Steps(v, dve_step, l * STEPS_L)

                def arg(i):
                    i.then_inc(act_arg, 1)

                def result(n):
                    v.wait_ge(act_res, l * RES_L + n)

                def tr(u):
                    v.wait_ge(tr_ready, l * TR_L + (u + 2))
                    return TR[u % 2]

                def tr_done(i):
                    i.then_inc(tr_used, 1)

                def sc(u):
                    v.wait_ge(sc_ready, l * SC_L + (u + 1))
                    return SC[u % 2]

                def sc_done(i):
                    i.then_inc(sc_used, 1)

                def gated(out, tanh, z):
                    return stt(out=out, in0=tanh, scalar=1.0, in1=z, op0=ALU.add, op1=ALU.mult)

                def head_norm(w, gate, nth, ready):
                    s = small[:, 128:136]
                    flat = yBC.rearrange("p (c h) d -> p c (h d)", c=TC)
                    st.do(v.tensor_reduce(s, yBC, AX, ALU.add))
                    st.do(ts(s, s, 1.0 / HD, None, ALU.mult))
                    st.do(tt(yBC, yBC, bc(s, HD), ALU.subtract))
                    st.do(tt(tmp, yBC, yBC, ALU.mult))
                    st.do(v.tensor_reduce(s, tmp, AX, ALU.add))
                    ts(small[:, 0:8], s, 1.0 / HD, HEAD_EPS, ALU.mult, ALU.add).then_inc(pow_arg, 1)
                    st.do(tt(flat, flat, w.unsqueeze(1).to_broadcast([P, TC, 256]), ALU.mult))
                    st.do(tt(flat, flat, gate, ALU.mult))
                    v.wait_ge(pow_res, l * POW_L + nth)
                    stt(out=yBC, in0=yBC, scalar=0.5, in1=bc(small[:, 32:40], HD), op0=ALU.mult,
                        op1=ALU.mult).then_inc(ready, 1)

                st.go(v.tensor_copy(cols[:, 0:N_ROWS1], cols_all[:, bass.ds(l * N_ROWS1, N_ROWS1)]))
                st.go(v.tensor_copy(gb[:, :], gb_all[:, bass.ds(l, 1), :].rearrange("p a b -> p (a b)")))
                st.go(v.tensor_copy(hw[:, :, :], hw_all[:, bass.ds(l, 1), :, :].rearrange("p a b c -> p (a b) c")))
                st.go(v.memset(rawC[:, :, 0:3], 0.0))
                result(1)
                ts(small[:, 0:2], small[:, 64:66], 1.0 / D, RMS_EPS, ALU.mult, ALU.add).then_inc(pow_arg, 1)
                v.wait_ge(pow_res, l * POW_L + 1)
                st.go(ts(xn[:, 0, :], x[:, 0, :], small[:, 32:33], None, ALU.mult))
                ts(xn[:, 1, :], x[:, 1, :], small[:, 33:34], None, ALU.mult).then_inc(xn_ready, 1)
                st.wait()
                for u in range(4):
                    b = tr(u)
                    st.go(ts(hT[:, 2 * u, :], b[:, 0:S], cols[:, 2 * u:2 * u + 1], None, ALU.mult))
                    tr_done(ts(hT[:, 2 * u + 1, :], b[:, S:512], cols[:, 2 * u + 1:2 * u + 2], None, ALU.mult))
                b = tr(4)
                st.go(ts(rw[:, 0, :], b[0:C_HEADS, 0:S], gb[:, 0:1], None, ALU.add))
                tr_done(ts(rw[:, 1, :], b[0:C_HEADS, S:512], gb[:, 1:2], None, ALU.add))
                v.wait_ge(tr_used, l * TR_L + 6)
                st.do(ts(rw[:, 2, :], rw[:, 1, :], -1.0, None, ALU.mult))
                arg(tt(rw[:, 2, :], rw[:, 1, :], rw[:, 2, :], ALU.min))
                result(2)
                arg(ts(rw[:, 4, :], rw[:, 3, :], 1.0, None, ALU.add))
                v.wait_ge(pj_used, l * PJ_L + 4)
                w = lambda j, c: cols[:, COL1["conv_w"] + 4 * j + c:COL1["conv_w"] + 4 * j + c + 1]
                for j in range(4):
                    for c in range(4):
                        if j == 0:
                            i = ts(qkC[:, c, :], rawC[:, c, 0:S], w(0, c),
                                   cols[:, COL1["conv_b"] + c:COL1["conv_b"] + c + 1], ALU.mult, ALU.add)
                        else:
                            i = stt(out=qkC[:, c, :], in0=rawC[:, c, j:j + S], scalar=w(j, c), in1=qkC[:, c, :],
                                    op0=ALU.mult, op1=ALU.add)
                        if (j, c) == (3, 3):
                            arg(i)
                        else:
                            st.go(i)
                    if j < 3:
                        st.wait()
                result(3)
                st.do(ts(rw[:, 6, :], rw[:, 4, :], -1.0, None, ALU.add))
                st.do(ts(rw[:, 7, :], rw[:, 6, :], 0.0, None, ALU.is_equal))
                st.go(tt(rw[:, 5, :], rw[:, 5, :], rw[:, 7, :], ALU.add))
                st.do(tt(rw[:, 6, :], rw[:, 6, :], rw[:, 7, :], ALU.add))
                st.go(tt(rw[:, 5, :], rw[:, 5, :], rw[:, 3, :], ALU.mult))
                st.go(v.memset(rw[:, 7, :], 1.0))
                st.do(v.reciprocal(rw[:, 6, :], rw[:, 6, :]))
                st.do(tt(rw[:, 5, :], rw[:, 5, :], rw[:, 6, :], ALU.mult))
                st.do(stt(out=rw[:, 5, :], in0=rw[:, 1, :], scalar=0.0, in1=rw[:, 5, :], op0=ALU.min, op1=ALU.subtract))
                st.do(v.tensor_tensor_scan(rw[:, 6, :], rw[:, 7, :], rw[:, 5, :], 0.0, ALU.mult, ALU.add))
                st.do(tt(rw[:, 7, :], rw[:, 0, :], rw[:, 6, :], ALU.subtract))
                st.do(v.tensor_tensor_scan(rw[:, 8, :], rw[:, 7, :], rw[:, 7, :], 0.0, ALU.max, ALU.max))
                arg(tt(rw[:, 2, :], rw[:, 6, :], rw[:, 8, :], ALU.add))
                result(4)
                gated(qkC[:, :, :], eg[:, :, :], qkC[:, :, :]).then_inc(qkC_ready, 1)
                acol, emcol = small[:, 80:88], small[:, 88:96]
                b = tr(5)
                tr_done(v.tensor_copy(small[:, 80:96], b[:, 0:16]))
                v.wait_ge(tr_used, l * TR_L + 7)
                for pair in range(2):
                    b = sc(pair)
                    for j in range(2):
                        h = 2 * pair + j
                        st.go(ts(wC[:, h, 0:S], b[:, S * j:S * (j + 1)], acol[:, h:h + 1], 0.0, ALU.subtract, ALU.max))
                        i = ts(wC[:, h, S:CAUSAL], b[:, S * j + P:S * (j + 1)], acol[:, 4 + h:5 + h], 0.0,
                               ALU.subtract, ALU.max)
                        if j:
                            sc_done(i)
                        else:
                            st.go(i)
                result(7)
                blocks = wC.rearrange("p h (j n) -> p h j n", j=3)[:, :, 0:3:2, :]
                tri = K("tri").unsqueeze(1).unsqueeze(1).to_broadcast([P, C_HEADS, 2, P])
                v.wait_ge(consts_in, 16)
                st.do(tt(blocks, blocks, tri, ALU.mult))
                v.wait_ge(pj_used, l * PJ_L + 2)
                st.go(gated(cg[:, :, 0:256], eC[:, :, 256:512], cg[:, :, 0:256]))
                for h in range(C_HEADS):
                    b = sc(2 + h)
                    sc_done(stt(out=wC[:, h, :], in0=b[:, 0:CAUSAL], scalar=SCALE / 4, in1=wC[:, h, :],
                                op0=ALU.mult, op1=ALU.mult))

                def a_softmax(pair):
                    neg = small[:, 96 + 4 * (pair % 2):100 + 4 * (pair % 2)]
                    for j in range(2):
                        h = 2 * pair + j
                        b = sc([6, 10, 12, 15][pair] + j)
                        sc_done(stt(out=prob[:, h % 4, :], in0=K("dist"), scalar=-(2.0 ** (-8.0 * (h + 1) / A_HEADS)),
                                    in1=b[:, 0:CAUSAL], op0=ALU.mult, op1=ALU.add))
                        v.wait_ge(sc_used, l * SC_L + ([6, 10, 12, 15][pair] + j + 1))
                        st.go(v.tensor_reduce(neg[:, 2 * j:2 * j + 1], prob[:, h % 4, 0:P], AX, ALU.max))
                        st.go(v.tensor_reduce(neg[:, 2 * j + 1:2 * j + 2], prob[:, h % 4, P:CAUSAL], AX, ALU.max))
                    st.wait()
                    arg(ts(neg, neg, -1.0, None, ALU.mult))

                def a_normalise(pair):
                    result(8 + pair)
                    s = small[:, 104 + 4 * (pair % 2):108 + 4 * (pair % 2)]
                    st.do(v.reciprocal(s, s))
                    for j in range(2):
                        h = (2 * pair + j) % 4
                        st.go(ts(prob[:, h, 0:P], prob[:, h, 0:P], s[:, 2 * j:2 * j + 1], None, ALU.mult))
                        i = ts(prob[:, h, P:CAUSAL], prob[:, h, P:CAUSAL], s[:, 2 * j + 1:2 * j + 2], None, ALU.mult)
                        if j:
                            i.then_inc(probs_ready, 1)
                        else:
                            st.go(i)

                def a_turned(pair):
                    for j in range(2):
                        b = tr([6, 8, 10, 13][pair] + j)
                        tr_done(v.tensor_copy(probT[:, j, :], b[:, 0:CAUSAL]))

                def a_gate(pair):
                    b = sc([14, 17, 24, 25][pair])
                    sc_done(stt(out=agT[:, pair, :], in0=b[:, 0:S], scalar=0.5, in1=agT[:, pair, :], op0=ALU.mult,
                                op1=ALU.mult))

                a_softmax(0)
                a_normalise(0)
                den, rden = small[:, 112:120], small[:, 120:128]
                o = [sc(8 + c)[:, 0:(HD + 1) * C_HEADS].rearrange("p (h n) -> p h n", h=C_HEADS) for c in range(TC)]
                for c in range(TC):
                    st.go(v.tensor_copy(den[:, 4 * c:4 * c + 4].unsqueeze(2), o[c][:, :, HD:HD + 1]))
                st.wait()
                st.do(stt(out=rden, in0=den, scalar=-1.0, in1=den, op0=ALU.mult, op1=ALU.max))
                st.do(tt(rden, rden, emcol, ALU.max))
                st.do(ts(rden, rden, 2.0, None, ALU.mult))
                st.do(v.reciprocal(rden, rden))
                for c in range(TC):
                    sc_done(tt(yBC[:, 4 * c:4 * c + 4, :], o[c][:, :, 0:HD], bc(rden[:, 4 * c:4 * c + 4], HD), ALU.mult))
                v.wait_ge(sc_used, l * SC_L + 10)
                flat = yBC.rearrange("p (c h) d -> p c (h d)", c=TC)
                v.wait_ge(pj_used, l * PJ_L + 10)
                st.do(gated(flat, eC[:, :, 0:256], flat))
                a_softmax(1)
                head_norm(hw[:, 1, :], cg[:, :, 0:256], 2, yC_ready)
                a_normalise(1)
                a_turned(0)
                a_softmax(2)
                v.wait_ge(pj_used, l * PJ_L + 14)
                st.do(gated(agT[:, :, :], eg[:, :, :], agT[:, :, :]))
                a_normalise(2)
                a_gate(0)
                a_turned(1)
                a_softmax(3)
                v.wait_ge(pj_used, l * PJ_L + 16)
                table = lambda n: K(n).unsqueeze(1)
                st.go(tt(rotB, rawB, table("ret_cos").to_broadcast([P, 4, S]), ALU.mult))
                a_normalise(3)
                a_gate(1)
                for c in range(2):
                    b = sc(18 + c)
                    turned = tmp.rearrange("p g d -> p (g d)").rearrange("p (c s) -> p c s", c=2)
                    sc_done(tt(turned, b[:, :].rearrange("p (c s) -> p c s", c=2),
                               table("ret_sin").to_broadcast([P, 2, S]), ALU.mult))
                    v.wait_ge(sc_used, l * SC_L + (19 + c))
                    i = tt(rotB[:, 2 * c:2 * c + 2, :], rotB[:, 2 * c:2 * c + 2, :], turned, ALU.add)
                    if c:
                        i.then_inc(rotB_ready, 1)
                    else:
                        st.do(i)
                v.wait_ge(rotB_ready, l + 1)
                a_turned(2)
                b = tr(12)
                tr_done(v.tensor_copy(yT[:, 2:4, :], b[:, :].rearrange("p (c s) -> p c s", c=2)))
                decay = K("decay").rearrange("p (h n) -> p h n", h=B_HEADS)
                for h in range(B_HEADS):
                    b = sc(20 + h)
                    sc_done(tt(sB[:, h, :], b[:, 0:CAUSAL], decay[:, h, :], ALU.mult))
                a_gate(2)
                a_turned(3)
                a_gate(3)
                v.wait_ge(pj_used, l * PJ_L + 18)
                st.go(gated(vgB[:, :, 256:512], eB[:, :, :], vgB[:, :, 256:512]))
                b = sc(26)
                sc_done(v.tensor_copy(yBC, b[:, :].rearrange("p (g d) -> p g d", d=HD)))
                v.wait_ge(sc_used, l * SC_L + 27)
                head_norm(hw[:, 0, :], vgB[:, :, 256:512], 3, yB_ready)
                b = tr(15)
                tr_done(v.tensor_copy(yT[:, 0:2, :], b[:, :].rearrange("p (c s) -> p c s", c=2)))
                for c in range(TC):
                    for h in range(2):
                        v.wait_ge(out_ready, l * OUT_L + (OUT_0 + 2 * c + h + 1))
                        i = tt(x[:, c, 512 * h:512 * (h + 1)], x[:, c, 512 * h:512 * (h + 1)], PJ[2 * c + h][:, :], ALU.add)
                        if h:
                            i.then_inc(x_ready, 1)
                        else:
                            st.go(i)
                v.wait_ge(x_ready, 2 * l + 4)
                assert st.n == STEPS_L, f"STEPS_L = {st.n}"
            st = Steps(v, dve_step, DEPTH * STEPS_L)
            res = Steps(v, act_res, DEPTH * RES_L)
            n_pow, n_tr = [DEPTH * POW_L], [1 + DEPTH * TR_L]

            def arg2(i):
                i.then_inc(act_arg, 1)

            def result2():
                res.n += 1
                res.wait()

            def powered(i):
                i.then_inc(pow_arg, 1)
                n_pow[0] += 1
                v.wait_ge(pow_res, n_pow[0])

            def tr2():
                n_tr[0] += 1
                v.wait_ge(tr_ready, n_tr[0])
                return TR[n_tr[0] % 2]

            def tr2_done(i):
                i.then_inc(tr_used, 1)

            def rstd(eps):
                powered(ts(small[:, 0:2], small[:, 64:66], 1.0 / D, eps, ALU.mult, ALU.add))

            def turned_tokens(scale):
                for u in range(4):
                    b = tr2()
                    if scale is None:
                        tr2_done(v.tensor_copy(hT[:, 2 * u:2 * u + 2, :], b[:, :].rearrange("p (c s) -> p c s", c=2)))
                    else:
                        st.go(ts(hT[:, 2 * u, :], b[:, 0:S], scale(2 * u), None, ALU.mult))
                        tr2_done(ts(hT[:, 2 * u + 1, :], b[:, S:512], scale(2 * u + 1), None, ALU.mult))

            col = lambda key, i, n=1: cols_all[:, COL2[key] + i:COL2[key] + i + n]
            v.wait_ge(roww_in, 16)
            for c in range(TC):
                i = tt(xn[:, c, :], x[:, c, :], roww[:, :], ALU.mult)
                i.then_inc(xw_ready, 1)
            st.go(v.memset(lraw[:, :, 0:2], 0.0))
            st.go(v.memset(lraw[:, :, 2 + S:3 + S], 0.0))
            st.go(ts(half_b, col("ba", 0, 16), 0.5, None, ALU.mult))
            st.go(ts(lam(0), col("lam", 0, 8), -1.0, None, ALU.mult))
            result2()
            st.do(ts(small[:, 0:2], small[:, 64:66], 1.0 / D, RMS_EPS, ALU.mult, ALU.add))
            st.do(v.reciprocal(small[:, 2:4], small[:, 0:2]))
            result2()
            st.do(tt(small[:, 2:4], small[:, 2:4], small[:, 66:68], ALU.mult))
            powered(ts(small[:, 2:4], small[:, 2:4], 1.0 / D, NORM_EPS, ALU.mult, ALU.add))
            st.do(tt(small[:, 68:70], small[:, 32:34], small[:, 34:36], ALU.mult))
            for c in range(TC):
                i = ts(xn[:, c, :], xn[:, c, :], small[:, 68 + c:69 + c], None, ALU.mult)
                i.then_inc(xn_ready, 1) if c else st.go(i)
            st.wait()
            turned_tokens(lambda k: col("norm1", k))
            for c in range(TC):
                i = stt(out=x[:, c, :], in0=x[:, c, :], scalar=small[:, 32 + c:33 + c], in1=roww[:, :], op0=ALU.mult,
                        op1=ALU.mult)
                i.then_inc(x_ready, 1)
            arg2(tt(lam(0), lam(0), col("lam", 0, 8), ALU.min))
            result2()
            arg2(ts(lam(2), lam(1), 1.0, None, ALU.add))
            v.wait_ge(act_arg, DEPTH * ARG_L + 2)
            st.do(ts(lam(4), lam(2), -1.0, None, ALU.add))
            st.do(ts(lam(5), lam(4), 0.0, None, ALU.is_equal))
            result2()
            st.go(tt(lam(3), lam(3), lam(5), ALU.add))
            st.do(tt(lam(4), lam(4), lam(5), ALU.add))
            st.go(tt(lam(3), lam(3), lam(1), ALU.mult))
            st.do(v.reciprocal(lam(4), lam(4)))
            st.go(tt(lam(3), lam(3), lam(4), ALU.mult))
            st.do(ts(lam(5), col("lam", 0, 8), -1.0, 0.0, ALU.mult, ALU.max))
            st.do(tt(lam(3), lam(3), lam(5), ALU.add))
            st.do(ts(lam(5), lam(3), -LRU_C / 2, None, ALU.mult))
            v.wait_ge(pj_used, DEPTH * PJ_L + 2)
            for j in range(4):
                for c in range(LC):
                    if j == 0:
                        i = ts(xc[:, c, :], lraw[:, c, 0:S], col("conv_w", c), col("conv_b", c), ALU.mult, ALU.add)
                    else:
                        i = stt(out=xc[:, c, :], in0=lraw[:, c, j:j + S], scalar=col("conv_w", 4 * j + c), in1=xc[:, c, :],
                                op0=ALU.mult, op1=ALU.add)
                    i.then_inc(xc_ready, 1) if (j, c) == (3, 3) else st.go(i)
                if j < 3:
                    st.wait()
            v.wait_ge(xc_ready, 1)

            for c in range(TC):
                f = qk[:, c, :, :]
                v.wait_ge(pj_used, DEPTH * PJ_L + 5 + c)
                st.do(tt(rot1, f, f, ALU.mult))
                st.do(v.tensor_reduce(small[:, 10 * c:10 * c + 10], rot1, AX, ALU.add))
                if c:
                    ts(small[:, 0:20], small[:, 0:20], 1.0 / HD, 1e-6, ALU.mult, ALU.add).then_inc(pow_arg, 1)
                for a, n in ((0, Q_HEADS), (Q_HEADS, KV_HEADS)):
                    g = qk[:, c, a:a + n, :]
                    w = qkw[:, 1 if a else 0, :].unsqueeze(1).to_broadcast([P, n, HD])
                    st.go(tt(g, g, w, ALU.mult))
                st.wait()
                table = lambda name: K(name)[:, HD * c:HD * (c + 1)]
                st.go(tt(rot1, f, table("rope_cos").unsqueeze(1).to_broadcast([P, 10, HD]), ALU.mult))
                pairs = lambda a: a.rearrange("p h (a t i) -> p h a t i", a=2, t=2)
                sin = table("rope_sin").rearrange("p (a t i) -> p a t i", a=2, t=2)
                for t in range(2):
                    for a in range(2):
                        st.go(tt(pairs(rot2)[:, :, a, t, :], pairs(f)[:, :, a, 1 - t, :],
                                 sin[:, a, t, :].unsqueeze(1).to_broadcast([P, 10, 16]), ALU.mult))
                st.wait()
                st.do(tt(f, rot1, rot2, ALU.add))
            n_pow[0] += 1
            v.wait_ge(pow_res, n_pow[0])
            for c in range(TC):
                f = qk[:, c, :, :]
                i = tt(f, f, bc(small[:, 32 + 10 * c:42 + 10 * c], HD), ALU.mult)
                i.then_inc(qk_ready, 1) if c else st.go(i)

            for d in range(2):
                v.wait_ge(pj_used, DEPTH * PJ_L + 10 + 4 * d)
                c8 = lam(5)[:, 4 * d:4 * d + 4].unsqueeze(2).to_broadcast([P, LC, S])
                arg2(stt(out=gate[d][0][:, :, :], in0=gate[d][0][:, :, :], scalar=1.0, in1=c8, op0=ALU.add, op1=ALU.mult))
                st.go(stt(out=gate[d][1][:, :, :], in0=gate[d][1][:, :, :], scalar=1.0, in1=xc[:, :, :], op0=ALU.add,
                          op1=ALU.mult))
                if d == 0:
                    b = tr2()
                    tr2_done(v.tensor_copy(qkT[:, 4, :], b[:, 0:S]))
                    for n in range(2):
                        b = tr2()
                        tr2_done(v.tensor_copy(qkT[:, 2 * n:2 * n + 2, :], b[:, :].rearrange("p (c s) -> p c s", c=2)))
            def one_minus_a2(d):
                t = gate[d][0][:, :, :]
                st.do(tt(sq2[:, :, :], decay2[d][:, :, :], decay2[d][:, :, :], ALU.mult))
                arg2(stt(out=t, in0=sq2[:, :, :], scalar=1.0, in1=t, op0=ALU.add, op1=ALU.mult))
                v.wait_ge(act_arg, DEPTH * ARG_L + 7 + d)

            def recurrence(d):
                st.do(stt(out=gate[d][1][:, :, :], in0=gate[d][1][:, :, :], scalar=0.5, in1=gate[d][0][:, :, :],
                          op0=ALU.mult, op1=ALU.mult))
                way = (lambda a: a[:, ::-1]) if d else (lambda a: a)
                for c in range(LC):
                    st.go(v.tensor_tensor_scan(way(gate[d][0][:, c, :]), way(decay2[d][:, c, :]), way(gate[d][1][:, c, :]),
                                               0.0, ALU.mult, ALU.add))

            def weighted(src, key, chunks, first, ready):
                for n, c in enumerate(chunks):
                    i = ts(yT[:, first + c, :], src[:, c, :], col(key, c), None, ALU.mult)
                    i.then_inc(ready, 1) if n == len(chunks) - 1 else st.go(i)

            def maxima2(pair):
                neg = neg2[:, 4 * (pair % 2):4 * (pair % 2) + 4]
                v.wait_ge(sc_ready, DEPTH * SC_L + 2 * pair + 2)
                for j in range(2):
                    scores = score_banks(pair)[j][:, :].rearrange("p (c k) -> p c k", c=2)
                    st.go(v.tensor_reduce(neg[:, 2 * j:2 * j + 2], scores, AX, ALU.max))
                st.wait()
                arg2(ts(neg, neg, -SCALE, None, ALU.mult))

            def normalise2(pair):
                result2()
                s = sum2[:, 4 * (pair % 2):4 * (pair % 2) + 4]
                st.do(v.reciprocal(s, s))
                for j in range(2):
                    a = p2[:, 2 * (pair % 2) + j, :].rearrange("p (c k) -> p c k", c=2)
                    i = tt(a, a, bc(s[:, 2 * j:2 * j + 2], S), ALU.mult)
                    i.then_inc(probs_ready, 1) if j else st.go(i)

            def turned2(pair):
                for j in range(2):
                    b = tr2()
                    tr2_done(v.tensor_copy(pT2[:, j, :], b[:, :]))

            def out2(pair):
                b = tr2()
                r, c = HD * (pair % 2), pair // 2
                tr2_done(v.tensor_copy(ao[r:r + HD, c:c + 3:2, :], b[r:r + HD, :].rearrange("p (j s) -> p j s", j=2)))

            maxima2(0)
            maxima2(1)
            result2()
            result2()
            one_minus_a2(0)
            normalise2(0)
            one_minus_a2(1)
            turned2(0)
            normalise2(1)
            maxima2(2)
            out2(0)
            turned2(1)
            result2()
            result2()
            normalise2(2)
            maxima2(3)
            out2(1)
            v.wait_ge(pj_used, DEPTH * PJ_L + 16)
            v.wait_ge(tr_used, n_tr[0])
            weighted(ao, "attn_g", (0, 2), 0, y2_ready)
            turned2(2)
            normalise2(3)
            recurrence(0)
            recurrence(1)
            v.wait_ge(wr_in, 16)
            st.do(tt(wr[:, :, :], wr[:, :, :], bc(col("norm2", 0, KC), E), ALU.mult))
            lru = gate[0][0]
            st.wait()
            st.do(tt(lru[:, :, :], lru[:, :, :], gate[1][0][:, :, :], ALU.add))
            arg2(tt(lru[:, :, :], lru[:, :, :], gel[:, :, :], ALU.mult))
            out2(2)
            turned2(3)
            v.wait_ge(act_arg, DEPTH * ARG_L + 11)
            weighted(lru, "lru_g", range(LC), 4, lru_ready)
            b = tr2()
            r, c = HD * (3 % 2), 3 // 2
            arg2(v.tensor_copy(ao[r:r + HD, c:c + 3:2, :], b[r:r + HD, :].rearrange("p (j s) -> p j s", j=2)))
            v.wait_ge(act_arg, DEPTH * ARG_L + 12)
            v.sem_inc(tr_used, 1)
            weighted(ao, "attn_g", (1, 3), 0, y2_ready)
            b = tr2()
            powered(ts(small[:, 0:4], b[:, 0:4], 1.0 / LRU, NORM_EPS, ALU.mult, ALU.add))
            v.sem_inc(tr_used, 1)
            v.wait_ge(out_ready, OUT_0 + OUT_L * DEPTH + 3)
            for banks, at, last in ((PJ, 32, False), (LB, 34, True)):
                for n in range(4):
                    c, h = n // 2, n % 2
                    if last:
                        v.wait_ge(out_ready, OUT_0 + OUT_L * DEPTH + 2 + n)
                    part = x[:, c, 512 * h:512 * (h + 1)]
                    i = stt(out=part, in0=banks[n][:, :], scalar=small[:, at + c:at + c + 1], in1=part, op0=ALU.mult,
                            op1=ALU.add)
                    i.then_inc(x_ready, 1) if last and h else st.go(i)
                st.wait()
            v.wait_ge(x_ready, 2 * DEPTH + 6)

            iota = K("iota64")

            def select(at0, at1, ready):
                st2.go(ts(sel[:, 0, :], iota[:, 0:T], at0, None, ALU.is_equal))
                ts(sel[:, 1, :], iota[:, 0:T], at1, None, ALU.is_equal).then_inc(ready, 1)

            turned_tokens(None)
            res.n += 2
            result2()
            rstd(NORM_EPS)
            v.wait_ge(roww_in, 32)
            for c in range(TC):
                i = stt(out=xn[:, c, :], in0=x[:, c, :], scalar=small[:, 32 + c:33 + c], in1=roww[:, :], op0=ALU.mult,
                        op1=ALU.mult)
                i.then_inc(xn_ready, 1) if c else st.go(i)
            v.wait_ge(out_ready, OUT_0 + OUT_L * DEPTH + 6)
            for c in range(TC):
                st.go(stt(out=logits[:, c, :], in0=PJ[0][:, E * c:E * (c + 1)], scalar=small[:, 32 + c:33 + c],
                          in1=brout[:, :], op0=ALU.mult, op1=ALU.add))
            st.wait()
            for c in range(TC):
                st.go(v.max(out=top[:, c, :], in_=logits[:, c, :]))
            st.wait()
            arg2(ts(negL.unsqueeze(2), top[:, :, 0:1], -1.0, None, ALU.mult))
            for c in range(TC):
                st.go(v.max_index(top_at[:, c, :], top[:, c, :], logits[:, c, :]))
            st.wait()
            st.do(v.tensor_copy(top_atf, top_at[:, :, :]))
            for k in range(TOPK):
                for c in range(TC):
                    at = top_atf[:, c, k:k + 1]
                    if k == 0:
                        i = ts(mask[:, c, :], K("iota32"), at, None, ALU.is_equal)
                    else:
                        i = stt(out=mask[:, c, :], in0=K("iota32"), scalar=at, in1=mask[:, c, :], op0=ALU.is_equal, op1=ALU.add)
                    i.then_inc(mask_ready, 1) if (k, c) == (TOPK - 1, TC - 1) else st.go(i)
                if k < TOPK - 1:
                    st.wait()
            result2()
            v.wait_ge(mask_ready, 1)
            st.do(tt(gates, expL, mask, ALU.mult))
            st.do(v.tensor_reduce(rsum, gates, AX, ALU.add))
            st.do(v.reciprocal(rsum, rsum))
            tt(gates, gates, bc(rsum, E), ALU.mult).then_inc(gates_ready, 1)
            v.wait_ge(gates_ready, 1)
            st.go(ts(half_gates, gates, 0.5, None, ALU.mult))
            v.wait_ge(out_ready, OUT_0 + OUT_L * DEPTH + 7)
            st.go(v.memset(place[:, :, E:E + 1], -1.0))
            st.do(stt(out=place[:, :, 0:E], in0=PJ[1][:, 0:2 * E].rearrange("p (c e) -> p c e", c=2), scalar=1.0, in1=mask,
                      op0=ALU.add, op1=ALU.mult))
            st.do(ts(place[:, :, 0:E], place[:, :, 0:E], -1.0, None, ALU.add))
            st2 = st
            select(place[:, 0, 0:1], place[:, 1, 0:1], ex["sel"])
            st.do(ts(nblk, PJ[1][:, 2 * E:3 * E], float(T), None, ALU.is_gt))
            for b in range(2, S // T):
                st.do(stt(out=nblk, in0=PJ[1][:, 2 * E:3 * E], scalar=float(T * b), in1=nblk, op0=ALU.is_gt, op1=ALU.add))
            st.do(v.tensor_tensor_scan(ncum, ones[:, 0:E], nblk, 0.0, ALU.mult, ALU.add))
            v.tensor_copy(n_more[:, :], nblk).then_inc(count_ready, 1)
            tt(n_before[:, :], ncum, nblk, ALU.subtract).then_inc(count_ready, 1)
            b = tr2()
            tr2_done(v.tensor_copy(gatesT, b[0:E, 0:S]))
            st.go(v.memset(y_sb, 0.0))
            st.go(v.memset(gT, 0.0))
            v.tensor_copy(bsel[:, :], ident[:, 0:1].to_broadcast([P, T])).then_inc(ex["bsel"], 1)
            for c in range(TC):
                v.wait_ge(out_ready, OUT_0 + OUT_L * DEPTH + 8 + c)
                for h in range(2):
                    part = x[:, c, 512 * h:512 * (h + 1)]
                    st.go(tt(part, part, DB[2 * c + h][:, :], ALU.add))
                st.wait()
                if c == 0:
                    v.wait_ge(ex["xt"], 1)
                    v.tensor_copy(xT, XTB[:, :]).then_inc(ex["xt_out"], 1)
            v.sem_inc(ex["gt_out"], 1)

            def select_gates(at, e):
                for c in range(TC):
                    i = ts(selg[:, c, :], iota, at[c], half_gates[:, c, bass.ds(e, 1)], ALU.is_equal, ALU.mult)
                    yield i

            def hidden(ready, gc_ready, up_ready, tanh_ready):
                i = ts(g_sb, GB[:, :], SWIGLU_LIMIT, None, ALU.min)
                gc_ready(i)
                tanh_ready()
                st2.go(gated(g_sb, tanh_g, g_sb))
                up_ready()
                st2.do(ts(u_sb, UB[:, :], SWIGLU_LIMIT, -SWIGLU_LIMIT, ALU.min, ALU.max))
                stt(out=h_sb.rearrange("q (c p) -> q p c", c=4), in0=u_sb.rearrange("q (p c) -> q p c", c=4), scalar=1.0,
                    in1=g_sb.rearrange("q (p c) -> q p c", c=4), op0=ALU.add, op1=ALU.mult).then_inc(ready, 1)

            def add_sums(c, ready, banks=OB):
                for n in range(2):
                    i = tt(x[:, c, 512 * n:512 * (n + 1)], x[:, c, 512 * n:512 * (n + 1)], banks[n][:, :], ALU.add)
                    i.then_inc(ready, 1) if n else st2.go(i)

            st_main = st.base + st.n
            with v.Fori(0, E) as e:
                first = v.value_load(n_before[0:1, bass.ds(e, 1)], min_val=0, max_val=16)
                more = v.value_load(n_more[0:1, bass.ds(e, 1)], min_val=0, max_val=3)
                st2 = Steps(v, ex_step, first * EX_STEPS + e * PRE_STEPS)
                st2.go(v.tensor_copy(rest, place[:, :, bass.ds(e, 1)].rearrange("p c a -> p (c a)")))
                assert st2.n == PRE_STEPS
                with v.If(more > 0):
                    with v.Fori(0, more) as b:
                        j = first + b
                        st2 = Steps(v, ex_step, j * EX_STEPS + (e * PRE_STEPS + PRE_STEPS))
                        done = ex["dve"]
                        pe_at = lambda n: v.wait_ge(ex["pe"], j * 8 + n)
                        act_at = lambda n: v.wait_ge(ex["act"], j * 4 + n)
                        st2.wait()
                        st2.do(ts(rest, rest, -float(T), None, ALU.add))
                        select(rest[:, 0:1], rest[:, 1:2], done)
                        for i in select_gates([rest[:, 0:1], rest[:, 1:2]], e):
                            st2.go(i)
                        pe_at(2)
                        v.tensor_copy(xTx, XTB[:, :]).then_inc(done, 1)
                        pe_at(3)
                        hidden(done, lambda i: i.then_inc(done, 1), lambda: pe_at(4), lambda: (act_at(2), st2.wait()))
                        pe_at(5)
                        v.tensor_copy(gTx, XS[:, 0:S]).then_inc(done, 1)
                        pe_at(7)
                        add_sums(0, done)
                        pe_at(8)
                        add_sums(1, done, (XTB, HTB))
                        assert st2.n == EX_STEPS, f"EX_STEPS = {st2.n}"

                v.wait_ge(ex_step, (first + more) * EX_STEPS + (e * PRE_STEPS + PRE_STEPS))
                st2 = Steps(v, dve_step, e * MAIN_STEPS + st_main)
                v.wait_ge(ex["xs"], e + 1)
                select(place[:, 0, bass.ds(e + 1, 1)], place[:, 1, bass.ds(e + 1, 1)], ex["sel"])
                for c, i in enumerate(select_gates([place[:, 0, bass.ds(e, 1)], place[:, 1, bass.ds(e, 1)]], e)):
                    i.then_inc(ex["selg"], 1) if c else st2.go(i)
                v.wait_ge(ex["gu"], e + 1)
                hidden(ex["h"], lambda i: i.then_inc(ex["gc"], 1), lambda: None, lambda: (v.wait_ge(ex["eg"], e + 1), st2.wait()))
                v.tensor_copy(bsel[:, :], ident[:, bass.ds(e + 1, 1)].to_broadcast([P, T])).then_inc(ex["bsel"], 1)
                v.wait_ge(ex["xt"], e + 2)
                v.tensor_copy(xT, XTB[:, :]).then_inc(ex["xt_out"], 1)
                v.wait_ge(ex["o"], e * 2 + 1)
                add_sums(0, ex["acc"])
                v.wait_ge(ex["o"], e * 2 + 2)
                add_sums(1, ex["acc"])
                v.wait_ge(ex["gt"], e + 1)
                v.tensor_copy(gT, XS[:, 0:S]).then_inc(ex["gt_out"], 1)
                assert st2.n == MAIN_STEPS, f"MAIN_STEPS = {st2.n}"
            st = Steps(v, dve_step, st_main + E * MAIN_STEPS)
            st2 = st
            v.wait_ge(ex["o"], 2 * E + 1)
            add_sums(0, ex["acc"])
            v.wait_ge(ex["acc"], 2 * E + 1)
            v.sem_inc(x_ready, 1)
            v.wait_ge(ex["o"], 2 * E + 2)
            add_sums(1, ex["acc"])
            v.wait_ge(ex["acc"], 2 * E + 2)
            v.sem_inc(x_ready, 1)
            result2()
            rstd(NORM_EPS)
            v.wait_ge(roww_in, 48)
            for c in range(TC):
                i = stt(out=xn[:, c, :], in0=x[:, c, :], scalar=small[:, 32 + c:33 + c], in1=roww[:, :], op0=ALU.mult,
                        op1=ALU.mult)
                i.then_inc(x_ready, 1)


_INS = ['x', 'norm_w', 'w_in', 'conv_w', 'conv_b', 'gate_bias', 'ret_norm_w', 'mlstm_norm_w', 'w_out', 'final_norm_w',
        'norm1_g_2', 'w_in_2', 'q_norm_g_2', 'k_norm_g_2', 'conv_w_2', 'conv_b_2', 'lru_wa_2', 'lru_ba_2', 'lru_wi_2',
        'lru_bi_2', 'lru_lam_2', 'attn_out_g_2', 'lru_out_g_2', 'w_out_2', 'norm2_g_2', 'w_router_2', 'b_router_2',
        'w_gate_2', 'b_gate_2', 'w_up_2', 'b_up_2', 'w_down_2', 'b_down_2', 'final_g_2']


def kernel(**inputs):
    import concourse.bacc as _bacc
    from concourse.bass_utils import run_bass_kernel_spmd as _run

    nc = _bacc.Bacc("TRN2", target_bir_lowering=False, num_devices=1)
    arrays, args = {}, {}
    tables, where = shape_constants()
    for name in _INS + ["consts"]:
        a = np.ascontiguousarray(tables if name == "consts" else inputs[name])
        arrays[f"in_{name}_dram"] = a
        args[name] = nc.dram_tensor(f"in_{name}_dram", a.shape, mybir.dt.from_np(a.dtype), kind="ExternalInput").ap()
    args["consts_at"] = where
    out = nc.dram_tensor("out_0_dram", (1, S, D), F32, kind="ExternalOutput").ap()
    build(nc, args, out)
    r = _run(nc, [arrays], core_ids=[0])
    return r.results[0]["out_0_dram"]
```
